# Optimizing a Trainium2 kernel written in Bass

```python
import math
import jax
import jax.numpy as jnp
from jax import lax
import numpy as np

D_MODEL = 2048
BATCH = 1
SEQ = 512
DEPTH = 2

CHUNK = 64
N_MEM = 256
N_EVEN = (DEPTH + 1) // 2
N_ODD = DEPTH // 2
EPS = 1e-6
A_HEADS = 8
A_HEAD_DIM = 128
A_WIDTH = A_HEADS * A_HEAD_DIM
A_CONV = 4
B_HEADS = 8
B_QK_DIM = 64
B_QK_WIDTH = B_HEADS * 2 * B_QK_DIM
B_V_DIM = 2 * B_QK_DIM
B_WIDTH = B_HEADS * B_V_DIM
Q_BLOCK = 128
ROPE_THETA = 10000.0
C_WIDTH = D_MODEL
C_CONV = 3
M_HEADS = 4
M_HEAD_DIM = 128
M_WIDTH = M_HEADS * M_HEAD_DIM
AB_SIZES = (3 * A_WIDTH, A_WIDTH, A_HEADS, A_HEADS, B_QK_WIDTH, B_QK_WIDTH, B_WIDTH, B_WIDTH)
AB_IN = 4 * A_WIDTH + 2 * A_HEADS + 2 * B_QK_WIDTH + 2 * B_WIDTH
AB_OUT = A_WIDTH + B_WIDTH

kernel_name = 'hybrid_gdn_diffattn_shortconv_trunk'

def rms_norm(x, gain):
    xf = x.astype(jnp.float32)
    y = xf * lax.rsqrt(jnp.mean(xf * xf, axis=-1, keepdims=True) + EPS)
    return (y * gain.astype(jnp.float32)).astype(x.dtype)

def l2_normalize(x):
    xf = x.astype(jnp.float32)
    return (xf * lax.rsqrt(jnp.sum(xf * xf, axis=-1, keepdims=True) + EPS)).astype(x.dtype)

def split_sizes(t, sizes):
    return jnp.split(t, np.cumsum(sizes)[:-1].tolist(), axis=-1)

def causal_depthwise_conv(u, w):
    k = w.shape[0]
    return lax.conv_general_dilated(u, w[:, None, :].astype(u.dtype), window_strides=(1,),
                                    padding=[(k - 1, 0)], dimension_numbers=('NWC', 'WIO', 'NWC'),
                                    feature_group_count=u.shape[-1])

def rope_tables(seq, dim):
    inv_freq = ROPE_THETA ** (-jnp.arange(0, dim, 2, dtype=jnp.float32) / dim)
    ang = jnp.arange(seq, dtype=jnp.float32)[:, None] * inv_freq[None, :]
    return jnp.cos(ang), jnp.sin(ang)

def apply_rope(t, cos, sin):
    tf = t.astype(jnp.float32)
    t1, t2 = jnp.split(tf, 2, axis=-1)
    c = cos[None, :, None, None, :]
    s = sin[None, :, None, None, :]
    return jnp.concatenate([t1 * c - t2 * s, t2 * c + t1 * s], axis=-1).astype(t.dtype)

def lambda_init(layer):
    return 0.8 - 0.6 * math.exp(-0.3 * layer)

def gated_delta_rule(q, k, v, g, beta):
    bsz, seq, heads, dk = q.shape
    dv = v.shape[-1]
    n = seq // CHUNK
    f32 = jnp.float32

    def chunks(t):
        t = t.astype(f32).reshape((bsz, n, CHUNK, heads) + t.shape[3:])
        return jnp.moveaxis(t, 3, 1)

    q = chunks(q) * (dk ** -0.5)
    k = chunks(k)
    v = chunks(v)
    g = chunks(g)
    beta = chunks(beta)
    decay = jnp.cumsum(g, axis=-1)
    tril = jnp.tril(jnp.ones((CHUNK, CHUNK), dtype=bool))
    strict = jnp.tril(jnp.ones((CHUNK, CHUNK), dtype=bool), -1)
    diff = decay[..., :, None] - decay[..., None, :]
    gamma = jnp.where(tril, jnp.exp(jnp.where(tril, diff, 0.0)), 0.0)
    k_beta = k * beta[..., None]
    n_mat = jnp.where(strict, jnp.einsum('bhnid,bhnjd->bhnij', k_beta, k) * gamma, 0.0)
    eye = jnp.eye(CHUNK, dtype=f32)
    rhs = jnp.concatenate([v * beta[..., None], k_beta * jnp.exp(decay)[..., None]], axis=-1)
    sol = lax.linalg.triangular_solve(eye + n_mat, rhs, left_side=True, lower=True, unit_diagonal=True)
    u, w = sol[..., :dv], sol[..., dv:]
    qk = jnp.where(tril, jnp.einsum('bhnid,bhnjd->bhnij', q, k) * gamma, 0.0)
    q_dec = q * jnp.exp(decay)[..., None]
    k_dec = k * jnp.exp(decay[..., -1:] - decay)[..., None]
    chunk_decay = jnp.exp(decay[..., -1])

    def step(state, xs):
        qk_i, qd_i, kd_i, u_i, w_i, cd_i = xs
        v_new = u_i - jnp.einsum('bhcd,bhde->bhce', w_i, state)
        o = jnp.einsum('bhcd,bhde->bhce', qd_i, state) + jnp.einsum('bhij,bhje->bhie', qk_i, v_new)
        state = state * cd_i[..., None, None] + jnp.einsum('bhcd,bhce->bhde', kd_i, v_new)
        return state, o

    xs = tuple(jnp.moveaxis(t, 2, 0) for t in (qk, q_dec, k_dec, u, w, chunk_decay))
    state0 = jnp.zeros((bsz, heads, dk, dv), f32)
    _, o = lax.scan(step, state0, xs)
    return jnp.transpose(o, (1, 0, 3, 2, 4)).reshape(bsz, seq, heads, dv)

def differential_attention(q, k, v, lam):
    bsz, seq = q.shape[:2]
    nqb = seq // Q_BLOCK
    scale = B_QK_DIM ** -0.5
    qb = jnp.transpose(q.reshape(bsz, nqb, Q_BLOCK, B_HEADS, 2, B_QK_DIM), (1, 0, 3, 4, 2, 5))
    kt = jnp.transpose(k, (0, 2, 3, 1, 4))
    vt = jnp.transpose(v, (0, 2, 1, 3)).astype(jnp.float32)
    key_chunk = jnp.arange(seq) // CHUNK

    def one_block(args):
        blk, q_blk = args
        s = jnp.einsum('bhmqd,bhmkd->bhmqk', q_blk, kt, preferred_element_type=jnp.float32) * scale
        q_chunk = (blk * Q_BLOCK + jnp.arange(Q_BLOCK)) // CHUNK
        allowed = key_chunk[None, :] <= q_chunk[:, None]
        p = jax.nn.softmax(jnp.where(allowed, s, -jnp.inf), axis=-1)
        a = p[:, :, 0] - lam * p[:, :, 1]
        return jnp.einsum('bhqk,bhkd->bhqd', a, vt)

    o = lax.map(one_block, (jnp.arange(nqb), qb))
    return jnp.transpose(o, (1, 0, 3, 2, 4)).reshape(bsz, seq, B_HEADS, B_V_DIM)

def ab_mixer(h, w_in, conv_w, a_log, dt_bias, a_norm, lam_params, b_norm, w_out, lam_init, cos, sin):
    bsz, seq, _ = h.shape
    qkv_a, z_a, b_a, g_a, q_b, k_b, v_b, z_b = split_sizes(h @ w_in, AB_SIZES)
    qkv_a = jax.nn.silu(causal_depthwise_conv(qkv_a, conv_w))
    q_a, k_a, v_a = jnp.split(qkv_a, 3, axis=-1)
    a_heads = lambda t: t.reshape(bsz, seq, A_HEADS, A_HEAD_DIM)
    q_a = l2_normalize(a_heads(q_a))
    k_a = l2_normalize(a_heads(k_a))
    beta = jax.nn.sigmoid(b_a.astype(jnp.float32))
    log_decay = -jnp.exp(a_log.astype(jnp.float32)) * jax.nn.softplus(g_a.astype(jnp.float32) + dt_bias.astype(jnp.float32))
    o_a = gated_delta_rule(q_a, k_a, a_heads(v_a), log_decay, beta).astype(h.dtype)
    y_a = rms_norm(o_a, a_norm) * jax.nn.silu(a_heads(z_a))
    q_b = apply_rope(q_b.reshape(bsz, seq, B_HEADS, 2, B_QK_DIM), cos, sin)
    k_b = apply_rope(k_b.reshape(bsz, seq, B_HEADS, 2, B_QK_DIM), cos, sin)
    lp = lam_params.astype(jnp.float32)
    lam = jnp.exp(jnp.sum(lp[0] * lp[1])) - jnp.exp(jnp.sum(lp[2] * lp[3])) + lam_init
    o_b = differential_attention(q_b, k_b, v_b.reshape(bsz, seq, B_HEADS, B_V_DIM), lam).astype(h.dtype)
    y_b = rms_norm(o_b, b_norm) * (1.0 - lam_init) * jax.nn.silu(z_b.reshape(bsz, seq, B_HEADS, B_V_DIM))
    y = jnp.concatenate([y_a.reshape(bsz, seq, A_WIDTH), y_b.reshape(bsz, seq, B_WIDTH)], axis=-1)
    return y @ w_out

def conv_mixer(h, w_in, conv_w, w_out):
    u, b_gate, c_gate, z = jnp.split(h @ w_in, 4, axis=-1)
    y = b_gate * causal_depthwise_conv(c_gate * u, conv_w)
    return (y * jax.nn.silu(z)) @ w_out

def memory_cross_attention(h, mem_h, w_q, w_kv, w_o):
    bsz, seq, _ = h.shape
    n_mem = mem_h.shape[1]
    q, z = jnp.split(h @ w_q, 2, axis=-1)
    k, v = jnp.split(mem_h @ w_kv, 2, axis=-1)
    q = q.reshape(bsz, seq, M_HEADS, M_HEAD_DIM)
    k = k.reshape(bsz, n_mem, M_HEADS, M_HEAD_DIM)
    v = v.reshape(bsz, n_mem, M_HEADS, M_HEAD_DIM)
    s = jnp.einsum('bshd,bmhd->bhsm', q, k, preferred_element_type=jnp.float32) * (M_HEAD_DIM ** -0.5)
    p = jax.nn.softmax(s, axis=-1)
    o = jnp.einsum('bhsm,bmhd->bshd', p.astype(v.dtype), v).reshape(bsz, seq, M_WIDTH)
    return (o * jax.nn.silu(z)) @ w_o

def setup_inputs(seed: int = 0) -> dict:
    key = jax.random.key(seed)
    ks = jax.random.split(key, 22)
    f32 = jnp.float32

    def normal(k, shape, scale):
        return jax.random.normal(k, shape, f32) * scale

    def gain(k, shape):
        return 1.0 + normal(k, shape, 0.05)

    dt = jnp.exp(jax.random.uniform(ks[10], (N_EVEN, A_HEADS), f32, math.log(1e-3), math.log(1e-1)))
    return {
        'x': normal(ks[0], (BATCH, SEQ, D_MODEL), 1.0),
        'mem': normal(ks[1], (BATCH, N_MEM, D_MODEL), 1.0),
        'norm_pre': gain(ks[2], (DEPTH, D_MODEL)),
        'norm_post': gain(ks[3], (DEPTH, D_MODEL)),
        'xattn_norm_pre': gain(ks[4], (DEPTH, D_MODEL)),
        'xattn_norm_post': gain(ks[5], (DEPTH, D_MODEL)),
        'mem_norm': gain(ks[6], (DEPTH, D_MODEL)),
        'ab_w_in': normal(ks[7], (N_EVEN, D_MODEL, AB_IN), D_MODEL ** -0.5),
        'a_conv': normal(ks[8], (N_EVEN, A_CONV, 3 * A_WIDTH), A_CONV ** -0.5),
        'a_A_log': jnp.log(jax.random.uniform(ks[9], (N_EVEN, A_HEADS), f32, 1.0, 16.0)),
        'a_dt_bias': jnp.log(jnp.expm1(dt)),
        'a_out_norm': gain(ks[11], (N_EVEN, A_HEAD_DIM)),
        'b_lambda': normal(ks[12], (N_EVEN, 4, B_QK_DIM), 0.1),
        'b_out_norm': gain(ks[13], (N_EVEN, B_V_DIM)),
        'ab_w_out': normal(ks[14], (N_EVEN, AB_OUT, D_MODEL), AB_OUT ** -0.5),
        'c_w_in': normal(ks[15], (N_ODD, D_MODEL, 4 * C_WIDTH), D_MODEL ** -0.5),
        'c_conv': normal(ks[16], (N_ODD, C_CONV, C_WIDTH), C_CONV ** -0.5),
        'c_w_out': normal(ks[17], (N_ODD, C_WIDTH, D_MODEL), C_WIDTH ** -0.5),
        'm_w_q': normal(ks[18], (DEPTH, D_MODEL, 2 * M_WIDTH), D_MODEL ** -0.5),
        'm_w_kv': normal(ks[19], (DEPTH, D_MODEL, 2 * M_WIDTH), D_MODEL ** -0.5),
        'm_w_o': normal(ks[20], (DEPTH, M_WIDTH, D_MODEL), M_WIDTH ** -0.5),
    }

def reference(x, mem, norm_pre, norm_post, xattn_norm_pre, xattn_norm_post, mem_norm,
              ab_w_in, a_conv, a_A_log, a_dt_bias, a_out_norm, b_lambda, b_out_norm, ab_w_out,
              c_w_in, c_conv, c_w_out, m_w_q, m_w_kv, m_w_o):
    cos, sin = rope_tables(x.shape[1], B_QK_DIM)
    for layer in range(DEPTH):
        h = rms_norm(x, norm_pre[layer])
        if layer % 2 == 0:
            e = layer // 2
            y = ab_mixer(h, ab_w_in[e], a_conv[e], a_A_log[e], a_dt_bias[e], a_out_norm[e],
                         b_lambda[e], b_out_norm[e], ab_w_out[e], lambda_init(layer), cos, sin)
        else:
            o = layer // 2
            y = conv_mixer(h, c_w_in[o], c_conv[o], c_w_out[o])
        x = x + rms_norm(y, norm_post[layer])
        h = rms_norm(x, xattn_norm_pre[layer])
        m = rms_norm(mem, mem_norm[layer])
        y = memory_cross_attention(h, m, m_w_q[layer], m_w_kv[layer], m_w_o[layer])
        x = x + rms_norm(y, xattn_norm_post[layer])
    return x


_drawn_inputs = setup_inputs


def setup_inputs(seed=0):
    import zlib

    import numpy as np

    out = dict(_drawn_inputs(seed))
    spreads = {}
    factors = {}
    for name, (base, spread) in spreads.items():
        noise = np.random.default_rng([zlib.crc32(name.encode()), seed]).standard_normal(out[name].shape)
        drawn = base * np.exp(spread * noise) if base else spread * noise
        out[name] = jnp.asarray(drawn.astype(out[name].dtype))
    for name, factor in factors.items():
        out[name] = (out[name] * factor).astype(out[name].dtype)
    return out
```

```python
import concourse.bass as bass
import concourse.mybir as mybir
import math
from contextlib import ExitStack
import numpy as np

F32, F32R = mybir.dt.float32, mybir.dt.float32r
ALU, ACT, AX = mybir.AluOpType, mybir.ActivationFunctionType, mybir.AxisListType

P = 128
T, D, MEM = 512, 2048, 256
KT = D // P
TT = T // P
EPS = 1e-6
HEADS, HD = 8, 128
QK = 64
MH = 4
CH = 64
LAM_INIT = 0.8 - 0.6 * math.exp(0.0)
AB_B = 4 * 1024 + 2 * HEADS
RAW_SLOTS, SPLIT_SLOTS = 4, 2
CW = 4 * 256
NEG = -1e30
LEVELS = (1, 2, 4, 8, 16, 32)

AB_ITERS = 8
C_AB, P_AB = 0, 0
C_KV, P_KV = C_AB + 16 * AB_ITERS, P_AB + 4 * AB_ITERS
C_OUT0, P_OUT0 = C_KV + 32, P_KV + 8
C_Q0, P_Q0 = C_OUT0 + 32, P_OUT0 + 8
C_O0, P_O0 = C_Q0 + 16, P_Q0 + 4
C_C, P_C = C_O0 + 8, P_O0 + 8
C_OUT1, P_OUT1 = C_C + 128, P_C + 32
C_Q1, P_Q1 = C_OUT1 + 32, P_OUT1 + 8
C_O1, P_O1 = C_Q1 + 16, P_Q1 + 4
CHUNKS = C_O1 + 8

CONST = {}
_at = 0
for _name, _width in (("ident", P), ("cumsum", P), ("suffix", P), ("half0", P), ("half1", P), ("causal", P),
                      ("levels", len(LEVELS) * P), ("ones", 1), ("cos", T), ("sin", T)):
    CONST[_name] = (_at, _at + _width)
    _at += _width
CONST_W = _at
RESIDENT_W = CONST["cos"][0]

PARAM = {}
_at = 0
for _name, _width in (("norm_pre", 2 * KT), ("norm_post", 2 * KT), ("x_pre", 2 * KT), ("x_post", 2 * KT),
                      ("mem_norm", 2 * KT), ("a_conv", 24 * 4), ("c_conv", 16 * 3), ("a_norm", 1),
                      ("b_norm", 1), ("A_log", HEADS), ("dt_bias", HEADS)):
    PARAM[_name] = (_at, _at + _width)
    _at += _width
PARAM_W = _at


class Steps:

    def __init__(self, sem, book):
        self.sem, self.book, self.n, self.i = sem, book, 0, 0

    def round(self, i):
        self.n, self.i = 0, i

    def did(self, name=None):
        self.n += 1
        if name is not None:
            self.book[name] = self.n
        self.book["/"] = max(self.book.get("/", 0), self.n)
        return self.sem, 1

    def __call__(self, name, i=0):
        return self.sem, i * self.book.get("/", 0) + self.book.get(name, 1)

    def last(self):
        return self.sem, self.i * self.book.get("/", 0) + self.n


def spread(n_hops, first, last):
    return [first + (k * (last - first)) // max(n_hops - 1, 1) for k in range(n_hops)]



D_HOPS = (["ss", "rows", "tr", "dk", "qb", "p0"] + [f"{x}{s}" for s in range(1, 6) for x in ("p", "y")]
          + ["uw"] + [f"{x}{c}" for c in range(T // CH) for x in ("r", "s")] + ["fs", "fb"])
B_HOPS = ["vt"]
for _h in "01":
    B_HOPS += ["a" + _h + "0"] + [f"{x}{_h}{t + (x == 'a')}" for t in range(TT) for x in ("a", "b")]
    B_HOPS += ["fs" + _h, "fb" + _h]
C_HOPS = [f"{x}{h}" for h in range(MH) for x in "sto"]
D_SLOTS, B_SLOTS, C_SLOTS = spread(len(D_HOPS), 12, 62), spread(len(B_HOPS), 14, 62), spread(len(C_HOPS), 34, 62)


def hops_at(names, slots, lo, hi):
    return [n for n, s in zip(names, slots) if lo <= s < hi]


def build(nc, books, dram):
    ctx = ExitStack()
    with ctx:
        sb = lambda name, width, dt=F32: ctx.enter_context(nc.sbuf_tensor(name, [P, width], dt))
        sem = lambda name: ctx.enter_context(nc.semaphore(name))
        steps = lambda name: Steps(sem(name), books.setdefault(name, {}))

        X = sb("residual", KT * T)
        H_hi, H_lo = sb("input_hi", KT * T, F32R), sb("input_lo", KT * T, F32R)
        raw = sb("weights_raw", RAW_SLOTS * CW)
        w_hi, w_lo = sb("weights_hi", SPLIT_SLOTS * CW, F32R), sb("weights_lo", SPLIT_SLOTS * CW, F32R)
        const = sb("constants", RESIDENT_W)
        par = sb("parameters", PARAM_W)
        rs = sb("rstd_rows", T)
        small = sb("small", 512)
        gate_hi, gate_lo = sb("gate_hi", KT * 16, F32R), sb("gate_lo", KT * 16, F32R)
        work_w = 17000
        work = sb("work", work_w)

        acc = [ctx.enter_context(nc.psum_tensor(f"acc{n}", [P, T], F32)) for n in range(4)]
        m01 = ctx.enter_context(nc.psum_tensor("m01", [P, 2, T], F32))
        m23 = ctx.enter_context(nc.psum_tensor("m23", [P, 2, T], F32))
        M = [m01[:, 0, :], m01[:, 1, :], m23[:, 0, :], m23[:, 1, :]]

        c_ = lambda name: const[:, CONST[name][0]:CONST[name][1]]
        p_ = lambda name: par[:, PARAM[name][0]:PARAM[name][1]]
        pcol = lambda name, k: par[:, bass.ds(PARAM[name][0] + k, 1)]
        ident, ones = c_("ident"), c_("ones")
        level_mask = lambda s: const[:, CONST["levels"][0] + s * P:CONST["levels"][0] + (s + 1) * P]

        at = [0]

        def cols(n):
            at[0] += n
            assert at[0] <= 512
            return small[:, at[0] - n:at[0]]
        stat, powed, minus_half = cols(16), cols(16), cols(16)
        beta, decay, g_col, k_in_scale, k_out_scale, v_scale = (cols(32) for _ in range(6))
        chunk_decay = cols(64)
        t1, t2, t3, t4, t5 = (cols(32) for _ in range(5))
        a_gain, b_gain, neg_lam, coef = (cols(1) for _ in range(4))
        mx, nmx, ssum, rsum, lam2 = (cols(4) for _ in range(5))

        def wk(n, start=None):
            start = wk.end if start is None else start
            wk.end = start + n
            assert wk.end <= work_w, wk.end
            return work[:, start:start + n]
        x_tok, sq_junk, norm_buf, gate_w = wk(TT * D, 0), wk(D), wk(2 * T), wk(KT * 16)
        lam_in = wk(4 * QK)
        qc, kc, vc, tanh_t = wk(2 * T, 0), wk(2 * T), wk(2 * T), wk(2 * T)
        side = wk.end
        k_in, k_out, v_in, q_dec, qk_t = (wk(2 * T) for _ in range(5))
        gam, n_t, c_t, inv, inv_t, prod = (wk(2 * T) for _ in range(6))
        v_new, state = wk(2 * HD), wk(2 * HD)
        w_t, u_tok = gam, n_t
        sq = work[:, side + 16 * T:side + 20 * T]
        qr, kr, rot, rope_tab, v_tok, prob = (wk(2 * T, side if n == 0 else None) for n in range(6))
        att, att_t, o_sb, o_sq = (wk(T) for _ in range(4))
        v_feat = wk(2 * MEM)
        mem_tok = work[:, 0:D]
        kv_at = work_w - 4 * MH * MEM
        assert wk.end <= kv_at
        mk, mv = wk(2 * MH * MEM, kv_at), wk(2 * MH * MEM)
        Y, acc_sq, cq, cz = wk(KT * T, 0), wk(T), wk(MH * T), wk(MH * T)
        assert wk.end <= kv_at
        sqt = cq[:, 0:2 * T]
        cp, cpt = Y[:, 0:2 * T], Y[:, 2 * T:4 * T]
        uu, cu, cv, bb = cq[:, 0:2 * T], cq[:, 2 * T:4 * T], cz[:, 0:2 * T], cz[:, 2 * T:4 * T]

        head2 = lambda t: t.rearrange("p (h n) -> p h n", h=2)
        tiles = lambda t: t.rearrange("p (t n) -> p t n", n=P)
        over_tiles = lambda t, n: t.unsqueeze(1).broadcast_to([P, n, P])
        over_row = lambda t, n, w: t.unsqueeze(2).broadcast_to([P, n, w])
        psum_tiles = lambda m: m[:, :, :].rearrange("p b (t n) -> p (b t) n", n=P)
        flat = lambda m: m[:, :, :].rearrange("p b n -> p (b n)")
        xt = lambda k: X[:, bass.ds(k * T, T)]
        yt = lambda k: Y[:, bass.ds(k * T, T)]
        mem_h = lambda H, l, k: H[:, l * KT * MEM + k * MEM:l * KT * MEM + (k + 1) * MEM]
        mkt = lambda l, h: mk[:, (l * MH + h) * MEM:(l * MH + h + 1) * MEM]

        params_in, tables_in, gate_in, spilled, reloaded, out_done = (
            sem(n) for n in ("params_in", "tables_in", "gate_in", "spilled", "reloaded", "out_done"))
        x_in, mem_in = [sem(f"x_in{t}") for t in range(TT)], [sem(f"mem_in{m}") for m in range(2)]
        raw_in = [sem(f"raw_in{n}") for n in range(RAW_SLOTS)]
        hi_ready, lo_ready, chunk_used = sem("hi_ready"), sem("lo_ready"), sem("chunk_used")
        acc_free, z_tanh = sem("acc_free"), sem("z_tanh")
        const_set = sem("const_set")
        SM, SA, SV, SG = steps("start_mm"), steps("start_act"), steps("start_vec"), steps("start_pool")
        EA, EV = steps("evac_act"), steps("evac_vec")
        GM, GA, GV, GG = steps("delta_mm"), steps("delta_act"), steps("delta_vec"), steps("delta_pool")
        BM, BA, BV, BG = steps("attn_mm"), steps("attn_act"), steps("attn_vec"), steps("attn_pool")
        MM, MA, MV, MG = steps("mem_mm"), steps("mem_act"), steps("mem_vec"), steps("mem_pool")
        OA, OG = steps("outproj_act"), steps("outproj_pool")
        ZA, ZV = steps("split_act"), steps("split_vec")
        NM, NA, NV, NG = steps("norm_mm"), steps("norm_act"), steps("norm_vec"), steps("norm_pool")
        CM, CA, CV = steps("cross_mm"), steps("cross_act"), steps("cross_vec")
        VA, VV = steps("conv_act"), steps("conv_vec")
        FM, FV = steps("final_mm"), steps("final_vec")

        block = ctx.enter_context(nc.Block())
        LAYERS_Q, LAYERS_O, P_Q, P_O = (C_Q0, C_Q1), (C_O0, C_O1), (P_Q0, P_Q1), (P_O0, P_O1)

        @block.sync
        def _(sp):
            sp.dma_start(const[:, :], dram["constants"][:, 0:RESIDENT_W]).then_inc(params_in, 16)
            sp.dma_start(par[:, :], dram["parameters"]).then_inc(params_in, 16)
            for t in range(TT):
                sp.dma_start(x_tok[:, t * D:(t + 1) * D], dram["x"][t * P:(t + 1) * P, :]).then_inc(x_in[t], 16)
            sp.dma_start(gate_w.rearrange("p (k n) -> p k n", n=16),
                         dram["ab_w_in"].rearrange("(k p) n -> p k n", p=P)[:, :, 4096:4096 + 16]).then_inc(gate_in, 16)
            sp.dma_start(lam_in, dram["lambda"]).then_inc(gate_in, 16)

            def load(w, col, g, kt0):
                if g >= RAW_SLOTS:
                    sp.wait_ge(lo_ready, g - RAW_SLOTS + 1)
                c = g % RAW_SLOTS
                src = w.rearrange("(k p) n -> p k n", p=P)[:, kt0:kt0 + 4, bass.ds(col, 256)]
                sp.dma_start(raw[:, c * CW:(c + 1) * CW].rearrange("p (k n) -> p k n", k=4), src)\
                    .then_inc(raw_in[c], 16)

            def load_pair(w, col, g):
                for c in range(4):
                    load(w, col, g + c, 4 * c)

            for it in range(AB_ITERS):
                i = it % 4
                for j, sec in enumerate((3072, 0, 1024, 2048)):
                    load_pair(dram["ab_w_in"], (AB_B if it >= 4 else 0) + sec + 256 * i, C_AB + 16 * it + 4 * j)
                    if it == 0 and j == 0:
                        for k in range(KT):
                            sp.wait_ge(*SA(f"copy{k}"))
                            sp.dma_start(dram["spill"][k], xt(k)).then_inc(spilled, 16)
            for l in range(2):
                for j in range(4):
                    load_pair(dram["m_w_kv"][l], 256 * j, C_KV + 16 * l + 4 * j)
                    if l == 0 and j == 0:
                        sp.wait_ge(*BV("rk", 3))
                        sp.dma_start(mem_tok, dram["mem"][0:P, :]).then_inc(mem_in[0], 16)
                        sp.wait_ge(*MM("t03"))
                        sp.dma_start(mem_tok, dram["mem"][P:2 * P, :]).then_inc(mem_in[1], 16)
            for n in range(8):
                load_pair(dram["ab_w_out"], 256 * n, C_OUT0 + 4 * n)
                if n == 0:
                    for k in range(KT):
                        sp.wait_ge(*ZV(f"lo{k}"))
                        sp.dma_start(xt(k), dram["spill"][k]).then_inc(reloaded, 16)

            def cross_loads(l):
                for j in range(4):
                    load_pair(dram["m_w_q"][l], 256 * j, LAYERS_Q[l] + 4 * j)
                for n in range(8):
                    load(dram["m_w_o"][l], 256 * n, LAYERS_O[l] + n, 0)
            cross_loads(0)
            for n in range(8):
                for j, sec in enumerate((0, 2, 1, 3)):
                    load_pair(dram["c_w_in"], sec * D + 256 * n, C_C + 16 * n + 4 * j)
            for n in range(8):
                load_pair(dram["c_w_out"], 256 * n, C_OUT1 + 4 * n)
            cross_loads(1)
            for n in range(16):
                kg, t = n // TT, n % TT
                sp.wait_ge(*FV(f"o{n}"))
                sp.dma_start(dram["out"][t * P:(t + 1) * P, kg * T:(kg + 1) * T], yt(n)).then_inc(out_done, 16)
            sp.wait_ge(out_done, 16 * 16)
            sp.wait_ge(spilled, 16 * KT)

        @block.scalar
        def _(act):
            def split(g):
                if g >= CHUNKS:
                    return
                c, s = g % RAW_SLOTS, g % SPLIT_SLOTS
                act.wait_ge(raw_in[c], 16 * (g // RAW_SLOTS + 1))
                if g >= SPLIT_SLOTS:
                    act.wait_ge(chunk_used, g - SPLIT_SLOTS + 1)
                act.activation(w_hi[:, s * CW:(s + 1) * CW], raw[:, c * CW:(c + 1) * CW], ACT.Copy)\
                    .then_inc(hi_ready, 1)

            act.wait_ge(params_in, 32)
            for t in range(TT):
                act.wait_ge(x_in[t], 16)
                if t:
                    act.wait_ge(*SA.last())
                act.activation(sq_junk, x_tok[:, t * D:(t + 1) * D], ACT.Square,
                               accum_out=stat[:, t:t + 1]).then_inc(*SA.did(f"ss{t}"))
            split(0)
            act.wait_ge(gate_in, 32)
            act.activation(gate_hi[:, :], gate_w, ACT.Copy).then_inc(*SA.did("gate_hi"))
            for k in range(KT):
                act.wait_ge(*SM(f"tr{k}"))
                act.activation(xt(k), acc[k % 4][:, :], ACT.Copy).then_inc(*SA.did(f"copy{k}"))
                act.wait_ge(*SV(f"norm{k}"))
                act.activation(H_hi[:, k * T:(k + 1) * T], norm_buf[:, (k % 2) * T:(k % 2 + 1) * T], ACT.Copy)\
                    .then_inc(*SA.did(f"hi{k}"))

            def gates():
                act.wait_ge(*SV("gates"))
                act.activation(t1, t1, ACT.Exp, scale=-1.0).then_inc(*SA.did("eb"))
                act.activation(t3, t2, ACT.Abs).then_inc(*SA.did())
                act.wait_ge(*SA.last())
                act.activation(t3, t3, ACT.Exp, scale=-1.0).then_inc(*SA.did("eg"))
                act.activation(p_("A_log"), p_("A_log"), ACT.Exp).then_inc(*SA.did())
                act.activation(lam2[:, 0:2], lam2[:, 0:2], ACT.Exp).then_inc(*SA.did("small_exp"))

            def decays():
                act.wait_ge(*SM("decays"))
                act.wait_ge(*SV("decay"))
                act.activation(k_in_scale, M[0][:, 0:32], ACT.Exp).then_inc(*SA.did())
                act.activation(k_out_scale, M[0][:, 32:64], ACT.Exp).then_inc(*SA.did())
                act.activation(chunk_decay, M[0][:, 64:128], ACT.Exp).then_inc(*SA.did("decays"))

            def delta(name, i):
                if name == "begin":
                    GA.round(i)
                    act.wait_ge(*EV("s11", i))
                    act.activation(sq[:, 0:2 * T], qc, ACT.Square).then_inc(*GA.did())
                    act.activation(sq[:, 2 * T:4 * T], kc, ACT.Square).then_inc(*GA.did("sq"))
                elif name == "tr":
                    act.wait_ge(*GM("tr", i))
                    for h in range(2):
                        for t in range(TT):
                            c = bass.ds((2 * i + h) * TT + t, 1)
                            o = slice(h * T + t * P, h * T + (t + 1) * P)
                            act.activation(k_in[:, o], M[h][:, t * P:(t + 1) * P], ACT.Copy, scale=k_in_scale[:, c])\
                                .then_inc(*GA.did())
                            act.activation(v_in[:, o], M[2 + h][:, t * P:(t + 1) * P], ACT.Copy, scale=v_scale[:, c])\
                                .then_inc(*GA.did("kv"))
                elif name == "dk":
                    act.wait_ge(*GV("gam", i))
                    act.activation(prod, flat(m01), ACT.Exp).then_inc(*GA.did("edec"))
                    act.activation(gam, gam, ACT.Exp).then_inc(*GA.did("gam"))
                elif name[0] == "p" and name != "p0":
                    act.wait_ge(*GM(name, i))
                    act.activation(prod, flat(m01), ACT.Copy).then_inc(*GA.did(name))
                elif name == "uw":
                    act.wait_ge(*GM("uw", i))
                    act.activation(u_tok, flat(m01), ACT.Copy).then_inc(*GA.did("u"))
                    act.activation(w_t, flat(m23), ACT.Copy).then_inc(*GA.did("w"))
                elif name == "s7":
                    act.wait_ge(*GM("s7", i))
                    act.activation(prod, flat(m23), ACT.Copy).then_inc(*GA.did())
                    act.activation(inv, flat(m23), ACT.Square).then_inc(*GA.did("o"))
                elif name == "end":
                    act.wait_ge(*GV("end", i))
                    act.activation(coef, minus_half[:, 0:1], ACT.Copy).then_inc(*GA.did("end"))

            def attn(name, i):
                if name == "begin":
                    BA.round(i)
                    act.wait_ge(acc_free, 2 * (P_AB + 4 * (4 + i) + 3))
                    for src, tag in ((qc, "rq"), (kc, "rk")):
                        if tag == "rk":
                            act.wait_ge(*BV("rq", i))
                        for a in range(4):
                            b = a ^ 1
                            act.activation(rot[32 * a:32 * a + 32, :], src[32 * b:32 * b + 32, :], ACT.Copy)\
                                .then_inc(*BA.did(tag))
                elif name == "vt":
                    act.wait_ge(*BM("vt", i))
                    act.activation(v_tok, flat(m01), ACT.Copy).then_inc(*BA.did("v"))
                elif name[0] == "a":
                    h, t = int(name[1]), int(name[2])
                    act.wait_ge(*BM(name, i))
                    if t:
                        act.activation(att_t[:, 0:t * P], M[2][:, 0:t * P], ACT.Copy)\
                            .then_inc(*BA.did(f"at{h}{t - 1}"))
                    if t < TT:
                        n = (t + 1) * P
                        act.wait_ge(*BV(f"nm{h}{t}", i))
                        for m in range(2):
                            act.activation(prob[:, m * T:m * T + n], M[m][:, 0:n], ACT.Exp, bias=nmx[:, m:m + 1],
                                           scale=QK ** -0.5, accum_out=ssum[:, m:m + 1])\
                                .then_inc(*BA.did(f"p{h}{t}"))
                elif name in ("b03", "b13"):
                    act.wait_ge(*BM(name, i))
                    act.activation(o_sb, M[3], ACT.Copy).then_inc(*BA.did())
                    act.activation(o_sq, M[3], ACT.Square).then_inc(*BA.did(f"o{name[1]}"))

            def tanh_z(it):
                pair = P_AB + 4 * it
                act.wait_ge(chunk_used, done_at(pair))
                if it:
                    act.wait_ge(acc_free, 2 * pair)
                    if it <= 4:
                        act.wait_ge(*EV("s21", it - 1))
                for n in range(2):
                    act.activation(tanh_t[:, n * T:(n + 1) * T], acc[2 * (pair % 2) + n][:, :], ACT.Tanh, scale=0.5)\
                        .then_inc(z_tanh, 1)

            def tanh_conv(it, sec, n):
                act.wait_ge(acc_free, 2 * (P_AB + 4 * it + 1 + sec) + n + 1)
                act.activation(tanh_t[:, n * T:(n + 1) * T], (qc, kc, vc)[sec][:, n * T:(n + 1) * T], ACT.Tanh,
                               scale=0.5).then_inc(*EA.did(f"t{sec}{n}"))

            for it in range(AB_ITERS):
                reply, i = (delta, it - 1) if it <= 4 else (attn, it - 5)
                for c in range(16):
                    split(C_AB + 16 * it + c + 1)
                    if 1 <= it <= 4 and c < 2:
                        tanh_conv(it - 1, 2, c)
                    if c == 2:
                        EA.round(it)
                    if it == 0 and c == 4:
                        gates()
                    if c == 4:
                        tanh_z(it)
                    if it == 0 and c == 6:
                        decays()
                    if it < 4 and c in (8, 9):
                        tanh_conv(it, 0, c - 8)
                    if it < 4 and c in (12, 13):
                        tanh_conv(it, 1, c - 12)
                    if it:
                        if c == 2:
                            reply("begin", i)
                        names, slots = (D_HOPS, D_SLOTS) if it <= 4 else (B_HOPS, B_SLOTS)
                        for name in hops_at(names, slots, 4 * c, 4 * c + 4):
                            reply(name, i)
                        if c == 15 and it <= 4:
                            reply("end", i)
                        if c == 15 and it == 4:
                            act.wait_ge(*GA.last())
                            act.dma_start(rope_tab, dram["constants"][:, RESIDENT_W:]).then_inc(tables_in, 16)

            attn("begin", 3)
            for m in range(2):
                act.wait_ge(mem_in[m], 16)
                for h in range(2):
                    if h or m:
                        act.wait_ge(*MA.last())
                    act.activation(tanh_t, mem_tok[:, h * 2 * T:(h + 1) * 2 * T], ACT.Square,
                                   accum_out=t1[:, h:h + 1]).then_inc(*MA.did(f"ss{m}"))
                act.wait_ge(*MG(f"pow{m}"))
                act.activation(mem_tok, mem_tok, ACT.Copy, scale=t2[:, 0:1]).then_inc(*MA.did(f"n{m}"))
                act.wait_ge(chunk_used, C_KV)
                for kg in range(4):
                    act.wait_ge(*MM(f"t{m}{kg}"))
                    for j in range(4):
                        for l in range(2):
                            k = 4 * kg + j
                            act.activation(mem_h(H_hi, l, k)[:, m * P:(m + 1) * P],
                                           acc[kg % 2][:, j * P:(j + 1) * P], ACT.Copy,
                                           scale=pcol("mem_norm", l * KT + k)).then_inc(*MA.did(f"hi{m}{k}{l}"))
            for c in range(32):
                split(C_KV + c + 1)
                for name in hops_at(B_HOPS, B_SLOTS, 2 * c, 2 * c + 2):
                    attn(name, 3)

            def split_input(r, src, c0):
                ZA.round(r)
                act.wait_ge(chunk_used, c0)
                for k in range(KT):
                    if k == 0:
                        act.wait_ge(*((BV("y1", 3)) if r == 0 else VV("y1", 7)))
                    act.activation(H_hi[:, k * T:(k + 1) * T], src(k), ACT.Copy).then_inc(*ZA.did(f"hi{k}"))

            def out_square(r, n, pair):
                for j in range(2):
                    act.wait_ge(acc_free, 2 * pair + j + 1)
                    if n:
                        act.wait_ge(*OG(f"a{2 * n + j - 2}", r))
                    act.activation(sqt[:, j * T:(j + 1) * T], yt(2 * n + j), ACT.Square)\
                        .then_inc(*OA.did(f"s{2 * n + j}"))

            def out_phase(r, c0, p0, per):
                OA.round(r)
                for n in range(8):
                    for c in range(per):
                        split(c0 + per * n + c + 1)
                        if c == 0 and n:
                            out_square(r, n - 1, p0 + n - 1)
                out_square(r, 7, p0 + 7)

            def norm(r):
                NA.round(r)
                gain = ("x_pre", "norm_pre", "x_pre")[r]
                layer = (0, 1, 1)[r]
                for k in range(KT):
                    act.wait_ge(*NG(f"x{k}", r))
                    act.activation(H_hi[:, k * T:(k + 1) * T], xt(k), ACT.Copy, scale=pcol(gain, layer * KT + k))\
                        .then_inc(*NA.did(f"hi{k}"))
                    act.activation(yt(k), xt(k), ACT.Square).then_inc(*NA.did(f"sq{k}"))

            def cross(l):
                CA.round(l)
                for c in range(16):
                    split(LAYERS_Q[l] + c + 1)
                    for name in hops_at(C_HOPS, C_SLOTS, 4 * c, 4 * c + 4):
                        h = int(name[1])
                        if name[0] == "s":
                            act.wait_ge(*CV(f"nm{h}", l))
                            for t in range(TT):
                                act.activation(cp[:, t * MEM:(t + 1) * MEM], flat(m01)[:, t * MEM:(t + 1) * MEM],
                                               ACT.Exp, bias=nmx[:, t:t + 1], scale=P ** -0.5,
                                               accum_out=ssum[:, t:t + 1]).then_inc(*CA.did(f"p{h}"))
                        elif name[0] == "t":
                            act.wait_ge(*CM(name, l))
                            act.activation(cpt, flat(m23), ACT.Copy).then_inc(*CA.did(f"t{h}"))
                        else:
                            act.wait_ge(*CM(name, l))
                            act.activation(cq[:, h * T:(h + 1) * T], M[0], ACT.Copy, scale=0.5)\
                                .then_inc(*CA.did(f"o{h}"))
                for n in range(4):
                    act.wait_ge(*CV(f"z{n}", l))
                    if n:
                        act.wait_ge(*CV(f"zz{n - 1}", l))
                    act.activation(acc_sq, cz[:, n * T:(n + 1) * T], ACT.Tanh, scale=0.5).then_inc(*CA.did(f"zt{n}"))
                for h in range(MH):
                    act.wait_ge(*CV(f"y{h}", l))
                    act.activation(H_hi[:, h * T:(h + 1) * T], cq[:, h * T:(h + 1) * T], ACT.Copy)\
                        .then_inc(*CA.did(f"hi{h}"))

            split_input(0, xt, C_OUT0)
            out_phase(0, C_OUT0, P_OUT0, 4)
            norm(0)
            cross(0)
            out_phase(1, C_O0, P_O0, 1)
            norm(1)

            def conv_tanh(n):
                pair = P_C + 4 * n + 3
                for j in range(2):
                    act.wait_ge(acc_free, 2 * pair + j + 1)
                    act.activation(uu[:, j * T:(j + 1) * T], bb[:, j * T:(j + 1) * T], ACT.Tanh, scale=0.5)\
                        .then_inc(*VA.did(f"z{j}"))
            for n in range(8):
                for c in range(16):
                    split(C_C + 16 * n + c + 1)
                    if n and c == 0:
                        conv_tanh(n - 1)
                    if c == 1:
                        VA.round(n)
            conv_tanh(7)
            split_input(1, yt, C_OUT1)
            out_phase(2, C_OUT1, P_OUT1, 4)
            norm(2)
            cross(1)
            out_phase(3, C_O1, P_O1, 1)

        @block.tensor
        def _(pe):
            def rows(out, col, n, at_=None):
                for t in range(n):
                    last = pe.matmul(out(t), col(t).broadcast_to([P, P]), ident, start=True, stop=True)
                return last

            def chunk(g, pair, kt0, last_kt, width=T, hi=None, lo=None, ready=None, between=None):
                s = g % SPLIT_SLOTS
                hi = hi or (lambda k: H_hi[:, k * T:(k + 1) * T])
                lo = lo or (lambda k: H_lo[:, k * T:(k + 1) * T])
                pe.wait_ge(lo_ready, g + 1)
                if kt0 == 0 and pair >= 2:
                    pe.wait_ge(acc_free, 2 * (pair - 1))
                for k in range(4):
                    kt = kt0 + k
                    if ready is not None:
                        pe.wait_ge(*ready(kt))
                    for j in range(2):
                        o = s * CW + k * 256 + j * P
                        out = acc[2 * (pair % 2) + j][:, 0:width]
                        pe.matmul(out, w_hi[:, o:o + P], hi(kt), start=kt == 0, stop=False)
                        pe.matmul(out, w_hi[:, o:o + P], lo(kt), start=False, stop=False)
                        last = pe.matmul(out, w_lo[:, o:o + P], hi(kt), start=False, stop=kt == last_kt)
                    if k == 3:
                        last.then_inc(chunk_used, 1)
                    if between is not None:
                        between(k)

            pe.wait_ge(params_in, 32)
            for t in range(TT):
                pe.wait_ge(x_in[t], 16)
            for k in range(KT):
                if k >= 4:
                    pe.wait_ge(*SA(f"hi{k - 4}"))
                if k == 2:
                    pe.wait_ge(*SG("pow"))
                    rows(lambda t: M[1][:, t * P:(t + 1) * P], lambda t: powed[:, t:t + 1], TT)\
                        .then_inc(*SM.did("rows"))
                for t in range(TT):
                    last = pe.transpose(acc[k % 4][:, t * P:(t + 1) * P], x_tok[:, t * D + k * P:t * D + (k + 1) * P],
                                        ident)
                last.then_inc(*SM.did(f"tr{k}"))
            pe.wait_ge(*SA("hi15"))

            def gates():
                pe.wait_ge(*SV("gate_lo"))
                for t in range(TT):
                    for k in range(KT):
                        x = slice(k * T + t * P, k * T + (t + 1) * P)
                        for n, (a, b) in enumerate(((H_hi, gate_hi), (H_lo, gate_hi), (H_hi, gate_lo))):
                            last = pe.matmul(M[0][:, t * 16:(t + 1) * 16], a[:, x], b[:, k * 16:(k + 1) * 16],
                                             start=t == k == n == 0, stop=t == TT - 1 and k == KT - 1 and n == 2,
                                             skip_group_check=True)
                last.then_inc(*SM.did("gates"))

            def decays():
                pe.wait_ge(*SV("g"))
                for n, name in enumerate(("cumsum", "suffix", "half0", "half1")):
                    last = pe.matmul(M[0][:, 32 * n:32 * n + 32], c_(name), g_col, start=True, stop=True)
                last.then_inc(*SM.did("decays"))

            def delta(name, i):
                hc = lambda h, t: bass.ds((2 * i + h) * TT + t, 1)
                ht = [(h, t) for h in range(2) for t in range(TT)]
                o = lambda h, t: slice(h * T + t * P, h * T + (t + 1) * P)
                m = lambda bank, h, t: bank[:, h, t * P:(t + 1) * P]
                if name == "ss":
                    GM.round(i)
                    pe.wait_ge(*GA("sq", i))
                    if i == 0:
                        pe.wait_ge(*SA("decays"))
                    for n in range(16):
                        last = pe.matmul(M[0][:, n:n + 1], sq[:, n * P:(n + 1) * P], ones, start=True, stop=True)
                elif name == "rows":
                    pe.wait_ge(*GV("pw", i))
                    for h, t in ht:
                        n = h * TT + t
                        pe.matmul(m(m01, h, t), powed[:, 8 + n:9 + n].broadcast_to([P, P]), ident, start=True, stop=True)
                        last = pe.matmul(m(m23, h, t), powed[:, n:n + 1].broadcast_to([P, P]), ident, start=True, stop=True)
                elif name == "tr":
                    pe.wait_ge(*GV("qn", i))
                    pe.wait_ge(*EV("s21", i))
                    for h, t in ht:
                        pe.transpose(m(m01, h, t), kc[:, o(h, t)], ident)
                        last = pe.transpose(m(m23, h, t), vc[:, o(h, t)], ident)
                elif name == "dk":
                    pe.wait_ge(*GA("kv", i))
                    pe.wait_ge(*GV("k_out", i))
                    for h, t in ht:
                        pe.matmul(m(m01, h, t), g_col[:, hc(h, t)].broadcast_to([P, P]), c_("cumsum"),
                                  start=True, stop=True)
                        last = pe.matmul(m(m23, h, t), kc[:, o(h, t)], kc[:, o(h, t)], start=True, stop=True)
                elif name == "qb":
                    pe.wait_ge(*GV("nt0", i))
                    for h, t in ht:
                        pe.matmul(m(m01, h, t), kc[:, o(h, t)], qc[:, o(h, t)], start=True, stop=True)
                        last = pe.matmul(m(m23, h, t), beta[:, hc(h, t)].broadcast_to([P, P]), ident,
                                         start=True, stop=True)
                elif name == "p0":
                    pe.wait_ge(*GG("c0", i))
                    pe.wait_ge(*GV("qk", i))
                    for h, t in ht:
                        last = pe.matmul(m(m01, h, t), c_t[:, o(h, t)], ident, start=True, stop=True)
                elif name[0] == "p":
                    pe.wait_ge(*GG("c" + name[1], i))
                    pe.wait_ge(*GV("y" + str(int(name[1]) - 1), i))
                    for h, t in ht:
                        last = pe.matmul(m(m01, h, t), c_t[:, o(h, t)], inv[:, o(h, t)], start=True, stop=True)
                elif name[0] == "y":
                    pe.wait_ge(*GA("p" + name[1], i))
                    for h, t in ht:
                        if name != "y5":
                            pe.matmul(m(m23, h, t), inv_t[:, o(h, t)], prod[:, o(h, t)], start=True, stop=True)
                        last = pe.matmul(m(m01, h, t), prod[:, o(h, t)], inv_t[:, o(h, t)], start=True, stop=True)
                elif name == "uw":
                    pe.wait_ge(*GV("y5", i))
                    for h, t in ht:
                        pe.matmul(m(m01, h, t), inv_t[:, o(h, t)], v_in[:, o(h, t)], start=True, stop=True)
                        last = pe.matmul(m(m23, h, t), k_in[:, o(h, t)], inv_t[:, o(h, t)], start=True, stop=True)
                elif name[0] == "r":
                    c = int(name[1])
                    p0 = CH * (c % 2)
                    if c == 0:
                        pe.wait_ge(*GA("w", i))
                    pe.wait_ge(*GV(f"st{c}", i))
                    for h in range(2):
                        st = state[:, h * HD:(h + 1) * HD]
                        pe.matmul(M[0][p0:p0 + CH, h * HD:(h + 1) * HD], w_t[:, h * T + c * CH:h * T + (c + 1) * CH],
                                  st, start=True, stop=True)
                        last = pe.matmul(m23[:, h, c * CH:(c + 1) * CH], st,
                                         q_dec[:, h * T + c * CH:h * T + (c + 1) * CH], start=True, stop=False)
                elif name[0] == "s":
                    c = int(name[1])
                    t, p0 = c // 2, CH * (c % 2)
                    ps = slice(p0, p0 + CH)
                    pe.wait_ge(*GV(f"vn{c}", i))
                    for h in range(2):
                        vn = v_new[ps, h * HD:(h + 1) * HD]
                        q0 = h * T + t * P + p0
                        last = pe.matmul(m23[:, h, c * CH:(c + 1) * CH], vn, qk_t[ps, q0:q0 + CH],
                                         start=False, stop=True)
                        if c < T // CH - 1:
                            last = pe.matmul(M[1][:, h * HD:(h + 1) * HD], k_out[ps, o(h, t)], vn, start=True, stop=True)
                elif name == "fs":
                    pe.wait_ge(*GA("o", i))
                    for n in range(8):
                        last = pe.matmul(M[0][:, n:n + 1], inv[:, n * P:(n + 1) * P], ones, start=True, stop=True)
                elif name == "fb":
                    pe.wait_ge(*GG("fpow", i))
                    for h, t in ht:
                        n = h * TT + t
                        last = pe.matmul(m(m01, h, t), powed[:, n:n + 1].broadcast_to([P, P]), ident, start=True, stop=True)
                last.then_inc(*GM.did(name))

            def attn(name, i):
                if name == "vt":
                    BM.round(i)
                    if i == 0:
                        pe.wait_ge(*GA("end", 3))
                    else:
                        pe.wait_ge(*BV("y1", i - 1))
                    pe.wait_ge(acc_free, 2 * (P_AB + 4 * (4 + i) + 4))
                    for n in range(8):
                        last = pe.transpose(m01[:, n // TT, (n % TT) * P:(n % TT + 1) * P], vc[:, n * P:(n + 1) * P], ident)
                elif name[0] == "a":
                    h, t = int(name[1]), int(name[2])
                    if t:
                        pe.wait_ge(*BV(f"att{h}{t - 1}", i))
                        for j in range(t):
                            last = pe.transpose(M[2][:, j * P:(j + 1) * P], att[:, j * P:(j + 1) * P], ident)
                    elif h == 0:
                        pe.wait_ge(*BA("v", i))
                        pe.wait_ge(*BV("rk", i))
                    else:
                        pe.wait_ge(*BV("y0", i))
                    if t < TT:
                        if t:
                            pe.wait_ge(*BA(f"p{h}{t - 1}", i))
                        for mp in range(2):
                            r = slice(QK * mp, QK * mp + QK)
                            last = pe.matmul(M[mp][:, 0:(t + 1) * P], qr[r, h * T + t * P:h * T + (t + 1) * P],
                                             kr[r, h * T:h * T + (t + 1) * P], start=True, stop=True)
                elif name[0] == "b":
                    h, t = int(name[1]), int(name[2])
                    pe.wait_ge(*BA(f"at{h}{t}", i))
                    if h and t == 0:
                        pe.wait_ge(*BA("o0", i))
                    for j in range(t + 1):
                        last = pe.matmul(M[3][:, t * P:(t + 1) * P], v_tok[:, h * T + j * P:h * T + (j + 1) * P],
                                         att_t[:, j * P:(j + 1) * P], start=j == 0, stop=j == t)
                elif name[:2] == "fs":
                    pe.wait_ge(*BA("o" + name[2], i))
                    for t in range(TT):
                        last = pe.matmul(M[0][:, t:t + 1], o_sq[:, t * P:(t + 1) * P], ones, start=True, stop=True)
                else:
                    pe.wait_ge(*BG("pow" + name[2], i))
                    last = rows(lambda t: M[0][:, t * P:(t + 1) * P], lambda t: powed[:, t:t + 1], TT)
                last.then_inc(*BM.did(name))

            for it in range(AB_ITERS):
                hop, i = (delta, it - 1) if it <= 4 else (attn, it - 5)
                names, slots = (D_HOPS, D_SLOTS) if it <= 4 else (B_HOPS, B_SLOTS)
                for c in range(16):
                    def between(k):
                        if it:
                            for name in hops_at(names, slots, 4 * c + k, 4 * c + k + 1):
                                hop(name, i)
                    if it == 0 and c == 4:
                        gates()
                    if it == 0 and c == 6:
                        decays()
                    chunk(C_AB + 16 * it + c, P_AB + 4 * it + c // 4, 4 * (c % 4), KT - 1, between=between,
                          ready=(lambda kt: SV(f"lo{kt}")) if it == 0 and c < 4 else None)

            for m in range(2):
                pe.wait_ge(*MA(f"n{m}"))
                pe.wait_ge(acc_free, 2 * (P_KV - 1))
                for kg in range(4):
                    if m or kg >= 2:
                        q = 4 * m + kg - 2
                        pe.wait_ge(*MV(f"lo{q // 4}{4 * (q % 4) + 3}1"))
                    for j in range(4):
                        last = pe.transpose(acc[kg % 2][:, j * P:(j + 1) * P],
                                            mem_tok[:, (4 * kg + j) * P:(4 * kg + j + 1) * P], ident)
                    last.then_inc(*MM.did(f"t{m}{kg}"))
            pe.wait_ge(*MV("lo1151"))

            def value_transposes(l, j, pair):
                pe.wait_ge(*MV(f"vf{l}{j}"))
                for n in range(4):
                    last = pe.transpose(acc[2 * (pair % 2)][:, n * P:(n + 1) * P], v_feat[:, n * P:(n + 1) * P], ident)
                last.then_inc(*MM.did(f"v{l}{j}"))

            for c in range(32):
                l, q = c // 16, c // 4 - 1

                def between(k):
                    if k % 2:
                        for name in hops_at(B_HOPS, B_SLOTS, 2 * c + k // 2, 2 * c + k // 2 + 1):
                            attn(name, 3)
                if q >= 0 and c % 4 == 1 and q % 4 >= 2:
                    value_transposes(q // 4, q % 4, P_KV + q)
                chunk(C_KV + c, P_KV + c // 4, 4 * (c % 4), KT - 1, width=MEM, between=between,
                      hi=lambda k: mem_h(H_hi, l, k), lo=lambda k: mem_h(H_lo, l, k))
            value_transposes(1, 3, P_KV + 7)

            def out_phase(c0, p0, per, ready):
                for n in range(8):
                    for c in range(per):
                        chunk(c0 + per * n + c, p0 + n, 4 * c, 4 * per - 1, ready=ready if n == 0 else None)

            def norm(r):
                NM.round(r)
                pe.wait_ge(*OG("a15", r))
                for t in range(TT):
                    last = pe.matmul(M[0][:, t:t + 1], acc_sq[:, t * P:(t + 1) * P], ones, start=True, stop=True)
                last.then_inc(*NM.did("ss"))
                pe.wait_ge(*NG("pow", r))
                rows(lambda t: M[1][:, t * P:(t + 1) * P], lambda t: powed[:, t:t + 1], TT).then_inc(*NM.did("rows"))

            def next_rms(r, c):
                if c == 5:
                    pe.wait_ge(*NV("sum", r))
                    for t in range(TT):
                        last = pe.matmul(M[0][:, t:t + 1], acc_sq[:, t * P:(t + 1) * P], ones, start=True, stop=True)
                    last.then_inc(*NM.did("ss2"))
                if c == 6:
                    pe.wait_ge(*NG("pow2", r))
                    rows(lambda t: M[1][:, t * P:(t + 1) * P], lambda t: powed[:, t:t + 1], TT)\
                        .then_inc(*NM.did("rows2"))

            def cross(l, r):
                CM.round(l)

                def hop(name):
                    h = int(name[1])
                    if name[0] == "s":
                        pe.wait_ge(acc_free, 2 * (P_Q[l] + h // 2) + h % 2 + 1)
                        pe.wait_ge(*(NV("rs", r) if h == 0 else CA(f"o{h - 1}", l)))
                        for t in range(TT):
                            last = pe.matmul(flat(m01)[:, t * MEM:(t + 1) * MEM], cq[:, h * T + t * P:h * T + (t + 1) * P],
                                             mkt(l, h), start=True, stop=True)
                    elif name[0] == "t":
                        pe.wait_ge(*CV(f"p{h}", l))
                        for t in range(TT):
                            for m in range(2):
                                last = pe.transpose(m23[:, m, t * P:(t + 1) * P],
                                                    cp[:, t * MEM + m * P:t * MEM + (m + 1) * P], ident)
                    else:
                        pe.wait_ge(*CA(f"t{h}", l))
                        for m in range(2):
                            v0 = (l * 2 + m) * MH * HD + h * HD
                            last = pe.matmul(M[0], mv[:, v0:v0 + HD], cpt[:, m * T:(m + 1) * T], start=m == 0, stop=m == 1)
                    last.then_inc(*CM.did(name))
                for c in range(16):
                    def between(k):
                        for name in hops_at(C_HOPS, C_SLOTS, 4 * c + k, 4 * c + k + 1):
                            hop(name)
                    next_rms(r, c)
                    chunk(LAYERS_Q[l] + c, P_Q[l] + c // 4, 4 * (c % 4), KT - 1, between=between,
                          ready=(lambda kt: NV(f"lo{kt}", r)) if c < 4 else None)
                out_phase(LAYERS_O[l], P_O[l], 1, lambda kt: CV(f"lo{kt}", l))

            out_phase(C_OUT0, P_OUT0, 4, lambda kt: ZV(f"lo{kt}", 0))
            norm(0)
            cross(0, 0)
            norm(1)
            for n in range(8):
                for c in range(16):
                    if n == 0:
                        next_rms(1, c)
                    chunk(C_C + 16 * n + c, P_C + 4 * n + c // 4, 4 * (c % 4), KT - 1,
                          ready=(lambda kt: NV(f"lo{kt}", 1)) if n == 0 and c < 4 else None)
            out_phase(C_OUT1, P_OUT1, 4, lambda kt: ZV(f"lo{kt}", 1))
            norm(2)
            cross(1, 2)
            norm(3)
            for n in range(16):
                kg, t = n // TT, n % TT
                pe.wait_ge(*NG(f"x{4 * kg + 3}", 3))
                if n >= 4:
                    pe.wait_ge(*FV(f"o{n - 4}"))
                else:
                    pe.wait_ge(acc_free, 2 * (P_O1 + 8))
                for j in range(4):
                    last = pe.transpose(acc[n % 4][:, j * P:(j + 1) * P],
                                        X[:, (4 * kg + j) * T + t * P:(4 * kg + j) * T + (t + 1) * P], ident)
                last.then_inc(*FM.did(f"o{n}"))

        @block.vector
        def _(dve):
            TTO, STT, TS = dve.tensor_tensor, dve.scalar_tensor_tensor, dve.tensor_scalar

            def split(g):
                if g >= CHUNKS:
                    return
                c, s = g % RAW_SLOTS, g % SPLIT_SLOTS
                dve.wait_ge(hi_ready, g + 1)
                TTO(w_lo[:, s * CW:(s + 1) * CW], raw[:, c * CW:(c + 1) * CW],
                    w_hi[:, s * CW:(s + 1) * CW].bitcast(F32), ALU.subtract).then_inc(lo_ready, 1)

            def bank(pair, n, width=T):
                return acc[2 * (pair % 2) + n][:, 0:width]

            dve.wait_ge(params_in, 32)
            dve.wait_ge(gate_in, 32)
            lam4 = lam_in.rearrange("p (a b n) -> p a b n", a=2, b=2)
            TTO(norm_buf[:, 0:2 * QK].rearrange("p (a n) -> p a n", a=2), lam4[:, :, 0, :], lam4[:, :, 1, :], ALU.mult)\
                .then_inc(*SV.did())
            dve.wait_ge(*SV.last())
            dve.reduce_sum(lam2[:, 0:2], norm_buf[:, 0:2 * QK].rearrange("p (a n) -> p a n", a=2), axis=AX.X)\
                .then_inc(*SV.did("lamsum"))
            dve.wait_ge(*SA("ss3"))
            TS(stat[:, 0:4], stat[:, 0:4], 1.0 / D, EPS, ALU.mult, ALU.add).then_inc(*SV.did("stat"))
            split(0)
            dve.wait_ge(*SA("gate_hi"))
            TTO(gate_lo[:, :], gate_w, gate_hi[:, :].bitcast(F32), ALU.subtract).then_inc(*SV.did("gate_lo"))
            dve.wait_ge(*SM("rows"))
            dve.tensor_copy(rs[:, :], M[1]).then_inc(*SV.did("rs"))

            def start_low(k):
                dve.wait_ge(*SA(f"hi{k}"))
                TTO(H_lo[:, k * T:(k + 1) * T], norm_buf[:, (k % 2) * T:(k % 2 + 1) * T],
                    H_hi[:, k * T:(k + 1) * T].bitcast(F32), ALU.subtract).then_inc(*SV.did(f"lo{k}"))
            for k in range(KT):
                dve.wait_ge(*SA(f"copy{k}"))
                dve.wait_ge(*SV.last())
                STT(out=norm_buf[:, (k % 2) * T:(k % 2 + 1) * T], in0=acc[k % 4][:, :], scalar=pcol("norm_pre", k),
                    in1=rs[:, :], op0=ALU.mult, op1=ALU.mult).then_inc(*SV.did(f"norm{k}"))
                if k:
                    start_low(k - 1)
            start_low(KT - 1)

            def gates_in():
                dve.wait_ge(*SM("gates"))
                g16 = M[0][:, 0:TT * 16].rearrange("p (t n) -> p n t", n=16)
                v = lambda t: t.rearrange("p (h t) -> p h t", t=TT)
                dve.tensor_copy(v(t1), g16[:, 0:HEADS, :]).then_inc(*SV.did())
                TTO(v(t2), g16[:, HEADS:2 * HEADS, :], over_row(p_("dt_bias"), HEADS, TT), ALU.add)\
                    .then_inc(*SV.did("gates"))

            def gates_out():
                dve.wait_ge(*SA("small_exp"))

                def then(ins, name=None):
                    ins.then_inc(*SV.did(name))
                    dve.wait_ge(*SV.last())
                then(STT(out=neg_lam, in0=lam2[:, 1:2], scalar=LAM_INIT, in1=lam2[:, 0:1], op0=ALU.subtract,
                         op1=ALU.subtract))
                then(TS(a_gain, p_("a_norm"), 0.5, None, ALU.mult))
                then(TS(b_gain, p_("b_norm"), 0.5 * (1.0 - LAM_INIT), None, ALU.mult))
                then(TS(t1, t1, 1.0, None, ALU.add))
                then(dve.reciprocal(beta, t1))
                then(TS(v_scale, beta, 0.5, None, ALU.mult))
                then(TS(t4, t3, 2.0, None, ALU.add))
                then(dve.reciprocal(t4, t4))
                then(TTO(t4, t3, t4, ALU.mult))
                then(TTO(t5, t4, t4, ALU.mult))
                then(TS(t3, t5, 1.0 / 15, None, ALU.mult))
                for n in (13, 11, 9, 7, 5, 3):
                    then(STT(out=t3, in0=t3, scalar=1.0 / n, in1=t5, op0=ALU.add, op1=ALU.mult))
                then(STT(out=t3, in0=t3, scalar=1.0, in1=t4, op0=ALU.add, op1=ALU.mult))
                then(TS(t2, t2, 0.0, None, ALU.max))
                then(STT(out=t2, in0=t3, scalar=2.0, in1=t2, op0=ALU.mult, op1=ALU.add))
                v = lambda t: t.rearrange("p (h t) -> p h t", t=TT)
                then(STT(out=v(g_col), in0=v(t2), scalar=-1.0, in1=over_row(p_("A_log"), HEADS, TT), op0=ALU.mult,
                         op1=ALU.mult), "g")

            def decays():
                dve.wait_ge(*SM("decays"))
                dve.tensor_copy(decay, M[0][:, 0:32]).then_inc(*SV.did("decay"))
                dve.wait_ge(*SA("decays"))
                TTO(k_in_scale, k_in_scale, beta, ALU.mult).then_inc(*SV.did("kin"))

            def delta(name, i):
                def then(ins, tag=None):
                    ins.then_inc(*GV.did(tag))
                    dve.wait_ge(*GV.last())
                hc = bass.ds(2 * i * TT, 2 * TT)
                if name == "ss":
                    GV.round(i)
                    dve.wait_ge(*GM("ss", i))
                    TS(stat, M[0][:, 0:16], 0.25, EPS, ALU.mult, ALU.add).then_inc(*GV.did("stat"))
                    dve.wait_ge(*GG("pow", i))
                    TS(powed[:, 0:8], powed[:, 0:8], 0.5 * HD ** -0.5, None, ALU.mult).then_inc(*GV.did())
                    TS(powed[:, 8:16], powed[:, 8:16], 0.5, None, ALU.mult).then_inc(*GV.did("pw"))
                elif name == "rows":
                    dve.wait_ge(*GM("rows", i))
                    TTO(kc, kc, flat(m01), ALU.mult).then_inc(*GV.did())
                    TTO(qc, qc, flat(m23), ALU.mult).then_inc(*GV.did("qn"))
                elif name == "tr":
                    dve.wait_ge(*GA("kv", i))
                    TTO(tiles(k_out), psum_tiles(m01), over_row(k_out_scale[:, hc], 8, P), ALU.mult)\
                        .then_inc(*GV.did("k_out"))
                elif name == "dk":
                    dve.wait_ge(*GM("dk", i))
                    then(TTO(tiles(gam), psum_tiles(m01), over_row(decay[:, hc], 8, P), ALU.subtract))
                    then(TTO(tiles(gam), tiles(gam), over_tiles(c_("causal"), 8), ALU.add), "gam")
                    dve.wait_ge(*GA("edec", i))
                    TTO(q_dec, qc, prod, ALU.mult).then_inc(*GV.did("qd"))
                    dve.wait_ge(*GA("gam", i))
                    then(TTO(n_t, flat(m23), gam, ALU.mult), "nt0")
                elif name == "qb":
                    dve.wait_ge(*GM("qb", i))
                    TTO(n_t, flat(m23), n_t, ALU.mult).then_inc(*GV.did("nt"))
                    TTO(qk_t, flat(m01), gam, ALU.mult).then_inc(*GV.did("qk"))
                elif name == "p0":
                    dve.wait_ge(*GM("p0", i))
                    TTO(tiles(inv), over_tiles(ident, 8), psum_tiles(m01), ALU.subtract).then_inc(*GV.did())
                    TTO(tiles(inv_t), over_tiles(ident, 8), tiles(c_t), ALU.subtract).then_inc(*GV.did("y0"))
                elif name[0] == "y":
                    dve.wait_ge(*GM(name, i))
                    if name != "y5":
                        dve.wait_ge(*GV.last())
                        TTO(inv, inv, flat(m23), ALU.subtract).then_inc(*GV.did())
                    TTO(inv_t, inv_t, flat(m01), ALU.subtract).then_inc(*GV.did(name))
                elif name == "uw":
                    dve.memset(state, 0.0).then_inc(*GV.did("st0"))
                elif name[0] == "r":
                    c = int(name[1])
                    t, p0 = c // 2, CH * (c % 2)
                    ps = slice(p0, p0 + CH)
                    dve.wait_ge(*GM(name, i))
                    TTO(head2(v_new[ps, :]), head2(u_tok[ps, :])[:, :, t * P:(t + 1) * P],
                        head2(M[0][ps, 0:2 * HD]), ALU.subtract).then_inc(*GV.did(f"vn{c}"))
                elif name[0] == "s" and name != "s7":
                    c = int(name[1])
                    t, half = c // 2, c % 2
                    dve.wait_ge(*GM(name, i))
                    for h in range(2):
                        o = slice(h * HD, (h + 1) * HD)
                        STT(out=state[:, o], in0=state[:, o], scalar=chunk_decay[:, bass.ds(half * 32 + (2 * i + h) * TT + t, 1)],
                            in1=M[1][:, o], op0=ALU.mult, op1=ALU.add).then_inc(*GV.did(f"st{c + 1}"))
                elif name == "fs":
                    dve.wait_ge(*GM("fs", i))
                    TS(stat[:, 0:8], M[0][:, 0:8], 1.0 / HD, EPS, ALU.mult, ALU.add).then_inc(*GV.did("fstat"))
                elif name == "fb":
                    dve.wait_ge(*GM("fb", i))
                    then(STT(out=prod, in0=prod, scalar=a_gain, in1=flat(m01), op0=ALU.mult, op1=ALU.mult))
                    y = X[:, bass.ds(2 * i * T, 2 * T)]
                    TTO(y, y, prod, ALU.mult).then_inc(*GV.did("end"))

            def attn(name, i):
                def then(ins, tag=None):
                    ins.then_inc(*BV.did(tag))
                    dve.wait_ge(*BV.last())
                if name == "begin":
                    BV.round(i)
                    dve.wait_ge(tables_in, 16)
                    cos = rope_tab[:, 0:T].unsqueeze(1).broadcast_to([P, 2, T])
                    sin = rope_tab[:, T:2 * T].unsqueeze(1).broadcast_to([P, 2, T])
                    for src, dst, tag in ((qc, qr, "rq"), (kc, kr, "rk")):
                        dve.wait_ge(*BA(tag, i))
                        TTO(head2(dst), head2(src), cos, ALU.mult).then_inc(*BV.did())
                        then(TTO(head2(rot), head2(rot), sin, ALU.mult))
                        TTO(dst, dst, rot, ALU.add).then_inc(*BV.did(tag))
                elif name[0] == "a" and name[2] != "4":
                    h, t = int(name[1]), int(name[2])
                    n = (t + 1) * P
                    dve.wait_ge(*BM(name, i))
                    then(dve.memset(m01[0:CH, :, n - CH:n], NEG))
                    then(dve.reduce_max(mx[:, 0:2], m01[:, :, 0:n], axis=AX.X))
                    TS(nmx[:, 0:2], mx[:, 0:2], -QK ** -0.5, None, ALU.mult).then_inc(*BV.did(f"nm{h}{t}"))
                    dve.wait_ge(*BA(f"p{h}{t}", i))
                    then(dve.reciprocal(rsum[:, 0:2], ssum[:, 0:2]))
                    TTO(coef, rsum[:, 1:2], neg_lam, ALU.mult).then_inc(*BV.did())
                    then(TS(att[:, 0:n], prob[:, 0:n], rsum[:, 0:1], None, ALU.mult))
                    STT(out=att[:, 0:n], in0=prob[:, T:T + n], scalar=coef, in1=att[:, 0:n], op0=ALU.mult,
                        op1=ALU.add).then_inc(*BV.did(f"att{h}{t}"))
                elif name[:2] == "fs":
                    dve.wait_ge(*BM(name, i))
                    TS(stat[:, 0:4], M[0][:, 0:4], 1.0 / HD, EPS, ALU.mult, ALU.add).then_inc(*BV.did("stat" + name[2]))
                elif name[:2] == "fb":
                    h = int(name[2])
                    dve.wait_ge(*BM(name, i))
                    then(STT(out=o_sb, in0=o_sb, scalar=b_gain, in1=M[0], op0=ALU.mult, op1=ALU.mult))
                    y = xt(HEADS + 2 * i + h)
                    TTO(y, y, o_sb, ALU.mult).then_inc(*BV.did(f"y{h}"))

            def convolve(it, sec, n):
                pair = P_AB + 4 * it + 1 + sec
                src, dst = bank(pair, n), (qc, kc, vc)[sec][:, n * T:(n + 1) * T]
                tap = lambda k: pcol("a_conv", (8 * sec + 2 * it + n) * 4 + k)
                dve.wait_ge(chunk_used, done_at(pair))
                TS(dst, src, tap(3), None, ALU.mult).then_inc(*EV.did())
                for d in (1, 2, 3):
                    dve.wait_ge(*EV.last())
                    ins = STT(out=dst[:, d:T], in0=src[:, 0:T - d], scalar=tap(3 - d), in1=dst[:, d:T],
                              op0=ALU.mult, op1=ALU.add)
                    if d < 3:
                        ins.then_inc(*EV.did())
                    else:
                        ins.then_inc(acc_free, 1)

            def gate(it, sec, n):
                dst, o = (qc, kc, vc)[sec], slice(n * T, (n + 1) * T)
                dve.wait_ge(*EA(f"t{sec}{n}", it))
                STT(out=dst[:, o], in0=tanh_t[:, o], scalar=1.0, in1=dst[:, o], op0=ALU.add, op1=ALU.mult)\
                    .then_inc(*EV.did(f"s{sec}{n}"))

            def keep(it, sec, n):
                pair = P_AB + 4 * it + 1 + sec
                dve.wait_ge(chunk_used, done_at(pair))
                dve.tensor_copy((qc, kc, vc)[sec][:, n * T:(n + 1) * T], bank(pair, n)).then_inc(acc_free, 1)

            def gate_z(it):
                pair = P_AB + 4 * it
                if it == 0:
                    dve.wait_ge(spilled, 16 * KT)
                for n in range(2):
                    dve.wait_ge(z_tanh, 2 * it + n + 1)
                    head = (HEADS if it >= 4 else 0) + 2 * (it % 4) + n
                    STT(out=xt(head), in0=tanh_t[:, n * T:(n + 1) * T], scalar=1.0, in1=bank(pair, n), op0=ALU.add,
                        op1=ALU.mult).then_inc(acc_free, 1)

            def evacuate(it, sec, c):
                if it < 4:
                    if c:
                        gate(it, sec, c - 1)
                    if c < 2:
                        convolve(it, sec, c)
                elif c < 2:
                    keep(it, sec, c)

            for it in range(AB_ITERS):
                reply, i = (delta, it - 1) if it <= 4 else (attn, it - 5)
                for c in range(16):
                    split(C_AB + 16 * it + c + 1)
                    if it and c < 3:
                        evacuate(it - 1, 2, c)
                    if c == 2:
                        EV.round(it)
                    if it == 0 and c == 4:
                        gates_in()
                    if c == 4:
                        gate_z(it)
                    if it == 0 and c == 5:
                        gates_out()
                    if it == 0 and c == 6:
                        decays()
                    for sec, at_ in ((0, 8), (1, 12)):
                        if at_ <= c < at_ + 3:
                            evacuate(it, sec, c - at_)
                    if it:
                        if c == 2:
                            reply("begin", i)
                        names, slots = (D_HOPS, D_SLOTS) if it <= 4 else (B_HOPS, B_SLOTS)
                        for name in hops_at(names, slots, 4 * c, 4 * c + 4):
                            reply(name, i)

            for c in range(2):
                keep(7, 2, c)
            attn("begin", 3)
            for m in range(2):
                dve.wait_ge(*MA(f"ss{m}"))
                TTO(t1[:, 2:3], t1[:, 0:1], t1[:, 1:2], ALU.add).then_inc(*MV.did())
                dve.wait_ge(*MV.last())
                TS(t1[:, 3:4], t1[:, 2:3], 1.0 / D, EPS, ALU.mult, ALU.add).then_inc(*MV.did(f"stat{m}"))
                for kg in range(4):
                    dve.wait_ge(*MA(f"hi{m}{4 * kg + 3}1"))
                    for j in range(4):
                        for l in range(2):
                            k = 4 * kg + j
                            STT(out=mem_h(H_lo, l, k)[:, m * P:(m + 1) * P], in0=acc[kg % 2][:, j * P:(j + 1) * P],
                                scalar=pcol("mem_norm", l * KT + k), in1=mem_h(H_hi, l, k)[:, m * P:(m + 1) * P].bitcast(F32),
                                op0=ALU.mult, op1=ALU.subtract).then_inc(*MV.did(f"lo{m}{k}{l}"))

            def take_kv(q, c):
                l, j, pair = q // 4, q % 4, P_KV + q
                if c == 0:
                    dve.wait_ge(chunk_used, done_at(pair))
                    for n in range(2):
                        if j < 2:
                            dve.tensor_copy(mkt(l, 2 * j + n), bank(pair, n, MEM)).then_inc(acc_free, 1)
                        else:
                            dve.tensor_copy(v_feat[:, n * MEM:(n + 1) * MEM], bank(pair, n, MEM))\
                                .then_inc(*MV.did(f"vf{l}{j}"))
                elif c == 2 and j >= 2:
                    dve.wait_ge(*MM(f"v{l}{j}"))
                    for n in range(2):
                        h = 2 * (j - 2) + n
                        dst = mv[:, l * 2 * MH * HD:(l + 1) * 2 * MH * HD].rearrange("p (m h n) -> p m h n", m=2, h=MH)
                        dve.tensor_copy(dst[:, :, h, :], bank(pair, 0)[:, n * MEM:(n + 1) * MEM].rearrange(
                            "p (m n) -> p m n", m=2)).then_inc(acc_free, 1)
            for c in range(32):
                split(C_KV + c + 1)
                if c >= 4:
                    take_kv(c // 4 - 1, c % 4)
                for name in hops_at(B_HOPS, B_SLOTS, 2 * c, 2 * c + 2):
                    attn(name, 3)
            take_kv(7, 0)
            take_kv(7, 2)

            def split_input(r, src):
                ZV.round(r)
                for k in range(KT):
                    dve.wait_ge(*ZA(f"hi{k}", r))
                    TTO(H_lo[:, k * T:(k + 1) * T], src(k), H_hi[:, k * T:(k + 1) * T].bitcast(F32), ALU.subtract)\
                        .then_inc(*ZV.did(f"lo{k}"))

            def out_phase(c0, p0, per):
                def take(n):
                    dve.wait_ge(chunk_used, done_at(p0 + n))
                    for j in range(2):
                        dve.tensor_copy(yt(2 * n + j), bank(p0 + n, j)).then_inc(acc_free, 1)
                for n in range(8):
                    for c in range(per):
                        split(c0 + per * n + c + 1)
                        if c == 0 and n:
                            take(n - 1)
                take(7)

            def norm(r):
                NV.round(r)
                dve.wait_ge(*NM("ss", r))
                TS(stat[:, 0:4], M[0][:, 0:4], 1.0 / D, EPS, ALU.mult, ALU.add).then_inc(*NV.did("stat"))
                dve.wait_ge(*NM("rows", r))
                post = ("norm_post", "x_post", "norm_post", "x_post")[r]
                pre = ("x_pre", "norm_pre", "x_pre", None)[r]
                layer, next_layer = r // 2, (0, 1, 1, 1)[r]

                def low(k):
                    dve.wait_ge(*NA(f"hi{k}", r))
                    STT(out=H_lo[:, k * T:(k + 1) * T], in0=xt(k), scalar=pcol(pre, next_layer * KT + k),
                        in1=H_hi[:, k * T:(k + 1) * T].bitcast(F32), op0=ALU.mult, op1=ALU.subtract)\
                        .then_inc(*NV.did(f"lo{k}"))
                for k in range(KT):
                    if k == 0:
                        dve.wait_ge(acc_free, 2 * (P_OUT0 + 8, P_O0 + 8, P_OUT1 + 8, P_O1 + 8)[r])
                    STT(out=yt(k), in0=yt(k), scalar=pcol(post, layer * KT + k), in1=M[1], op0=ALU.mult, op1=ALU.mult)\
                        .then_inc(*(NV if r < 3 else FV).did(f"y{k}"))
                    if k >= 2 and pre:
                        low(k - 2)
                if pre:
                    low(KT - 2)
                    low(KT - 1)
                    dve.wait_ge(*NA("sq15", r))

            def sum_squares(r, c):
                if c < 4:
                    o = slice(c * P, (c + 1) * P)
                    dve.reduce_sum(acc_sq[:, o], Y[:, :].rearrange("p (k t) -> p t k", k=KT)[:, o, :], axis=AX.X)\
                        .then_inc(*NV.did("sum"))
                elif c == 5:
                    dve.wait_ge(*NM("ss2", r))
                    TS(stat[:, 0:4], M[0][:, 0:4], 1.0 / D, EPS, ALU.mult, ALU.add).then_inc(*NV.did("stat2"))
                elif c == 6:
                    dve.wait_ge(*NM("rows2", r))
                    dve.tensor_copy(rs[:, :], M[1]).then_inc(*NV.did("rs"))
                    dve.wait_ge(*NV.last())

            def cross(l, r):
                CV.round(l)

                def then(ins, tag=None):
                    ins.then_inc(*CV.did(tag))
                    dve.wait_ge(*CV.last())

                def take(n):
                    dve.wait_ge(chunk_used, done_at(P_Q[l] + n))
                    for j in range(2):
                        dst = (cq, cz)[n // 2][:, (2 * (n % 2) + j) * T:(2 * (n % 2) + j + 1) * T]
                        TTO(dst, bank(P_Q[l] + n, j), rs[:, :], ALU.mult).then_inc(acc_free, 1)
                        if n >= 2:
                            dve.wait_ge(acc_free, 2 * (P_Q[l] + n) + j + 1)
                            TS(coef, minus_half[:, 0:1], 1.0, None, ALU.mult).then_inc(*CV.did(f"z{2 * (n - 2) + j}"))

                def reply(name):
                    h = int(name[1])
                    s4 = flat(m01).rearrange("p (t m) -> p t m", m=MEM)
                    if name[0] == "s":
                        dve.wait_ge(*CM(name, l))
                        then(dve.reduce_max(mx, s4, axis=AX.X))
                        TS(nmx, mx, -P ** -0.5, None, ALU.mult).then_inc(*CV.did(f"nm{h}"))
                        dve.wait_ge(*CA(f"p{h}", l))
                        then(dve.reciprocal(rsum, ssum))
                        c4 = cp.rearrange("p (t m) -> p t m", m=MEM)
                        TTO(c4, c4, over_row(rsum, TT, MEM), ALU.mult).then_inc(*CV.did(f"p{h}"))
                for c in range(16):
                    sum_squares(r, c)
                    split(LAYERS_Q[l] + c + 1)
                    if c in (6, 8, 12):
                        take({6: 0, 8: 1, 12: 2}[c])
                    for name in hops_at(C_HOPS, C_SLOTS, 4 * c, 4 * c + 4):
                        reply(name)
                take(3)
                for n in range(4):
                    o = slice(n * T, (n + 1) * T)
                    dve.wait_ge(*CA(f"zt{n}", l))
                    STT(out=cz[:, o], in0=acc_sq, scalar=1.0, in1=cz[:, o], op0=ALU.add, op1=ALU.mult)\
                        .then_inc(*CV.did(f"zz{n}"))
                dve.wait_ge(*CV.last())
                dve.wait_ge(*CA("o3", l))
                for h in range(MH):
                    o = slice(h * T, (h + 1) * T)
                    TTO(cq[:, o], cq[:, o], cz[:, o], ALU.mult).then_inc(*CV.did(f"y{h}"))
                for h in range(MH):
                    o = slice(h * T, (h + 1) * T)
                    dve.wait_ge(*CA(f"hi{h}", l))
                    TTO(H_lo[:, o], cq[:, o], H_hi[:, o].bitcast(F32), ALU.subtract).then_inc(*CV.did(f"lo{h}"))
                out_phase(LAYERS_O[l], P_O[l], 1)

            def take_conv(n, j):
                pair = P_C + 4 * n + j
                dve.wait_ge(chunk_used, done_at(pair))
                for k in range(2):
                    o = slice(k * T, (k + 1) * T)
                    dst = (uu, cu, bb, bb)[j]
                    if j == 3:
                        dve.wait_ge(*VV.last())
                    TTO(dst[:, o], bank(pair, k), rs[:, :], ALU.mult).then_inc(acc_free, 1)
                dve.wait_ge(acc_free, 2 * (pair + 1))
                for k in range(2):
                    o = slice(k * T, (k + 1) * T)
                    tap = lambda d: pcol("c_conv", (2 * n + k) * 3 + d)
                    if j == 1:
                        TTO(cu[:, o], cu[:, o], uu[:, o], ALU.mult).then_inc(*VV.did())
                        dve.wait_ge(*VV.last())
                        TS(cv[:, o], cu[:, o], tap(2), None, ALU.mult).then_inc(*VV.did())
                        for d in (1, 2):
                            dve.wait_ge(*VV.last())
                            STT(out=cv[:, k * T + d:(k + 1) * T], in0=cu[:, k * T:(k + 1) * T - d], scalar=tap(2 - d),
                                in1=cv[:, k * T + d:(k + 1) * T], op0=ALU.mult, op1=ALU.add).then_inc(*VV.did())
                    elif j == 2:
                        if k == 0:
                            dve.wait_ge(*VV.last())
                        TTO(cv[:, o], cv[:, o], bb[:, o], ALU.mult).then_inc(*VV.did())
                    elif j == 3:
                        dve.wait_ge(*VA(f"z{k}", n))
                        STT(out=bb[:, o], in0=uu[:, o], scalar=1.0, in1=bb[:, o], op0=ALU.add, op1=ALU.mult)\
                            .then_inc(*VV.did())
                        dve.wait_ge(*VV.last())
                        STT(out=yt(2 * n + k), in0=cv[:, o], scalar=0.5, in1=bb[:, o], op0=ALU.mult, op1=ALU.mult)\
                            .then_inc(*VV.did(f"y{k}"))

            split_input(0, xt)
            out_phase(C_OUT0, P_OUT0, 4)
            norm(0)
            cross(0, 0)
            norm(1)
            for n in range(8):
                for c in range(16):
                    if n == 0:
                        sum_squares(1, c)
                    split(C_C + 16 * n + c + 1)
                    if n and c == 0:
                        take_conv(n - 1, 3)
                    if c == 1:
                        VV.round(n)
                    if c == (6 if n == 0 else 4):
                        take_conv(n, 0)
                    if c in (8, 12):
                        take_conv(n, c // 4 - 1)
            take_conv(7, 3)
            split_input(1, yt)
            out_phase(C_OUT1, P_OUT1, 4)
            norm(2)
            cross(1, 2)
            norm(3)
            for n in range(16):
                dve.wait_ge(*FM(f"o{n}"))
                dve.wait_ge(*NG(f"x{4 * (n // 4) + 3}", 3))
                dve.tensor_copy(yt(n), acc[n % 4][:, :]).then_inc(*FV.did(f"o{n}"))

        @block.gpsimd
        def _(pool):
            def power(src, dst, n):
                return pool.tensor_tensor(dst[:, 0:n], src[:, 0:n], minus_half[:, 0:n], ALU.pow)

            pool.memset(minus_half, -0.5).then_inc(const_set, 1)
            pool.wait_ge(const_set, 1)
            pool.wait_ge(*SV("stat"))
            power(stat, powed, 4).then_inc(*SG.did("pow"))

            for i in range(4):
                GG.round(i)
                if i:
                    pool.wait_ge(*GM("fb", i - 1))
                pool.wait_ge(*GV("stat", i))
                power(stat, powed, 16).then_inc(*GG.did("pow"))
                for s in range(len(LEVELS)):
                    if s == 0:
                        pool.wait_ge(*GV("nt", i))
                    else:
                        pool.wait_ge(*GM(f"p{s - 1}", i))
                        if s == 1:
                            pool.wait_ge(*GV("y0", i))
                    pool.tensor_tensor(tiles(c_t), tiles(n_t), over_tiles(level_mask(s), 8), ALU.mult)\
                        .then_inc(*GG.did(f"c{s}"))
                pool.wait_ge(*GV("fstat", i))
                power(stat, powed, 8).then_inc(*GG.did("fpow"))

            def attention_powers(i):
                BG.round(i)
                for h in range(2):
                    if h:
                        pool.wait_ge(*BM("fb0", i))
                    pool.wait_ge(*BV(f"stat{h}", i))
                    power(stat, powed, 4).then_inc(*BG.did(f"pow{h}"))
            pool.wait_ge(*GM("fb", 3))
            for i in range(3):
                attention_powers(i)
            for m in range(2):
                pool.wait_ge(*MV(f"stat{m}"))
                if m:
                    pool.wait_ge(*MA("n0"))
                pool.tensor_tensor(t2[:, 0:1], t1[:, 3:4], minus_half[:, 0:1], ALU.pow).then_inc(*MG.did(f"pow{m}"))
            attention_powers(3)

            for r in range(4):
                OG.round(r)
                NG.round(r)
                if r == 0:
                    pool.wait_ge(reloaded, 16 * KT)
                else:
                    pool.wait_ge(*(CV("zz3", r // 2) if r != 2 else NV("rs", 1)))
                pool.memset(acc_sq, 0.0).then_inc(*OG.did())
                for k in range(KT):
                    pool.wait_ge(*OA(f"s{k}", r))
                    pool.wait_ge(*OG.last())
                    pool.tensor_tensor(acc_sq, acc_sq, sqt[:, (k % 2) * T:(k % 2 + 1) * T], ALU.add)\
                        .then_inc(*OG.did(f"a{k}"))
                pool.wait_ge(*NV("stat", r))
                power(stat, powed, 4).then_inc(*NG.did("pow"))
                for k in range(KT):
                    pool.wait_ge(*(NV(f"y{k}", r) if r < 3 else FV(f"y{k}")))
                    pool.tensor_tensor(xt(k), xt(k), yt(k), ALU.add).then_inc(*NG.did(f"x{k}"))
                if r < 3:
                    pool.wait_ge(*NV("stat2", r))
                    power(stat, powed, 4).then_inc(*NG.did("pow2"))


def done_at(pair):
    for p0, c0, n, per in ((P_O1, C_O1, 8, 1), (P_Q1, C_Q1, 4, 4), (P_OUT1, C_OUT1, 8, 4), (P_C, C_C, 32, 4),
                           (P_O0, C_O0, 8, 1), (P_AB, C_AB, 52, 4)):
        if not isinstance(pair, int) or pair >= p0:
            return c0 + per * (pair - p0 + 1)


def shape_constants():
    c = np.zeros((P, CONST_W), np.float32)
    j, i = np.mgrid[0:P, 0:P]
    same = j // CH == i // CH
    put = lambda name, a: c.__setitem__((slice(None), slice(*CONST[name])), a)
    put("ident", j == i)
    put("cumsum", same & (j <= i))
    put("suffix", same & (j > i))
    put("half0", j < CH)
    put("half1", j >= CH)
    put("causal", np.where(same & (j <= i), 0.0, NEG))
    put("levels", np.concatenate([(j // (2 * s) == i // (2 * s)) & (j // s % 2 == 0) & (i // s % 2 == 1)
                                  for s in LEVELS], axis=1))
    put("ones", 1.0)
    inv_freq = (np.float32(10000.0) ** (-np.arange(0, QK, 2, dtype=np.float32) / np.float32(QK))).astype(np.float32)
    angle = (np.arange(T, dtype=np.float32)[None, :] * inv_freq[:, None]).astype(np.float32).astype(np.float64)
    put("cos", np.tile(np.cos(angle), (4, 1)))
    put("sin", np.concatenate([-np.sin(angle), np.sin(angle)] * 2, axis=0))
    return c


def kernel(x, mem, norm_pre, norm_post, xattn_norm_pre, xattn_norm_post, mem_norm, ab_w_in, a_conv, a_A_log,
           a_dt_bias, a_out_norm, b_lambda, b_out_norm, ab_w_out, c_w_in, c_conv, c_w_out, m_w_q, m_w_kv, m_w_o):
    import concourse.bacc as bacc
    from concourse.bass_utils import run_bass_kernel_spmd

    gains = lambda g: np.asarray(g).reshape(2 * KT, P).T
    taps = lambda w, n: np.asarray(w)[0].reshape(n, -1, P).transpose(2, 1, 0).reshape(P, -1)
    everywhere = lambda v: np.broadcast_to(np.asarray(v).reshape(1, -1), (P, np.asarray(v).size))
    parameters = np.concatenate([gains(norm_pre), gains(norm_post), gains(xattn_norm_pre), gains(xattn_norm_post),
                                 gains(mem_norm), taps(a_conv, 4), taps(c_conv, 3), np.asarray(a_out_norm).T,
                                 np.asarray(b_out_norm).T, everywhere(a_A_log), everywhere(a_dt_bias)], axis=1)
    arrays = {"x": np.asarray(x)[0], "mem": np.asarray(mem)[0], "constants": shape_constants(),
              "parameters": np.ascontiguousarray(parameters), "lambda": np.ascontiguousarray(everywhere(b_lambda)),
              "ab_w_in": np.asarray(ab_w_in)[0], "ab_w_out": np.asarray(ab_w_out)[0], "c_w_in": np.asarray(c_w_in)[0],
              "c_w_out": np.asarray(c_w_out)[0], "m_w_q": np.asarray(m_w_q), "m_w_kv": np.asarray(m_w_kv),
              "m_w_o": np.asarray(m_w_o)}
    books = {}
    for final in (False, True):
        nc = bacc.Bacc("TRN2", target_bir_lowering=False, num_devices=1)
        dram = {n: nc.dram_tensor("in_" + n, a.shape, F32, kind="ExternalInput").ap() for n, a in arrays.items()}
        dram["spill"] = nc.dram_tensor("spill", (KT, P, T), F32, kind="Internal").ap()
        dram["out"] = nc.dram_tensor("out", (T, D), F32, kind="ExternalOutput").ap()
        build(nc, books, dram)
    result = run_bass_kernel_spmd(nc, [{"in_" + n: np.ascontiguousarray(a) for n, a in arrays.items()}], core_ids=[0])
    return result.results[0]["out"].reshape(1, T, D)
```

```python
import concourse.bass as bass
import concourse.mybir as mybir
import math
from contextlib import ExitStack
import numpy as np

F32, F32R = mybir.dt.float32, mybir.dt.float32r
ALU, ACT, AX = mybir.AluOpType, mybir.ActivationFunctionType, mybir.AxisListType

P = 128
T, D, MEM = 512, 2048, 256
KT = D // P
TT = T // P
EPS = 1e-6
HEADS, HD = 8, 128
QK = 64
MH = 4
CH = 64
LAM_INIT = 0.8 - 0.6 * math.exp(0.0)
AB_B = 4 * 1024 + 2 * HEADS
RAW_SLOTS, SPLIT_SLOTS = 4, 2
CW = 4 * 256
NEG = -1e30
LEVELS = (1, 2, 4, 8, 16, 32)

AB_ITERS = 8
C_AB, P_AB = 0, 0
C_KV, P_KV = C_AB + 16 * AB_ITERS, P_AB + 4 * AB_ITERS
C_OUT0, P_OUT0 = C_KV + 32, P_KV + 8
C_Q0, P_Q0 = C_OUT0 + 32, P_OUT0 + 8
C_O0, P_O0 = C_Q0 + 16, P_Q0 + 4
C_C, P_C = C_O0 + 8, P_O0 + 8
C_OUT1, P_OUT1 = C_C + 128, P_C + 32
C_Q1, P_Q1 = C_OUT1 + 32, P_OUT1 + 8
C_O1, P_O1 = C_Q1 + 16, P_Q1 + 4
CHUNKS = C_O1 + 8

CONST = {}
_at = 0
for _name, _width in (("ident", P), ("cumsum", P), ("suffix", P), ("half0", P), ("half1", P), ("causal", P),
                      ("levels", len(LEVELS) * P), ("ones", 1), ("cos", T), ("sin", T)):
    CONST[_name] = (_at, _at + _width)
    _at += _width
CONST_W = _at
RESIDENT_W = CONST["cos"][0]

PARAM = {}
_at = 0
for _name, _width in (("norm_pre", 2 * KT), ("norm_post", 2 * KT), ("x_pre", 2 * KT), ("x_post", 2 * KT),
                      ("mem_norm", 2 * KT), ("a_conv", 24 * 4), ("c_conv", 16 * 3), ("a_norm", 1),
                      ("b_norm", 1), ("A_log", HEADS), ("dt_bias", HEADS)):
    PARAM[_name] = (_at, _at + _width)
    _at += _width
PARAM_W = _at


class Steps:

    def __init__(self, sem, book):
        self.sem, self.book, self.n, self.i = sem, book, 0, 0

    def round(self, i):
        self.n, self.i = 0, i

    def did(self, name=None):
        self.n += 1
        if name is not None:
            self.book[name] = self.n
        self.book["/"] = max(self.book.get("/", 0), self.n)
        return self.sem, 1

    def __call__(self, name, i=0):
        return self.sem, i * self.book.get("/", 0) + self.book.get(name, 1)

    def last(self):
        return self.sem, self.i * self.book.get("/", 0) + self.n


def spread(n_hops, first, last):
    return [first + (k * (last - first)) // max(n_hops - 1, 1) for k in range(n_hops)]



D_HOPS = (["ss", "rows", "tr", "dk", "qb", "p0"] + [f"{x}{s}" for s in range(1, 6) for x in ("p", "y")]
          + ["uw"] + [f"{x}{c}" for c in range(T // CH) for x in ("r", "s")] + ["fs", "fb"])
B_HOPS = ["vt"]
for _h in "01":
    B_HOPS += ["a" + _h + "0"] + [f"{x}{_h}{t + (x == 'a')}" for t in range(TT) for x in ("a", "b")]
    B_HOPS += ["fs" + _h, "fb" + _h]
C_HOPS = [f"{x}{h}" for h in range(MH) for x in "sto"]


def weighted(names, first, last, weights):
    at_, total = [0.0], sum(weights.get(n, weights.get(n[0], 1.0)) for n in names[:-1])
    for n in names[:-1]:
        at_.append(at_[-1] + weights.get(n, weights.get(n[0], 1.0)))
    return [first + int(a * (last - first) / total) for a in at_]


D_REPLY = {"ss": 4.5, "rows": 3.0, "tr": 6.0, "dk": 6.0, "qb": 3.5, "p0": 3.0, "p": 1.7, "y": 3.0, "uw": 3.0,
           "r": 1.5, "s": 1.9, "s7": 3.0, "fs": 4.5}
D_SLOTS, B_SLOTS, C_SLOTS = weighted(D_HOPS, 10, 63, D_REPLY), spread(len(B_HOPS), 16, 62), spread(len(C_HOPS), 34, 62)


AHEAD = (0, 8, 12, 15)


def split_ahead(split, k, c0):
    if k in AHEAD:
        split(c0 + AHEAD.index(k) + 1)


def hops_at(names, slots, lo, hi):
    return [n for n, s in zip(names, slots) if lo <= s < hi]


def build(nc, books, dram):
    ctx = ExitStack()
    with ctx:
        sb = lambda name, width, dt=F32: ctx.enter_context(nc.sbuf_tensor(name, [P, width], dt))
        sem = lambda name: ctx.enter_context(nc.semaphore(name))
        steps = lambda name: Steps(sem(name), books.setdefault(name, {}))

        X = sb("residual", KT * T)
        H_hi, H_lo = sb("input_hi", KT * T, F32R), sb("input_lo", KT * T, F32R)
        raw = sb("weights_raw", RAW_SLOTS * CW)
        w_hi, w_lo = sb("weights_hi", SPLIT_SLOTS * CW, F32R), sb("weights_lo", SPLIT_SLOTS * CW, F32R)
        const = sb("constants", RESIDENT_W)
        par = sb("parameters", PARAM_W)
        rs = sb("rstd_rows", T)
        small = sb("small", 512)
        gate_hi, gate_lo = sb("gate_hi", KT * 16, F32R), sb("gate_lo", KT * 16, F32R)
        work_w = 17000
        work = sb("work", work_w)

        acc = [ctx.enter_context(nc.psum_tensor(f"acc{n}", [P, T], F32)) for n in range(4)]
        m01 = ctx.enter_context(nc.psum_tensor("m01", [P, 2, T], F32))
        m23 = ctx.enter_context(nc.psum_tensor("m23", [P, 2, T], F32))
        start_banks = [acc[2][:, :], acc[3][:, :], m23[:, 0, :], m23[:, 1, :]]
        M = [m01[:, 0, :], m01[:, 1, :], m23[:, 0, :], m23[:, 1, :]]

        c_ = lambda name: const[:, CONST[name][0]:CONST[name][1]]
        p_ = lambda name: par[:, PARAM[name][0]:PARAM[name][1]]
        pcol = lambda name, k: par[:, bass.ds(PARAM[name][0] + k, 1)]
        ident, ones = c_("ident"), c_("ones")
        level_mask = lambda s: const[:, CONST["levels"][0] + s * P:CONST["levels"][0] + (s + 1) * P]

        at = [0]

        def cols(n):
            at[0] += n
            assert at[0] <= 512
            return small[:, at[0] - n:at[0]]
        stat, powed, minus_half = cols(16), cols(16), cols(16)
        beta, decay, g_col, k_in_scale, k_out_scale, v_scale = (cols(32) for _ in range(6))
        chunk_decay = cols(64)
        t1, t2, t3, t4, t5 = (cols(32) for _ in range(5))
        a_gain, b_gain, neg_lam, coef = (cols(1) for _ in range(4))
        mx, nmx, ssum, rsum, lam2 = (cols(4) for _ in range(5))

        def wk(n, start=None):
            start = wk.end if start is None else start
            wk.end = start + n
            assert wk.end <= work_w, wk.end
            return work[:, start:start + n]
        x_tok, sq_junk, norm_buf, gate_w = wk(TT * D, 0), wk(D), wk(2 * T), wk(KT * 16)
        lam_in = wk(4 * QK)
        qc, kc, vc, tanh_t = wk(2 * T, 0), wk(2 * T), wk(2 * T), wk(2 * T)
        side = wk.end
        k_in, k_out, v_in, q_dec, qk_t = (wk(2 * T) for _ in range(5))
        gam, n_t, c_t, inv, inv_t, prod = (wk(2 * T) for _ in range(6))
        v_new, state = wk(2 * HD), wk(2 * HD)
        w_t, u_tok = gam, n_t
        sq = work[:, side + 16 * T:side + 20 * T]
        qr, kr, rot, rope_tab, v_tok, prob = (wk(2 * T, side if n == 0 else None) for n in range(6))
        att, att_t, o_sb, o_sq = (wk(T) for _ in range(4))
        v_feat = wk(2 * MEM)
        kv_at = work_w - 4 * MH * MEM
        assert wk.end <= kv_at
        mk, mv = wk(2 * MH * MEM, kv_at), wk(2 * MH * MEM)
        mem_tok = work[:, kv_at:kv_at + 2 * D]
        mem_scaled = (rs, v_feat)
        Y, acc_sq, cq, cz = wk(KT * T, 0), wk(T), wk(MH * T), wk(MH * T)
        assert wk.end <= kv_at
        sqt = cq[:, 0:2 * T]
        cp, cpt = Y[:, 0:2 * T], Y[:, 2 * T:4 * T]
        zt = lambda h: Y[:, (4 + h) * T:(5 + h) * T]
        uu, cu, cv, bb = cq[:, 0:2 * T], cq[:, 2 * T:4 * T], cz[:, 0:2 * T], cz[:, 2 * T:4 * T]

        head2 = lambda t: t.rearrange("p (h n) -> p h n", h=2)
        tiles = lambda t: t.rearrange("p (t n) -> p t n", n=P)
        over_tiles = lambda t, n: t.unsqueeze(1).broadcast_to([P, n, P])
        over_row = lambda t, n, w: t.unsqueeze(2).broadcast_to([P, n, w])
        psum_tiles = lambda m: m[:, :, :].rearrange("p b (t n) -> p (b t) n", n=P)
        flat = lambda m: m[:, :, :].rearrange("p b n -> p (b n)")
        xt = lambda k: X[:, bass.ds(k * T, T)]
        yt = lambda k: Y[:, bass.ds(k * T, T)]
        mem_g = lambda H, l, g: H[:, (l * 8 + g) * T:(l * 8 + g + 1) * T]
        mem_h = lambda H, l, k: H[:, l * KT * MEM + k * MEM:l * KT * MEM + (k + 1) * MEM]
        mkt = lambda l, h: mk[:, (l * MH + h) * MEM:(l * MH + h + 1) * MEM]

        params_in, tables_in, gate_in, spilled, reloaded, out_done = (
            sem(n) for n in ("params_in", "tables_in", "gate_in", "spilled", "reloaded", "out_done"))
        x_in, mem_in = [sem(f"x_in{t}") for t in range(TT)], [sem(f"mem_in{m}") for m in range(2)]
        raw_in = [sem(f"raw_in{n}") for n in range(RAW_SLOTS)]
        hi_ready, lo_ready, chunk_used = sem("hi_ready"), sem("lo_ready"), sem("chunk_used")
        acc_free, z_tanh = sem("acc_free"), sem("z_tanh")
        const_set = sem("const_set")
        SM, SA, SV, SG = steps("start_mm"), steps("start_act"), steps("start_vec"), steps("start_pool")
        EA, EV = steps("evac_act"), steps("evac_vec")
        GM, GA, GV, GG = steps("delta_mm"), steps("delta_act"), steps("delta_vec"), steps("delta_pool")
        BM, BA, BV, BG = steps("attn_mm"), steps("attn_act"), steps("attn_vec"), steps("attn_pool")
        MM, MA, MV, MG = steps("mem_mm"), steps("mem_act"), steps("mem_vec"), steps("mem_pool")
        OA, OG = steps("outproj_act"), steps("outproj_pool")
        ZA, ZV = steps("split_act"), steps("split_vec")
        NM, NA, NV, NG = steps("norm_mm"), steps("norm_act"), steps("norm_vec"), steps("norm_pool")
        CM, CA, CV = steps("cross_mm"), steps("cross_act"), steps("cross_vec")
        VA, VV = steps("conv_act"), steps("conv_vec")
        FM, FV = steps("final_mm"), steps("final_vec")

        block = ctx.enter_context(nc.Block())
        LAYERS_Q, LAYERS_O, P_Q, P_O = (C_Q0, C_Q1), (C_O0, C_O1), (P_Q0, P_Q1), (P_O0, P_O1)

        @block.sync
        def _(sp):
            sp.dma_start(const[:, :], dram["constants"][:, 0:RESIDENT_W]).then_inc(params_in, 16)
            sp.dma_start(par[:, :], dram["parameters"]).then_inc(params_in, 16)
            for t in range(TT):
                sp.dma_start(x_tok[:, t * D:(t + 1) * D], dram["x"][t * P:(t + 1) * P, :]).then_inc(x_in[t], 16)
            sp.dma_start(gate_w.rearrange("p (k n) -> p k n", n=16),
                         dram["ab_w_in"].rearrange("(k p) n -> p k n", p=P)[:, :, 4096:4096 + 16]).then_inc(gate_in, 16)
            sp.dma_start(lam_in, dram["lambda"]).then_inc(gate_in, 16)

            def load(w, col, g, kt0):
                if g >= RAW_SLOTS:
                    sp.wait_ge(lo_ready, g - RAW_SLOTS + 1)
                c = g % RAW_SLOTS
                src = w.rearrange("(k p) n -> p k n", p=P)[:, kt0:kt0 + 4, bass.ds(col, 256)]
                sp.dma_start(raw[:, c * CW:(c + 1) * CW].rearrange("p (k n) -> p k n", k=4), src)\
                    .then_inc(raw_in[c], 16)

            def load_pair(w, col, g):
                for c in range(4):
                    load(w, col, g + c, 4 * c)

            for it in range(AB_ITERS):
                i = it % 4
                for j, sec in enumerate((3072, 0, 1024, 2048)):
                    if it == 5 and j == 3:
                        sp.wait_ge(*GA("end", 3))
                        for m in range(2):
                            sp.dma_start(mem_tok[:, m * D:(m + 1) * D], dram["mem"][m * P:(m + 1) * P, :])\
                                .then_inc(mem_in[m], 16)
                    load_pair(dram["ab_w_in"], (AB_B if it >= 4 else 0) + sec + 256 * i, C_AB + 16 * it + 4 * j)
                    if it == 0 and j == 0:
                        for k in range(KT):
                            sp.wait_ge(*SA(f"copy{k}"))
                            sp.dma_start(dram["spill"][k], xt(k)).then_inc(spilled, 16)
            for l in range(2):
                for j in range(4):
                    load_pair(dram["m_w_kv"][l], 256 * j, C_KV + 16 * l + 4 * j)
            for n in range(8):
                load_pair(dram["ab_w_out"], 256 * n, C_OUT0 + 4 * n)
                if n == 0:
                    for k in range(KT):
                        sp.wait_ge(*ZV(f"lo{k}"))
                        sp.dma_start(xt(k), dram["spill"][k]).then_inc(reloaded, 16)

            def cross_loads(l):
                for j in range(4):
                    load_pair(dram["m_w_q"][l], 256 * j, LAYERS_Q[l] + 4 * j)
                for n in range(8):
                    load(dram["m_w_o"][l], 256 * n, LAYERS_O[l] + n, 0)
            cross_loads(0)
            for n in range(8):
                for j, sec in enumerate((0, 2, 1, 3)):
                    load_pair(dram["c_w_in"], sec * D + 256 * n, C_C + 16 * n + 4 * j)
            for n in range(8):
                load_pair(dram["c_w_out"], 256 * n, C_OUT1 + 4 * n)
            cross_loads(1)
            for n in range(16):
                kg, t = n // TT, n % TT
                sp.wait_ge(*FV(f"o{n}"))
                sp.dma_start(dram["out"][t * P:(t + 1) * P, kg * T:(kg + 1) * T], yt(n)).then_inc(out_done, 16)
            sp.wait_ge(out_done, 16 * 16)
            sp.wait_ge(spilled, 16 * KT)

        @block.scalar
        def _(act):
            is_split = set()

            def split(g):
                if g >= CHUNKS or g in is_split:
                    return
                is_split.add(g)
                c, s = g % RAW_SLOTS, g % SPLIT_SLOTS
                act.wait_ge(raw_in[c], 16 * (g // RAW_SLOTS + 1))
                if g >= SPLIT_SLOTS:
                    act.wait_ge(chunk_used, g - SPLIT_SLOTS + 1)
                act.activation(w_hi[:, s * CW:(s + 1) * CW], raw[:, c * CW:(c + 1) * CW], ACT.Copy)\
                    .then_inc(hi_ready, 1)

            act.wait_ge(params_in, 32)
            for t in range(TT):
                act.wait_ge(x_in[t], 16)
                if t:
                    act.wait_ge(*SA.last())
                act.activation(sq_junk, x_tok[:, t * D:(t + 1) * D], ACT.Square,
                               accum_out=stat[:, t:t + 1]).then_inc(*SA.did(f"ss{t}"))
            split(0)
            act.wait_ge(gate_in, 32)
            act.activation(gate_hi[:, :], gate_w, ACT.Copy).then_inc(*SA.did("gate_hi"))

            def start_high(k):
                act.wait_ge(*SV(f"norm{k}"))
                act.activation(H_hi[:, k * T:(k + 1) * T], norm_buf[:, (k % 2) * T:(k % 2 + 1) * T], ACT.Copy)\
                    .then_inc(*SA.did(f"hi{k}"))
                split_ahead(split, k, C_AB)
            for k in range(KT):
                act.wait_ge(*SM(f"tr{k}"))
                act.activation(xt(k), start_banks[k % 4], ACT.Copy).then_inc(*SA.did(f"copy{k}"))
                if k:
                    start_high(k - 1)
            start_high(KT - 1)

            def gates():
                act.wait_ge(*SV("gates"))
                act.activation(t1, t1, ACT.Exp, scale=-1.0).then_inc(*SA.did("eb"))
                act.activation(t3, t2, ACT.Abs).then_inc(*SA.did())
                act.wait_ge(*SA.last())
                act.activation(t3, t3, ACT.Exp, scale=-1.0).then_inc(*SA.did("eg"))
                act.activation(p_("A_log"), p_("A_log"), ACT.Exp).then_inc(*SA.did())
                act.activation(lam2[:, 0:2], lam2[:, 0:2], ACT.Exp).then_inc(*SA.did("small_exp"))

            def decays():
                act.wait_ge(*SM("decays"))
                act.wait_ge(*SV("decay"))
                act.activation(k_in_scale, M[0][:, 0:32], ACT.Exp).then_inc(*SA.did())
                act.activation(k_out_scale, M[0][:, 32:64], ACT.Exp).then_inc(*SA.did())
                act.activation(chunk_decay, M[0][:, 64:128], ACT.Exp).then_inc(*SA.did("decays"))

            def delta(name, i):
                if name == "begin":
                    GA.round(i)
                    act.wait_ge(*EV("s11", i))
                    act.activation(sq[:, 0:2 * T], qc, ACT.Square).then_inc(*GA.did())
                    act.activation(sq[:, 2 * T:4 * T], kc, ACT.Square).then_inc(*GA.did("sq"))
                elif name == "tr":
                    act.wait_ge(*GM("tr", i))
                    for h in range(2):
                        for t in range(TT):
                            c = bass.ds((2 * i + h) * TT + t, 1)
                            o = slice(h * T + t * P, h * T + (t + 1) * P)
                            act.activation(k_in[:, o], M[h][:, t * P:(t + 1) * P], ACT.Copy, scale=k_in_scale[:, c])\
                                .then_inc(*GA.did())
                            act.activation(v_in[:, o], M[2 + h][:, t * P:(t + 1) * P], ACT.Copy, scale=v_scale[:, c])\
                                .then_inc(*GA.did("kv"))
                elif name == "dk":
                    act.wait_ge(*GV("gam", i))
                    act.activation(prod, flat(m01), ACT.Exp).then_inc(*GA.did("edec"))
                    act.activation(gam, gam, ACT.Exp).then_inc(*GA.did("gam"))
                elif name[0] == "p" and name != "p0":
                    act.wait_ge(*GM(name, i))
                    act.activation(prod, flat(m01), ACT.Copy).then_inc(*GA.did(name))
                elif name == "uw":
                    act.wait_ge(*GM("uw", i))
                    act.activation(u_tok, flat(m01), ACT.Copy).then_inc(*GA.did("u"))
                    act.activation(w_t, flat(m23), ACT.Copy).then_inc(*GA.did("w"))
                elif name == "s7":
                    act.wait_ge(*GM("s7", i))
                    act.activation(prod, flat(m23), ACT.Copy).then_inc(*GA.did())
                    act.activation(inv, flat(m23), ACT.Square).then_inc(*GA.did("o"))
                elif name == "end":
                    act.wait_ge(*GV("end", i))
                    act.activation(coef, minus_half[:, 0:1], ACT.Copy).then_inc(*GA.did("end"))

            def attn(name, i):
                if name in ("begin", "begin_k"):
                    src, tag = (kc, "rk") if name == "begin_k" else (qc, "rq")
                    if tag == "rk":
                        act.wait_ge(*BV("rq", i))
                    else:
                        BA.round(i)
                        act.wait_ge(acc_free, 2 * (P_AB + 4 * (4 + i) + 3))
                    for a in range(4):
                        b = a ^ 1
                        act.activation(rot[32 * a:32 * a + 32, :], src[32 * b:32 * b + 32, :], ACT.Copy)\
                            .then_inc(*BA.did(tag))
                elif name == "vt":
                    act.wait_ge(*BM("vt", i))
                    act.activation(v_tok, flat(m01), ACT.Copy).then_inc(*BA.did("v"))
                elif name[0] == "a":
                    h, t = int(name[1]), int(name[2])
                    act.wait_ge(*BM(name, i))
                    if t:
                        act.activation(att_t[:, 0:t * P], M[2][:, 0:t * P], ACT.Copy)\
                            .then_inc(*BA.did(f"at{h}{t - 1}"))
                    if t < TT:
                        n = (t + 1) * P
                        act.wait_ge(*BV(f"nm{h}{t}", i))
                        for m in range(2):
                            act.activation(prob[:, m * T:m * T + n], M[m][:, 0:n], ACT.Exp, bias=nmx[:, m:m + 1],
                                           scale=QK ** -0.5, accum_out=ssum[:, m:m + 1])\
                                .then_inc(*BA.did(f"p{h}{t}"))
                elif name in ("b03", "b13"):
                    act.wait_ge(*BM(name, i))
                    act.activation(o_sb, M[3], ACT.Copy).then_inc(*BA.did())
                    act.activation(o_sq, M[3], ACT.Square).then_inc(*BA.did(f"o{name[1]}"))

            def tanh_z(it):
                pair = P_AB + 4 * it
                act.wait_ge(chunk_used, done_at(pair))
                if it:
                    act.wait_ge(acc_free, 2 * pair)
                    if it <= 4:
                        act.wait_ge(*EV("s21", it - 1))
                for n in range(2):
                    act.activation(tanh_t[:, n * T:(n + 1) * T], acc[2 * (pair % 2) + n][:, :], ACT.Tanh, scale=0.5)\
                        .then_inc(z_tanh, 1)

            def tanh_conv(it, sec, n):
                act.wait_ge(acc_free, 2 * (P_AB + 4 * it + 1 + sec) + n + 1)
                act.activation(tanh_t[:, n * T:(n + 1) * T], (qc, kc, vc)[sec][:, n * T:(n + 1) * T], ACT.Tanh,
                               scale=0.5).then_inc(*EA.did(f"t{sec}{n}"))

            def mem_squares(m):
                act.wait_ge(mem_in[m], 16)
                for h in range(2):
                    if h or m:
                        act.wait_ge(*MA.last())
                    act.activation(tanh_t, mem_tok[:, m * D + h * 2 * T:m * D + (h + 1) * 2 * T], ACT.Square,
                                   accum_out=t1[:, 2 * h + m:2 * h + m + 1]).then_inc(*MA.did("ss"))

            def mem_rows(m):
                act.wait_ge(*MG("pow"))
                o = slice(m * D, (m + 1) * D)
                act.activation(mem_tok[:, o], mem_tok[:, o], ACT.Copy, scale=t2[:, m:m + 1]).then_inc(*MA.did(f"n{m}"))

            def mem_high(l, g):
                if g == 0:
                    act.wait_ge(chunk_used, C_KV - 2 if l == 0 else C_KV)
                act.wait_ge(*MV(f"m{l}{g}"))
                act.activation(mem_g(H_hi, l, g), mem_scaled[g % 2][:, :], ACT.Copy).then_inc(*MA.did(f"hi{l}{g}"))

            for it in range(AB_ITERS):
                reply, i = (delta, it - 1) if it <= 4 else (attn, it - 5)
                for c in range(16):
                    split(C_AB + 16 * it + c + 1)
                    if it == 6 and c in (8, 9):
                        if c == 8:
                            act.wait_ge(acc_free, 2 * (P_AB + 4 * it + 1))
                        mem_squares(c - 8)
                    if it == 7 and c in (8, 9):
                        mem_rows(c - 8)
                    if 1 <= it <= 4 and c < 2:
                        tanh_conv(it - 1, 2, c)
                    if c == 2:
                        EA.round(it)
                    if it == 0 and c == 5:
                        gates()
                    if c == 4:
                        tanh_z(it)
                    if it == 0 and c == 7:
                        decays()
                    if it < 4 and c in (8, 9):
                        tanh_conv(it, 0, c - 8)
                    if it < 4 and c in (12, 13):
                        tanh_conv(it, 1, c - 12)
                    if it:
                        if c == 2:
                            reply("begin", i)
                        if c == 3 and it > 4:
                            reply("begin_k", i)
                        names, slots = (D_HOPS, D_SLOTS) if it <= 4 else (B_HOPS, B_SLOTS)
                        for k in range(4):
                            for name in hops_at(names, slots, 4 * c + k, 4 * c + k + 1):
                                reply(name, i)
                            if it == 7 and c >= 14:
                                mem_high(0, 4 * (c - 14) + k)
                        if c == 15 and it <= 4:
                            reply("end", i)
                        if c == 15 and it == 4:
                            act.wait_ge(*GA.last())
                            act.dma_start(rope_tab, dram["constants"][:, RESIDENT_W:]).then_inc(tables_in, 16)

            for c in range(32):
                split(C_KV + c + 1)
                for k in range(4):
                    if 1 <= c <= 2:
                        mem_high(1, 4 * (c - 1) + k)
                if c in (0, 3):
                    attn("begin_k" if c else "begin", 3)
                for name in hops_at(B_HOPS, B_SLOTS, 2 * c, 2 * c + 2):
                    attn(name, 3)

            def split_input(r, src, c0):
                ZA.round(r)
                act.wait_ge(chunk_used, c0)
                for k in range(KT):
                    if k == 0:
                        act.wait_ge(*((BV("y1", 3)) if r == 0 else VV("y1", 7)))
                    act.activation(H_hi[:, k * T:(k + 1) * T], src(k), ACT.Copy).then_inc(*ZA.did(f"hi{k}"))
                    split_ahead(split, k, c0)

            def out_square(r, n, pair):
                for j in range(2):
                    act.wait_ge(acc_free, 2 * pair + j + 1)
                    if n:
                        act.wait_ge(*OG(f"a{2 * n + j - 2}", r))
                    act.activation(sqt[:, j * T:(j + 1) * T], yt(2 * n + j), ACT.Square)\
                        .then_inc(*OA.did(f"s{2 * n + j}"))

            def out_phase(r, c0, p0, per):
                OA.round(r)
                for n in range(8):
                    for c in range(per):
                        split(c0 + per * n + c + 1)
                        if c == 0 and n:
                            out_square(r, n - 1, p0 + n - 1)
                out_square(r, 7, p0 + 7)

            def norm(r):
                NA.round(r)
                split((C_Q0, C_C, C_Q1)[r] + 1)
                gain = ("x_pre", "norm_pre", "x_pre")[r]
                layer = (0, 1, 1)[r]
                for k in range(KT):
                    act.wait_ge(*NG(f"x{k}", r))
                    act.activation(H_hi[:, k * T:(k + 1) * T], xt(k), ACT.Copy, scale=pcol(gain, layer * KT + k))\
                        .then_inc(*NA.did(f"hi{k}"))
                    act.activation(yt(k), xt(k), ACT.Square).then_inc(*NA.did(f"sq{k}"))
                    split_ahead(split, k, (C_Q0, C_C, C_Q1)[r])

            def cross(l):
                CA.round(l)

                def gate(n):
                    for h in (2 * n, 2 * n + 1):
                        act.wait_ge(acc_free, 2 * (P_Q[l] + 2 + n) + h % 2 + 1)
                        act.activation(zt(h), cz[:, h * T:(h + 1) * T], ACT.Tanh, scale=0.5).then_inc(*CA.did(f"zt{h}"))

                def outputs(n):
                    act.wait_ge(chunk_used, LAYERS_Q[l] + 13)
                    for h in (2 * n, 2 * n + 1):
                        act.wait_ge(*CV(f"y{h}", l))
                        act.activation(H_hi[:, h * T:(h + 1) * T], cq[:, h * T:(h + 1) * T], ACT.Copy)\
                            .then_inc(*CA.did(f"hi{h}"))
                for c in range(16):
                    split(LAYERS_Q[l] + c + 1)
                    for name in hops_at(C_HOPS, C_SLOTS, 4 * c, 4 * c + 4):
                        h = int(name[1])
                        if name[0] == "s":
                            act.wait_ge(*CV(f"nm{h}", l))
                            for t in range(TT):
                                act.activation(cp[:, t * MEM:(t + 1) * MEM], flat(m01)[:, t * MEM:(t + 1) * MEM],
                                               ACT.Exp, bias=nmx[:, t:t + 1], scale=P ** -0.5,
                                               accum_out=ssum[:, t:t + 1]).then_inc(*CA.did(f"p{h}"))
                        elif name[0] == "t":
                            act.wait_ge(*CM(name, l))
                            act.activation(cpt, flat(m23), ACT.Copy).then_inc(*CA.did(f"t{h}"))
                        else:
                            act.wait_ge(*CM(name, l))
                            act.activation(cq[:, h * T:(h + 1) * T], M[0], ACT.Copy, scale=0.5)\
                                .then_inc(*CA.did(f"o{h}"))
                    if c == 13:
                        gate(0)
                    if c == 15:
                        outputs(0)
                gate(1)
                outputs(1)

            split_input(0, xt, C_OUT0)
            out_phase(0, C_OUT0, P_OUT0, 4)
            norm(0)
            cross(0)
            out_phase(1, C_O0, P_O0, 1)
            norm(1)

            def conv_tanh(n):
                pair = P_C + 4 * n + 3
                for j in range(2):
                    act.wait_ge(acc_free, 2 * pair + j + 1)
                    act.activation(uu[:, j * T:(j + 1) * T], bb[:, j * T:(j + 1) * T], ACT.Tanh, scale=0.5)\
                        .then_inc(*VA.did(f"z{j}"))
            for n in range(8):
                for c in range(16):
                    split(C_C + 16 * n + c + 1)
                    if n and c == 0:
                        conv_tanh(n - 1)
                    if c == 1:
                        VA.round(n)
            conv_tanh(7)
            split_input(1, yt, C_OUT1)
            out_phase(2, C_OUT1, P_OUT1, 4)
            norm(2)
            cross(1)
            out_phase(3, C_O1, P_O1, 1)

        @block.tensor
        def _(pe):
            def rows(out, col, n, at_=None):
                for t in range(n):
                    last = pe.matmul(out(t), col(t).broadcast_to([P, P]), ident, start=True, stop=True)
                return last

            def chunk(g, pair, kt0, last_kt, width=T, hi=None, lo=None, ready=None, between=None):
                s = g % SPLIT_SLOTS
                hi = hi or (lambda k: H_hi[:, k * T:(k + 1) * T])
                lo = lo or (lambda k: H_lo[:, k * T:(k + 1) * T])
                pe.wait_ge(lo_ready, g + 1)
                if kt0 == 0 and pair >= 2:
                    pe.wait_ge(acc_free, 2 * (pair - 1))
                for k in range(4):
                    kt = kt0 + k
                    if ready is not None:
                        pe.wait_ge(*ready(kt))
                    for j in range(2):
                        o = s * CW + k * 256 + j * P
                        out = acc[2 * (pair % 2) + j][:, 0:width]
                        pe.matmul(out, w_hi[:, o:o + P], hi(kt), start=kt == 0, stop=False)
                        pe.matmul(out, w_hi[:, o:o + P], lo(kt), start=False, stop=False)
                        last = pe.matmul(out, w_lo[:, o:o + P], hi(kt), start=False, stop=kt == last_kt)
                    if k == 3:
                        last.then_inc(chunk_used, 1)
                    if between is not None:
                        between(k)

            pe.wait_ge(params_in, 32)
            for t in range(TT):
                pe.wait_ge(x_in[t], 16)

            def start_transposes(k):
                if k >= 4:
                    pe.wait_ge(*SA(f"hi{k - 4}"))
                if k == 2:
                    pe.wait_ge(*SG("pow"))
                    rows(lambda t: M[1][:, t * P:(t + 1) * P], lambda t: powed[:, t:t + 1], TT)\
                        .then_inc(*SM.did("rows"))
                for t in range(TT):
                    last = pe.transpose(start_banks[k % 4][:, t * P:(t + 1) * P], x_tok[:, t * D + k * P:t * D + (k + 1) * P],
                                        ident)
                last.then_inc(*SM.did(f"tr{k}"))
            START_AHEAD = 4
            for k in range(START_AHEAD):
                start_transposes(k)

            def gates(step):
                if step == 0:
                    pe.wait_ge(*SV("gate_lo"))
                    pe.wait_ge(*SV("rs"))
                    for k in range(KT):
                        x, g = slice(k * T, (k + 1) * T), slice(k * 16, (k + 1) * 16)
                        pe.matmul(M[1][0:16, :], gate_hi[:, g], H_hi[:, x], start=k == 0, stop=False)
                        pe.matmul(M[1][0:16, :], gate_hi[:, g], H_lo[:, x], start=False, stop=False)
                        last = pe.matmul(M[1][0:16, :], gate_lo[:, g], H_hi[:, x], start=False, stop=k == KT - 1)
                    last.then_inc(*SM.did("gate_cols"))
                else:
                    pe.wait_ge(*SV("gate_cols"))
                    for t in range(TT):
                        last = pe.transpose(M[0][:, t * 16:(t + 1) * 16], norm_buf[0:16, t * P:(t + 1) * P],
                                            ident[0:16, 0:16])
                    last.then_inc(*SM.did("gates"))

            def decays():
                pe.wait_ge(*SV("g"))
                for n, name in enumerate(("cumsum", "suffix", "half0", "half1")):
                    last = pe.matmul(M[0][:, 32 * n:32 * n + 32], c_(name), g_col, start=True, stop=True)
                last.then_inc(*SM.did("decays"))

            def delta(name, i):
                hc = lambda h, t: bass.ds((2 * i + h) * TT + t, 1)
                ht = [(h, t) for h in range(2) for t in range(TT)]
                o = lambda h, t: slice(h * T + t * P, h * T + (t + 1) * P)
                m = lambda bank, h, t: bank[:, h, t * P:(t + 1) * P]
                if name == "ss":
                    GM.round(i)
                    pe.wait_ge(*GA("sq", i))
                    if i == 0:
                        pe.wait_ge(*SA("decays"))
                    for n in range(16):
                        last = pe.matmul(M[0][:, n:n + 1], sq[:, n * P:(n + 1) * P], ones, start=True, stop=True)
                elif name == "rows":
                    pe.wait_ge(*GV("pw", i))
                    for h, t in ht:
                        n = h * TT + t
                        pe.matmul(m(m01, h, t), powed[:, 8 + n:9 + n].broadcast_to([P, P]), ident, start=True, stop=True)
                        last = pe.matmul(m(m23, h, t), powed[:, n:n + 1].broadcast_to([P, P]), ident, start=True, stop=True)
                elif name == "tr":
                    pe.wait_ge(*GV("qn", i))
                    pe.wait_ge(*EV("s21", i))
                    for h, t in ht:
                        pe.transpose(m(m01, h, t), kc[:, o(h, t)], ident)
                        last = pe.transpose(m(m23, h, t), vc[:, o(h, t)], ident)
                elif name == "dk":
                    pe.wait_ge(*GA("kv", i))
                    pe.wait_ge(*GV("k_out", i))
                    for h, t in ht:
                        pe.matmul(m(m01, h, t), g_col[:, hc(h, t)].broadcast_to([P, P]), c_("cumsum"),
                                  start=True, stop=True)
                        last = pe.matmul(m(m23, h, t), kc[:, o(h, t)], kc[:, o(h, t)], start=True, stop=True)
                elif name == "qb":
                    pe.wait_ge(*GV("nt0", i))
                    for h, t in ht:
                        pe.matmul(m(m01, h, t), kc[:, o(h, t)], qc[:, o(h, t)], start=True, stop=True)
                        last = pe.matmul(m(m23, h, t), beta[:, hc(h, t)].broadcast_to([P, P]), ident,
                                         start=True, stop=True)
                elif name == "p0":
                    pe.wait_ge(*GG("c0", i))
                    pe.wait_ge(*GV("qk", i))
                    for h, t in ht:
                        last = pe.matmul(m(m01, h, t), c_t[:, o(h, t)], ident, start=True, stop=True)
                elif name[0] == "p":
                    pe.wait_ge(*GG("c" + name[1], i))
                    pe.wait_ge(*GV("y" + str(int(name[1]) - 1), i))
                    for h, t in ht:
                        last = pe.matmul(m(m01, h, t), c_t[:, o(h, t)], inv[:, o(h, t)], start=True, stop=True)
                elif name[0] == "y":
                    pe.wait_ge(*GA("p" + name[1], i))
                    for h, t in ht:
                        if name != "y5":
                            pe.matmul(m(m23, h, t), inv_t[:, o(h, t)], prod[:, o(h, t)], start=True, stop=True)
                        last = pe.matmul(m(m01, h, t), prod[:, o(h, t)], inv_t[:, o(h, t)], start=True, stop=True)
                elif name == "uw":
                    pe.wait_ge(*GV("y5", i))
                    for h, t in ht:
                        pe.matmul(m(m01, h, t), inv_t[:, o(h, t)], v_in[:, o(h, t)], start=True, stop=True)
                        last = pe.matmul(m(m23, h, t), k_in[:, o(h, t)], inv_t[:, o(h, t)], start=True, stop=True)
                elif name[0] == "r":
                    c = int(name[1])
                    p0 = CH * (c % 2)
                    if c == 0:
                        pe.wait_ge(*GA("w", i))
                    pe.wait_ge(*GV(f"st{c}", i))
                    for h in range(2):
                        st = state[:, h * HD:(h + 1) * HD]
                        pe.matmul(M[0][p0:p0 + CH, h * HD:(h + 1) * HD], w_t[:, h * T + c * CH:h * T + (c + 1) * CH],
                                  st, start=True, stop=True)
                        last = pe.matmul(m23[:, h, c * CH:(c + 1) * CH], st,
                                         q_dec[:, h * T + c * CH:h * T + (c + 1) * CH], start=True, stop=False)
                elif name[0] == "s":
                    c = int(name[1])
                    t, p0 = c // 2, CH * (c % 2)
                    ps = slice(p0, p0 + CH)
                    pe.wait_ge(*GV(f"vn{c}", i))
                    for h in range(2):
                        vn = v_new[ps, h * HD:(h + 1) * HD]
                        q0 = h * T + t * P + p0
                        last = pe.matmul(m23[:, h, c * CH:(c + 1) * CH], vn, qk_t[ps, q0:q0 + CH],
                                         start=False, stop=True)
                        if c < T // CH - 1:
                            last = pe.matmul(M[1][:, h * HD:(h + 1) * HD], k_out[ps, o(h, t)], vn, start=True, stop=True)
                elif name == "fs":
                    pe.wait_ge(*GA("o", i))
                    for n in range(8):
                        last = pe.matmul(M[0][:, n:n + 1], inv[:, n * P:(n + 1) * P], ones, start=True, stop=True)
                elif name == "fb":
                    pe.wait_ge(*GG("fpow", i))
                    for h, t in ht:
                        n = h * TT + t
                        last = pe.matmul(m(m01, h, t), powed[:, n:n + 1].broadcast_to([P, P]), ident, start=True, stop=True)
                last.then_inc(*GM.did(name))

            def attn(name, i):
                if name == "vt":
                    BM.round(i)
                    if i == 0:
                        pe.wait_ge(*GA("end", 3))
                    else:
                        pe.wait_ge(*BV("y1", i - 1))
                    pe.wait_ge(acc_free, 2 * (P_AB + 4 * (4 + i) + 4))
                    for n in range(8):
                        last = pe.transpose(m01[:, n // TT, (n % TT) * P:(n % TT + 1) * P], vc[:, n * P:(n + 1) * P], ident)
                elif name[0] == "a":
                    h, t = int(name[1]), int(name[2])
                    if t:
                        pe.wait_ge(*BV(f"att{h}{t - 1}", i))
                        for j in range(t):
                            last = pe.transpose(M[2][:, j * P:(j + 1) * P], att[:, j * P:(j + 1) * P], ident)
                    elif h == 0:
                        pe.wait_ge(*BA("v", i))
                        pe.wait_ge(*BV("rk", i))
                    else:
                        pe.wait_ge(*BV("y0", i))
                    if t < TT:
                        if t:
                            pe.wait_ge(*BA(f"p{h}{t - 1}", i))
                        for mp in range(2):
                            r = slice(QK * mp, QK * mp + QK)
                            last = pe.matmul(M[mp][:, 0:(t + 1) * P], qr[r, h * T + t * P:h * T + (t + 1) * P],
                                             kr[r, h * T:h * T + (t + 1) * P], start=True, stop=True)
                elif name[0] == "b":
                    h, t = int(name[1]), int(name[2])
                    pe.wait_ge(*BA(f"at{h}{t}", i))
                    if h and t == 0:
                        pe.wait_ge(*BA("o0", i))
                    for j in range(t + 1):
                        last = pe.matmul(M[3][:, t * P:(t + 1) * P], v_tok[:, h * T + j * P:h * T + (j + 1) * P],
                                         att_t[:, j * P:(j + 1) * P], start=j == 0, stop=j == t)
                elif name[:2] == "fs":
                    pe.wait_ge(*BA("o" + name[2], i))
                    for t in range(TT):
                        last = pe.matmul(M[0][:, t:t + 1], o_sq[:, t * P:(t + 1) * P], ones, start=True, stop=True)
                else:
                    pe.wait_ge(*BG("pow" + name[2], i))
                    last = rows(lambda t: M[0][:, t * P:(t + 1) * P], lambda t: powed[:, t:t + 1], TT)
                last.then_inc(*BM.did(name))

            def mem_transposes(l, g):
                if g == 0:
                    pe.wait_ge(*MA("n1"))
                    pe.wait_ge(acc_free, 2 * (P_KV - 1 + l))
                if g >= 2:
                    pe.wait_ge(*MV(f"m{l}{g - 2}"))
                for n in range(4):
                    k, m = 2 * g + n // 2, n % 2
                    last = pe.transpose(acc[2 * l + g % 2][:, n * P:(n + 1) * P],
                                        mem_tok[:, m * D + k * P:m * D + (k + 1) * P], ident)
                last.then_inc(*MM.did(f"t{l}{g}"))

            for it in range(AB_ITERS):
                hop, i = (delta, it - 1) if it <= 4 else (attn, it - 5)
                names, slots = (D_HOPS, D_SLOTS) if it <= 4 else (B_HOPS, B_SLOTS)
                for c in range(16):
                    def between(k):
                        if it == 0 and 4 * c + k + START_AHEAD < KT:
                            start_transposes(4 * c + k + START_AHEAD)
                        if it:
                            for name in hops_at(names, slots, 4 * c + k, 4 * c + k + 1):
                                hop(name, i)
                        if it == 7 and c >= 14:
                            mem_transposes(0, 4 * (c - 14) + k)
                    if it == 0 and c == 4:
                        pe.wait_ge(*SA("hi15"))
                    if it == 0 and c in (4, 5):
                        gates(c - 4)
                    if it == 0 and c == 7:
                        decays()
                    chunk(C_AB + 16 * it + c, P_AB + 4 * it + c // 4, 4 * (c % 4), KT - 1, between=between,
                          ready=(lambda kt: SV(f"lo{kt}")) if it == 0 and c < 4 else None)

            def value_transposes(l, j, pair):
                pe.wait_ge(*MV(f"vf{l}{j}"))
                for n in range(4):
                    last = pe.transpose(acc[2 * (pair % 2)][:, n * P:(n + 1) * P], v_feat[:, n * P:(n + 1) * P], ident)
                last.then_inc(*MM.did(f"v{l}{j}"))

            for c in range(32):
                l, q = c // 16, c // 4 - 1

                def between(k):
                    if 1 <= c <= 2:
                        mem_transposes(1, 4 * (c - 1) + k)
                    if k % 2:
                        for name in hops_at(B_HOPS, B_SLOTS, 2 * c + k // 2, 2 * c + k // 2 + 1):
                            attn(name, 3)
                if q >= 0 and c % 4 == 1 and q % 4 >= 2:
                    value_transposes(q // 4, q % 4, P_KV + q)
                if c % 16 == 0 or c == 4:
                    pe.wait_ge(*MV(f"m{int(c > 0)}7"))
                chunk(C_KV + c, P_KV + c // 4, 4 * (c % 4), KT - 1, width=MEM, between=between,
                      ready=(lambda kt: MV(f"lo{l}{kt // 2}")) if c % 16 < 4 else None,
                      hi=lambda k: mem_h(H_hi, l, k), lo=lambda k: mem_h(H_lo, l, k))
            value_transposes(1, 3, P_KV + 7)

            def out_phase(c0, p0, per, ready):
                for n in range(8):
                    for c in range(per):
                        chunk(c0 + per * n + c, p0 + n, 4 * c, 4 * per - 1, ready=ready if n == 0 else None)

            def norm(r):
                NM.round(r)
                pe.wait_ge(*OG("a13", r))
                pe.wait_ge(*OA("s15", r))
                for t in range(TT):
                    for n, part in enumerate((acc_sq, sqt[:, 0:T], sqt[:, T:2 * T])):
                        last = pe.matmul(M[0][:, t:t + 1], part[:, t * P:(t + 1) * P], ones, start=n == 0, stop=n == 2)
                last.then_inc(*NM.did("ss"))
                pe.wait_ge(*NG("pow", r))
                rows(lambda t: M[1][:, t * P:(t + 1) * P], lambda t: powed[:, t:t + 1], TT).then_inc(*NM.did("rows"))

            def next_rms(r, c, k):
                if (c, k) == (6, 1):
                    pe.wait_ge(*NV("sum", r))
                    for t in range(TT):
                        last = pe.matmul(M[0][:, t:t + 1], acc_sq[:, t * P:(t + 1) * P], ones, start=True, stop=True)
                    last.then_inc(*NM.did("ss2"))
                if (c, k) == (7, 1):
                    pe.wait_ge(*NG("pow2", r))
                    rows(lambda t: M[1][:, t * P:(t + 1) * P], lambda t: powed[:, t:t + 1], TT)\
                        .then_inc(*NM.did("rows2"))

            def cross(l, r):
                CM.round(l)

                def hop(name):
                    h = int(name[1])
                    if name[0] == "s":
                        pe.wait_ge(acc_free, 2 * (P_Q[l] + h // 2) + h % 2 + 1)
                        pe.wait_ge(*(NV("rs", r) if h == 0 else CA(f"o{h - 1}", l)))
                        for t in range(TT):
                            last = pe.matmul(flat(m01)[:, t * MEM:(t + 1) * MEM], cq[:, h * T + t * P:h * T + (t + 1) * P],
                                             mkt(l, h), start=True, stop=True)
                    elif name[0] == "t":
                        pe.wait_ge(*CV(f"p{h}", l))
                        for t in range(TT):
                            for m in range(2):
                                last = pe.transpose(m23[:, m, t * P:(t + 1) * P],
                                                    cp[:, t * MEM + m * P:t * MEM + (m + 1) * P], ident)
                    else:
                        pe.wait_ge(*CA(f"t{h}", l))
                        for m in range(2):
                            v0 = (l * 2 + m) * MH * HD + h * HD
                            last = pe.matmul(M[0], mv[:, v0:v0 + HD], cpt[:, m * T:(m + 1) * T], start=m == 0, stop=m == 1)
                    last.then_inc(*CM.did(name))
                for c in range(16):
                    def between(k):
                        next_rms(r, c, k)
                        for name in hops_at(C_HOPS, C_SLOTS, 4 * c + k, 4 * c + k + 1):
                            hop(name)
                    chunk(LAYERS_Q[l] + c, P_Q[l] + c // 4, 4 * (c % 4), KT - 1, between=between,
                          ready=(lambda kt: NV(f"lo{kt}", r)) if c < 4 else None)
                out_phase(LAYERS_O[l], P_O[l], 1, lambda kt: CV(f"lo{kt}", l))

            out_phase(C_OUT0, P_OUT0, 4, lambda kt: ZV(f"lo{kt}", 0))
            norm(0)
            cross(0, 0)
            norm(1)
            for n in range(8):
                for c in range(16):
                    chunk(C_C + 16 * n + c, P_C + 4 * n + c // 4, 4 * (c % 4), KT - 1,
                          between=(lambda k: next_rms(1, c, k)) if n == 0 else None,
                          ready=(lambda kt: NV(f"lo{kt}", 1)) if n == 0 and c < 4 else None)
            out_phase(C_OUT1, P_OUT1, 4, lambda kt: ZV(f"lo{kt}", 1))
            norm(2)
            cross(1, 2)
            norm(3)
            for n in range(16):
                kg, t = n // TT, n % TT
                pe.wait_ge(*NG(f"x{4 * kg + 3}", 3))
                if n >= 4:
                    pe.wait_ge(*FV(f"o{n - 4}"))
                else:
                    pe.wait_ge(acc_free, 2 * (P_O1 + 8))
                for j in range(4):
                    last = pe.transpose(acc[n % 4][:, j * P:(j + 1) * P],
                                        X[:, (4 * kg + j) * T + t * P:(4 * kg + j) * T + (t + 1) * P], ident)
                last.then_inc(*FM.did(f"o{n}"))

        @block.vector
        def _(dve):
            TTO, STT, TS = dve.tensor_tensor, dve.scalar_tensor_tensor, dve.tensor_scalar

            is_split = set()

            def split(g):
                if g >= CHUNKS or g in is_split:
                    return
                is_split.add(g)
                c, s = g % RAW_SLOTS, g % SPLIT_SLOTS
                dve.wait_ge(hi_ready, g + 1)
                TTO(w_lo[:, s * CW:(s + 1) * CW], raw[:, c * CW:(c + 1) * CW],
                    w_hi[:, s * CW:(s + 1) * CW].bitcast(F32), ALU.subtract).then_inc(lo_ready, 1)

            def bank(pair, n, width=T):
                return acc[2 * (pair % 2) + n][:, 0:width]

            dve.wait_ge(params_in, 32)
            dve.wait_ge(gate_in, 32)
            lam4 = lam_in.rearrange("p (a b n) -> p a b n", a=2, b=2)
            TTO(norm_buf[:, 0:2 * QK].rearrange("p (a n) -> p a n", a=2), lam4[:, :, 0, :], lam4[:, :, 1, :], ALU.mult)\
                .then_inc(*SV.did())
            dve.wait_ge(*SV.last())
            dve.reduce_sum(lam2[:, 0:2], norm_buf[:, 0:2 * QK].rearrange("p (a n) -> p a n", a=2), axis=AX.X)\
                .then_inc(*SV.did("lamsum"))
            dve.wait_ge(*SA("ss3"))
            TS(stat[:, 0:4], stat[:, 0:4], 1.0 / D, EPS, ALU.mult, ALU.add).then_inc(*SV.did("stat"))
            split(0)
            dve.wait_ge(*SA("gate_hi"))
            TTO(gate_lo[:, :], gate_w, gate_hi[:, :].bitcast(F32), ALU.subtract).then_inc(*SV.did("gate_lo"))
            dve.wait_ge(*SM("rows"))
            dve.tensor_copy(rs[:, :], M[1]).then_inc(*SV.did("rs"))

            def start_low(k):
                dve.wait_ge(*SA(f"hi{k}"))
                TTO(H_lo[:, k * T:(k + 1) * T], norm_buf[:, (k % 2) * T:(k % 2 + 1) * T],
                    H_hi[:, k * T:(k + 1) * T].bitcast(F32), ALU.subtract).then_inc(*SV.did(f"lo{k}"))
            for k in range(KT):
                dve.wait_ge(*SA(f"copy{k}"))
                dve.wait_ge(*SV.last())
                STT(out=norm_buf[:, (k % 2) * T:(k % 2 + 1) * T], in0=start_banks[k % 4], scalar=pcol("norm_pre", k),
                    in1=rs[:, :], op0=ALU.mult, op1=ALU.mult).then_inc(*SV.did(f"norm{k}"))
                if k:
                    start_low(k - 1)
                    split_ahead(split, k - 1, C_AB)
            start_low(KT - 1)

            def gate_columns():
                dve.wait_ge(*SM("gate_cols"))
                dve.tensor_copy(norm_buf[0:16, 0:T], M[1][0:16, :]).then_inc(*SV.did("gate_cols"))

            def gates_in():
                dve.wait_ge(*SM("gates"))
                g16 = M[0][:, 0:TT * 16].rearrange("p (t n) -> p n t", n=16)
                v = lambda t: t.rearrange("p (h t) -> p h t", t=TT)
                dve.tensor_copy(v(t1), g16[:, 0:HEADS, :]).then_inc(*SV.did())
                TTO(v(t2), g16[:, HEADS:2 * HEADS, :], over_row(p_("dt_bias"), HEADS, TT), ALU.add)\
                    .then_inc(*SV.did("gates"))

            def gates_out():
                dve.wait_ge(*SA("small_exp"))

                def then(ins, name=None):
                    ins.then_inc(*SV.did(name))
                    dve.wait_ge(*SV.last())
                then(STT(out=neg_lam, in0=lam2[:, 1:2], scalar=LAM_INIT, in1=lam2[:, 0:1], op0=ALU.subtract,
                         op1=ALU.subtract))
                then(TS(a_gain, p_("a_norm"), 0.5, None, ALU.mult))
                then(TS(b_gain, p_("b_norm"), 0.5 * (1.0 - LAM_INIT), None, ALU.mult))
                then(TS(t1, t1, 1.0, None, ALU.add))
                then(dve.reciprocal(beta, t1))
                then(TS(v_scale, beta, 0.5, None, ALU.mult))
                then(TS(t4, t3, 2.0, None, ALU.add))
                then(dve.reciprocal(t4, t4))
                then(TTO(t4, t3, t4, ALU.mult))
                then(TTO(t5, t4, t4, ALU.mult))
                then(TS(t3, t5, 1.0 / 15, None, ALU.mult))
                for n in (13, 11, 9, 7, 5, 3):
                    then(STT(out=t3, in0=t3, scalar=1.0 / n, in1=t5, op0=ALU.add, op1=ALU.mult))
                then(STT(out=t3, in0=t3, scalar=1.0, in1=t4, op0=ALU.add, op1=ALU.mult))
                then(TS(t2, t2, 0.0, None, ALU.max))
                then(STT(out=t2, in0=t3, scalar=2.0, in1=t2, op0=ALU.mult, op1=ALU.add))
                v = lambda t: t.rearrange("p (h t) -> p h t", t=TT)
                then(STT(out=v(g_col), in0=v(t2), scalar=-1.0, in1=over_row(p_("A_log"), HEADS, TT), op0=ALU.mult,
                         op1=ALU.mult), "g")

            def decays():
                dve.wait_ge(*SM("decays"))
                dve.tensor_copy(decay, M[0][:, 0:32]).then_inc(*SV.did("decay"))
                dve.wait_ge(*SA("decays"))
                TTO(k_in_scale, k_in_scale, beta, ALU.mult).then_inc(*SV.did("kin"))

            def delta(name, i):
                def then(ins, tag=None):
                    ins.then_inc(*GV.did(tag))
                    dve.wait_ge(*GV.last())
                hc = bass.ds(2 * i * TT, 2 * TT)
                if name == "ss":
                    GV.round(i)
                    dve.wait_ge(*GM("ss", i))
                    TS(stat, M[0][:, 0:16], 0.25, EPS, ALU.mult, ALU.add).then_inc(*GV.did("stat"))
                    dve.wait_ge(*GG("pow", i))
                    TS(powed[:, 0:8], powed[:, 0:8], 0.5 * HD ** -0.5, None, ALU.mult).then_inc(*GV.did())
                    TS(powed[:, 8:16], powed[:, 8:16], 0.5, None, ALU.mult).then_inc(*GV.did("pw"))
                elif name == "rows":
                    dve.wait_ge(*GM("rows", i))
                    TTO(kc, kc, flat(m01), ALU.mult).then_inc(*GV.did())
                    TTO(qc, qc, flat(m23), ALU.mult).then_inc(*GV.did("qn"))
                elif name == "tr":
                    dve.wait_ge(*GA("kv", i))
                    TTO(tiles(k_out), psum_tiles(m01), over_row(k_out_scale[:, hc], 8, P), ALU.mult)\
                        .then_inc(*GV.did("k_out"))
                elif name == "dk":
                    dve.wait_ge(*GM("dk", i))
                    then(TTO(tiles(gam), psum_tiles(m01), over_row(decay[:, hc], 8, P), ALU.subtract))
                    then(TTO(tiles(gam), tiles(gam), over_tiles(c_("causal"), 8), ALU.add), "gam")
                    dve.wait_ge(*GA("edec", i))
                    TTO(q_dec, qc, prod, ALU.mult).then_inc(*GV.did("qd"))
                    dve.wait_ge(*GA("gam", i))
                    then(TTO(n_t, flat(m23), gam, ALU.mult), "nt0")
                elif name == "qb":
                    dve.wait_ge(*GM("qb", i))
                    TTO(n_t, flat(m23), n_t, ALU.mult).then_inc(*GV.did("nt"))
                    TTO(qk_t, flat(m01), gam, ALU.mult).then_inc(*GV.did("qk"))
                elif name == "p0":
                    dve.wait_ge(*GM("p0", i))
                    TTO(tiles(inv), over_tiles(ident, 8), psum_tiles(m01), ALU.subtract).then_inc(*GV.did())
                    TTO(tiles(inv_t), over_tiles(ident, 8), tiles(c_t), ALU.subtract).then_inc(*GV.did("y0"))
                elif name[0] == "y":
                    dve.wait_ge(*GM(name, i))
                    if name != "y5":
                        dve.wait_ge(*GV.last())
                        TTO(inv, inv, flat(m23), ALU.subtract).then_inc(*GV.did())
                    TTO(inv_t, inv_t, flat(m01), ALU.subtract).then_inc(*GV.did(name))
                elif name == "uw":
                    dve.memset(state, 0.0).then_inc(*GV.did("st0"))
                elif name[0] == "r":
                    c = int(name[1])
                    t, p0 = c // 2, CH * (c % 2)
                    ps = slice(p0, p0 + CH)
                    dve.wait_ge(*GM(name, i))
                    TTO(head2(v_new[ps, :]), head2(u_tok[ps, :])[:, :, t * P:(t + 1) * P],
                        head2(M[0][ps, 0:2 * HD]), ALU.subtract).then_inc(*GV.did(f"vn{c}"))
                elif name[0] == "s" and name != "s7":
                    c = int(name[1])
                    t, half = c // 2, c % 2
                    dve.wait_ge(*GM(name, i))
                    for h in range(2):
                        o = slice(h * HD, (h + 1) * HD)
                        STT(out=state[:, o], in0=state[:, o], scalar=chunk_decay[:, bass.ds(half * 32 + (2 * i + h) * TT + t, 1)],
                            in1=M[1][:, o], op0=ALU.mult, op1=ALU.add).then_inc(*GV.did(f"st{c + 1}"))
                elif name == "fs":
                    dve.wait_ge(*GM("fs", i))
                    TS(stat[:, 0:8], M[0][:, 0:8], 1.0 / HD, EPS, ALU.mult, ALU.add).then_inc(*GV.did("fstat"))
                elif name == "fb":
                    dve.wait_ge(*GM("fb", i))
                    then(STT(out=prod, in0=prod, scalar=a_gain, in1=flat(m01), op0=ALU.mult, op1=ALU.mult))
                    y = X[:, bass.ds(2 * i * T, 2 * T)]
                    TTO(y, y, prod, ALU.mult).then_inc(*GV.did("end"))

            def attn(name, i):
                def then(ins, tag=None):
                    ins.then_inc(*BV.did(tag))
                    dve.wait_ge(*BV.last())
                if name in ("begin", "begin_k"):
                    dst, tag = (kr, "k") if name == "begin_k" else (qr, "q")
                    if tag == "q":
                        BV.round(i)
                        dve.wait_ge(tables_in, 16)
                    sin = rope_tab[:, T:2 * T].unsqueeze(1).broadcast_to([P, 2, T])
                    dve.wait_ge(*BA("r" + tag, i))
                    then(TTO(head2(rot), head2(rot), sin, ALU.mult))
                    dve.wait_ge(*BG("cos_" + tag, i))
                    TTO(dst, dst, rot, ALU.add).then_inc(*BV.did("r" + tag))
                elif name[0] == "a" and name[2] != "4":
                    h, t = int(name[1]), int(name[2])
                    n = (t + 1) * P
                    dve.wait_ge(*BM(name, i))
                    then(dve.memset(m01[0:CH, :, n - CH:n], NEG))
                    then(dve.reduce_max(mx[:, 0:2], m01[:, :, 0:n], axis=AX.X))
                    TS(nmx[:, 0:2], mx[:, 0:2], -QK ** -0.5, None, ALU.mult).then_inc(*BV.did(f"nm{h}{t}"))
                    dve.wait_ge(*BA(f"p{h}{t}", i))
                    then(dve.reciprocal(rsum[:, 0:2], ssum[:, 0:2]))
                    TTO(coef, rsum[:, 1:2], neg_lam, ALU.mult).then_inc(*BV.did())
                    then(TS(att[:, 0:n], prob[:, 0:n], rsum[:, 0:1], None, ALU.mult))
                    STT(out=att[:, 0:n], in0=prob[:, T:T + n], scalar=coef, in1=att[:, 0:n], op0=ALU.mult,
                        op1=ALU.add).then_inc(*BV.did(f"att{h}{t}"))
                elif name[:2] == "fs":
                    dve.wait_ge(*BM(name, i))
                    TS(stat[:, 0:4], M[0][:, 0:4], 1.0 / HD, EPS, ALU.mult, ALU.add).then_inc(*BV.did("stat" + name[2]))
                elif name[:2] == "fb":
                    h = int(name[2])
                    dve.wait_ge(*BM(name, i))
                    then(STT(out=o_sb, in0=o_sb, scalar=b_gain, in1=M[0], op0=ALU.mult, op1=ALU.mult))
                    y = xt(HEADS + 2 * i + h)
                    TTO(y, y, o_sb, ALU.mult).then_inc(*BV.did(f"y{h}"))

            def convolve(it, sec, n):
                pair = P_AB + 4 * it + 1 + sec
                src, dst = bank(pair, n), (qc, kc, vc)[sec][:, n * T:(n + 1) * T]
                tap = lambda k: pcol("a_conv", (8 * sec + 2 * it + n) * 4 + k)
                dve.wait_ge(chunk_used, done_at(pair))
                TS(dst, src, tap(3), None, ALU.mult).then_inc(*EV.did())
                for d in (1, 2, 3):
                    dve.wait_ge(*EV.last())
                    ins = STT(out=dst[:, d:T], in0=src[:, 0:T - d], scalar=tap(3 - d), in1=dst[:, d:T],
                              op0=ALU.mult, op1=ALU.add)
                    if d < 3:
                        ins.then_inc(*EV.did())
                    else:
                        ins.then_inc(acc_free, 1)

            def gate(it, sec, n):
                dst, o = (qc, kc, vc)[sec], slice(n * T, (n + 1) * T)
                dve.wait_ge(*EA(f"t{sec}{n}", it))
                STT(out=dst[:, o], in0=tanh_t[:, o], scalar=1.0, in1=dst[:, o], op0=ALU.add, op1=ALU.mult)\
                    .then_inc(*EV.did(f"s{sec}{n}"))

            def keep(it, sec, n):
                pair = P_AB + 4 * it + 1 + sec
                dve.wait_ge(chunk_used, done_at(pair))
                dve.tensor_copy((qc, kc, vc)[sec][:, n * T:(n + 1) * T], bank(pair, n)).then_inc(acc_free, 1)

            def gate_z(it):
                pair = P_AB + 4 * it
                if it == 0:
                    dve.wait_ge(spilled, 16 * KT)
                for n in range(2):
                    dve.wait_ge(z_tanh, 2 * it + n + 1)
                    head = (HEADS if it >= 4 else 0) + 2 * (it % 4) + n
                    STT(out=xt(head), in0=tanh_t[:, n * T:(n + 1) * T], scalar=1.0, in1=bank(pair, n), op0=ALU.add,
                        op1=ALU.mult).then_inc(acc_free, 1)

            def evacuate(it, sec, c):
                if it < 4:
                    if c:
                        gate(it, sec, c - 1)
                    if c < 2:
                        convolve(it, sec, c)
                elif c < 2:
                    keep(it, sec, c)

            def mem_stat():
                dve.wait_ge(*MA("ss"))
                TTO(t1[:, 4:6], t1[:, 0:2], t1[:, 2:4], ALU.add).then_inc(*MV.did())
                dve.wait_ge(*MV.last())
                TS(t1[:, 6:8], t1[:, 4:6], 1.0 / D, EPS, ALU.mult, ALU.add).then_inc(*MV.did("stat"))

            def mem_low(l, g):
                def low(g):
                    dve.wait_ge(*MA(f"hi{l}{g}"))
                    TTO(mem_g(H_lo, l, g), mem_scaled[g % 2][:, :], mem_g(H_hi, l, g).bitcast(F32), ALU.subtract)\
                        .then_inc(*MV.did(f"lo{l}{g}"))
                dve.wait_ge(*MM(f"t{l}{g}"))
                dve.wait_ge(*MV.last())
                gain = p_("mem_norm")[:, l * KT + 2 * g:l * KT + 2 * g + 2]
                rows_of = lambda t: t.rearrange("p (k n) -> p k n", n=MEM)
                TTO(rows_of(mem_scaled[g % 2][:, :]), rows_of(acc[2 * l + g % 2][:, :]), over_row(gain, 2, MEM), ALU.mult)\
                    .then_inc(*MV.did(f"m{l}{g}"))
                if g:
                    low(g - 1)
                if g == 7:
                    low(g)

            for it in range(AB_ITERS):
                reply, i = (delta, it - 1) if it <= 4 else (attn, it - 5)
                for c in range(16):
                    split(C_AB + 16 * it + c + 1)
                    if it == 6 and c == 12:
                        mem_stat()
                    if it and c < 3:
                        evacuate(it - 1, 2, c)
                    if c == 2:
                        EV.round(it)
                    if it == 0 and c == 4:
                        gate_columns()
                    if c == 4:
                        gate_z(it)
                    if it == 0 and c == 5:
                        gates_in()
                        gates_out()
                    if it == 0 and c == 7:
                        decays()
                    for sec, at_ in ((0, 8), (1, 12)):
                        if at_ <= c < at_ + 3:
                            evacuate(it, sec, c - at_)
                    if it:
                        if c == 2:
                            reply("begin", i)
                        if c == 3 and it > 4:
                            reply("begin_k", i)
                        names, slots = (D_HOPS, D_SLOTS) if it <= 4 else (B_HOPS, B_SLOTS)
                        for k in range(4):
                            for name in hops_at(names, slots, 4 * c + k, 4 * c + k + 1):
                                reply(name, i)
                            if it == 7 and c >= 14:
                                mem_low(0, 4 * (c - 14) + k)

            def take_kv(q, c):
                l, j, pair = q // 4, q % 4, P_KV + q
                if c == 0:
                    dve.wait_ge(chunk_used, done_at(pair))
                    for n in range(2):
                        if j < 2:
                            dve.tensor_copy(mkt(l, 2 * j + n), bank(pair, n, MEM)).then_inc(acc_free, 1)
                        else:
                            dve.tensor_copy(v_feat[:, n * MEM:(n + 1) * MEM], bank(pair, n, MEM))\
                                .then_inc(*MV.did(f"vf{l}{j}"))
                elif c == 2 and j >= 2:
                    dve.wait_ge(*MM(f"v{l}{j}"))
                    for n in range(2):
                        h = 2 * (j - 2) + n
                        dst = mv[:, l * 2 * MH * HD:(l + 1) * 2 * MH * HD].rearrange("p (m h n) -> p m h n", m=2, h=MH)
                        dve.tensor_copy(dst[:, :, h, :], bank(pair, 0)[:, n * MEM:(n + 1) * MEM].rearrange(
                            "p (m n) -> p m n", m=2)).then_inc(acc_free, 1)
            for c in range(32):
                split(C_KV + c + 1)
                if c == 0:
                    for n in range(2):
                        keep(7, 2, n)
                if 1 <= c <= 2:
                    for k in range(4):
                        mem_low(1, 4 * (c - 1) + k)
                if c in (0, 3):
                    attn("begin_k" if c else "begin", 3)
                if c >= 4:
                    take_kv(c // 4 - 1, c % 4)
                for name in hops_at(B_HOPS, B_SLOTS, 2 * c, 2 * c + 2):
                    attn(name, 3)
            take_kv(7, 0)
            take_kv(7, 2)

            def split_input(r, src, c0):
                ZV.round(r)
                for k in range(KT):
                    dve.wait_ge(*ZA(f"hi{k}", r))
                    TTO(H_lo[:, k * T:(k + 1) * T], src(k), H_hi[:, k * T:(k + 1) * T].bitcast(F32), ALU.subtract)\
                        .then_inc(*ZV.did(f"lo{k}"))
                    split_ahead(split, k, c0)

            def out_phase(c0, p0, per):
                def take(n):
                    dve.wait_ge(chunk_used, done_at(p0 + n))
                    for j in range(2):
                        dve.tensor_copy(yt(2 * n + j), bank(p0 + n, j)).then_inc(acc_free, 1)
                for n in range(8):
                    for c in range(per):
                        split(c0 + per * n + c + 1)
                        if c == 0 and n:
                            take(n - 1)
                take(7)

            def norm(r):
                NV.round(r)
                dve.wait_ge(*NM("ss", r))
                TS(stat[:, 0:4], M[0][:, 0:4], 1.0 / D, EPS, ALU.mult, ALU.add).then_inc(*NV.did("stat"))
                if r < 3:
                    split((C_Q0, C_C, C_Q1)[r] + 1)
                dve.wait_ge(*NM("rows", r))
                post = ("norm_post", "x_post", "norm_post", "x_post")[r]
                pre = ("x_pre", "norm_pre", "x_pre", None)[r]
                layer, next_layer = r // 2, (0, 1, 1, 1)[r]

                def low(k):
                    dve.wait_ge(*NA(f"hi{k}", r))
                    STT(out=H_lo[:, k * T:(k + 1) * T], in0=xt(k), scalar=pcol(pre, next_layer * KT + k),
                        in1=H_hi[:, k * T:(k + 1) * T].bitcast(F32), op0=ALU.mult, op1=ALU.subtract)\
                        .then_inc(*NV.did(f"lo{k}"))
                for k in range(KT):
                    if k == 0:
                        dve.wait_ge(acc_free, 2 * (P_OUT0 + 8, P_O0 + 8, P_OUT1 + 8, P_O1 + 8)[r])
                    STT(out=yt(k), in0=yt(k), scalar=pcol(post, layer * KT + k), in1=M[1], op0=ALU.mult, op1=ALU.mult)\
                        .then_inc(*(NV if r < 3 else FV).did(f"y{k}"))
                    if k >= 2 and pre:
                        low(k - 2)
                        if k > 2:
                            split_ahead(split, k, (C_Q0, C_C, C_Q1)[r])
                if pre:
                    low(KT - 2)
                    low(KT - 1)
                    dve.wait_ge(*NA("sq15", r))

            def sum_squares(r, c):
                for t in {3: (0, 1), 4: (2,), 5: (3,)}.get(c, ()):
                    o = slice(t * P, (t + 1) * P)
                    dve.reduce_sum(acc_sq[:, o], Y[:, :].rearrange("p (k t) -> p t k", k=KT)[:, o, :], axis=AX.X)\
                        .then_inc(*NV.did("sum"))
                if c == 6:
                    dve.wait_ge(*NM("ss2", r))
                    TS(stat[:, 0:4], M[0][:, 0:4], 1.0 / D, EPS, ALU.mult, ALU.add).then_inc(*NV.did("stat2"))
                elif c == 7:
                    dve.wait_ge(*NM("rows2", r))
                    dve.tensor_copy(rs[:, :], M[1]).then_inc(*NV.did("rs"))
                    dve.wait_ge(*NV.last())

            def cross(l, r):
                CV.round(l)

                def then(ins, tag=None):
                    ins.then_inc(*CV.did(tag))
                    dve.wait_ge(*CV.last())

                def take(n):
                    dve.wait_ge(chunk_used, done_at(P_Q[l] + n))
                    for j in range(2):
                        dst = (cq, cz)[n // 2][:, (2 * (n % 2) + j) * T:(2 * (n % 2) + j + 1) * T]
                        TTO(dst, bank(P_Q[l] + n, j), rs[:, :], ALU.mult).then_inc(acc_free, 1)

                def gate(n):
                    for h in (2 * n, 2 * n + 1):
                        o = slice(h * T, (h + 1) * T)
                        dve.wait_ge(*CA(f"zt{h}", l))
                        STT(out=cz[:, o], in0=zt(h), scalar=1.0, in1=cz[:, o], op0=ALU.add, op1=ALU.mult)\
                            .then_inc(*CV.did(f"zz{h}"))

                def outputs(n):
                    for h in (2 * n, 2 * n + 1):
                        o = slice(h * T, (h + 1) * T)
                        if n == 1 and h == 2:
                            dve.wait_ge(*CA("o3", l))
                        dve.wait_ge(*CV(f"zz{h}", l))
                        TTO(cq[:, o], cq[:, o], cz[:, o], ALU.mult).then_inc(*CV.did(f"y{h}"))
                    for h in (2 * n, 2 * n + 1):
                        o = slice(h * T, (h + 1) * T)
                        dve.wait_ge(*CA(f"hi{h}", l))
                        TTO(H_lo[:, o], cq[:, o], H_hi[:, o].bitcast(F32), ALU.subtract).then_inc(*CV.did(f"lo{h}"))

                def reply(name):
                    h = int(name[1])
                    s4 = flat(m01).rearrange("p (t m) -> p t m", m=MEM)
                    if name[0] == "s":
                        dve.wait_ge(*CM(name, l))
                        then(dve.reduce_max(mx, s4, axis=AX.X))
                        TS(nmx, mx, -P ** -0.5, None, ALU.mult).then_inc(*CV.did(f"nm{h}"))
                        dve.wait_ge(*CA(f"p{h}", l))
                        then(dve.reciprocal(rsum, ssum))
                        c4 = cp.rearrange("p (t m) -> p t m", m=MEM)
                        TTO(c4, c4, over_row(rsum, TT, MEM), ALU.mult).then_inc(*CV.did(f"p{h}"))
                for c in range(16):
                    split(LAYERS_Q[l] + c + 1)
                    sum_squares(r, c)
                    if c in (7, 8, 12):
                        take({7: 0, 8: 1, 12: 2}[c])
                    for name in hops_at(C_HOPS, C_SLOTS, 4 * c, 4 * c + 4):
                        reply(name)
                    if c == 13:
                        gate(0)
                    if c == 15:
                        outputs(0)
                take(3)
                gate(1)
                outputs(1)
                out_phase(LAYERS_O[l], P_O[l], 1)

            def take_conv(n, j):
                pair = P_C + 4 * n + j
                dve.wait_ge(chunk_used, done_at(pair))
                for k in range(2):
                    o = slice(k * T, (k + 1) * T)
                    dst = (uu, cu, bb, bb)[j]
                    if j == 3:
                        dve.wait_ge(*VV.last())
                    TTO(dst[:, o], bank(pair, k), rs[:, :], ALU.mult).then_inc(acc_free, 1)
                dve.wait_ge(acc_free, 2 * (pair + 1))
                for k in range(2):
                    o = slice(k * T, (k + 1) * T)
                    tap = lambda d: pcol("c_conv", (2 * n + k) * 3 + d)
                    if j == 1:
                        TTO(cu[:, o], cu[:, o], uu[:, o], ALU.mult).then_inc(*VV.did())
                        dve.wait_ge(*VV.last())
                        TS(cv[:, o], cu[:, o], tap(2), None, ALU.mult).then_inc(*VV.did())
                        for d in (1, 2):
                            dve.wait_ge(*VV.last())
                            STT(out=cv[:, k * T + d:(k + 1) * T], in0=cu[:, k * T:(k + 1) * T - d], scalar=tap(2 - d),
                                in1=cv[:, k * T + d:(k + 1) * T], op0=ALU.mult, op1=ALU.add).then_inc(*VV.did())
                    elif j == 2:
                        if k == 0:
                            dve.wait_ge(*VV.last())
                        TTO(cv[:, o], cv[:, o], bb[:, o], ALU.mult).then_inc(*VV.did())
                    elif j == 3:
                        dve.wait_ge(*VA(f"z{k}", n))
                        STT(out=bb[:, o], in0=uu[:, o], scalar=1.0, in1=bb[:, o], op0=ALU.add, op1=ALU.mult)\
                            .then_inc(*VV.did())
                        dve.wait_ge(*VV.last())
                        STT(out=yt(2 * n + k), in0=cv[:, o], scalar=0.5, in1=bb[:, o], op0=ALU.mult, op1=ALU.mult)\
                            .then_inc(*VV.did(f"y{k}"))

            split_input(0, xt, C_OUT0)
            out_phase(C_OUT0, P_OUT0, 4)
            norm(0)
            cross(0, 0)
            norm(1)
            for n in range(8):
                for c in range(16):
                    split(C_C + 16 * n + c + 1)
                    if n == 0:
                        sum_squares(1, c)
                    if n and c == 0:
                        take_conv(n - 1, 3)
                    if c == 1:
                        VV.round(n)
                    if c == (7 if n == 0 else 4):
                        take_conv(n, 0)
                    if c in (8, 12):
                        take_conv(n, c // 4 - 1)
            take_conv(7, 3)
            split_input(1, yt, C_OUT1)
            out_phase(C_OUT1, P_OUT1, 4)
            norm(2)
            cross(1, 2)
            norm(3)
            for n in range(16):
                dve.wait_ge(*FM(f"o{n}"))
                dve.wait_ge(*NG(f"x{4 * (n // 4) + 3}", 3))
                dve.tensor_copy(yt(n), acc[n % 4][:, :]).then_inc(*FV.did(f"o{n}"))

        @block.gpsimd
        def _(pool):
            def power(src, dst, n):
                return pool.tensor_tensor(dst[:, 0:n], src[:, 0:n], minus_half[:, 0:n], ALU.pow)

            pool.memset(minus_half, -0.5).then_inc(const_set, 1)
            pool.wait_ge(const_set, 1)
            pool.wait_ge(*SV("stat"))
            power(stat, powed, 4).then_inc(*SG.did("pow"))

            for i in range(4):
                GG.round(i)
                if i:
                    pool.wait_ge(*GM("fb", i - 1))
                pool.wait_ge(*GV("stat", i))
                power(stat, powed, 16).then_inc(*GG.did("pow"))
                for s in range(len(LEVELS)):
                    if s == 0:
                        pool.wait_ge(*GV("nt", i))
                    else:
                        pool.wait_ge(*GM(f"p{s - 1}", i))
                        if s == 1:
                            pool.wait_ge(*GV("y0", i))
                    pool.tensor_tensor(tiles(c_t), tiles(n_t), over_tiles(level_mask(s), 8), ALU.mult)\
                        .then_inc(*GG.did(f"c{s}"))
                pool.wait_ge(*GV("fstat", i))
                power(stat, powed, 8).then_inc(*GG.did("fpow"))

            def attention_pair(i):
                BG.round(i)
                pool.wait_ge(tables_in, 16)
                pool.wait_ge(acc_free, 2 * (P_AB + 4 * (4 + i) + 3))
                if i:
                    pool.wait_ge(*BM("a14", i - 1))
                cos = rope_tab[:, 0:T].unsqueeze(1).broadcast_to([P, 2, T])
                for src, dst, tag in ((qc, qr, "q"), (kc, kr, "k")):
                    pool.tensor_tensor(head2(dst), head2(src), cos, ALU.mult).then_inc(*BG.did("cos_" + tag))
                for h in range(2):
                    if h:
                        pool.wait_ge(*BM("fb0", i))
                    pool.wait_ge(*BV(f"stat{h}", i))
                    power(stat, powed, 4).then_inc(*BG.did(f"pow{h}"))
            pool.wait_ge(*GM("fb", 3))
            for i in range(4):
                attention_pair(i)
                if i == 1:
                    pool.wait_ge(*MV("stat"))
                    pool.tensor_tensor(t2[:, 0:2], t1[:, 6:8], minus_half[:, 0:2], ALU.pow).then_inc(*MG.did("pow"))

            for r in range(4):
                OG.round(r)
                NG.round(r)
                if r == 0:
                    pool.wait_ge(reloaded, 16 * KT)
                else:
                    pool.wait_ge(*NM("ss2", r - 1))
                pool.memset(acc_sq, 0.0).then_inc(*OG.did())
                for k in range(KT - 2):
                    pool.wait_ge(*OA(f"s{k}", r))
                    pool.wait_ge(*OG.last())
                    pool.tensor_tensor(acc_sq, acc_sq, sqt[:, (k % 2) * T:(k % 2 + 1) * T], ALU.add)\
                        .then_inc(*OG.did(f"a{k}"))
                pool.wait_ge(*NV("stat", r))
                power(stat, powed, 4).then_inc(*NG.did("pow"))
                for k in range(KT):
                    pool.wait_ge(*(NV(f"y{k}", r) if r < 3 else FV(f"y{k}")))
                    pool.tensor_tensor(xt(k), xt(k), yt(k), ALU.add).then_inc(*NG.did(f"x{k}"))
                if r < 3:
                    pool.wait_ge(*NV("stat2", r))
                    power(stat, powed, 4).then_inc(*NG.did("pow2"))


def done_at(pair):
    for p0, c0, n, per in ((P_O1, C_O1, 8, 1), (P_Q1, C_Q1, 4, 4), (P_OUT1, C_OUT1, 8, 4), (P_C, C_C, 32, 4),
                           (P_O0, C_O0, 8, 1), (P_AB, C_AB, 52, 4)):
        if not isinstance(pair, int) or pair >= p0:
            return c0 + per * (pair - p0 + 1)


def shape_constants():
    c = np.zeros((P, CONST_W), np.float32)
    j, i = np.mgrid[0:P, 0:P]
    same = j // CH == i // CH
    put = lambda name, a: c.__setitem__((slice(None), slice(*CONST[name])), a)
    put("ident", j == i)
    put("cumsum", same & (j <= i))
    put("suffix", same & (j > i))
    put("half0", j < CH)
    put("half1", j >= CH)
    put("causal", np.where(same & (j <= i), 0.0, NEG))
    put("levels", np.concatenate([(j // (2 * s) == i // (2 * s)) & (j // s % 2 == 0) & (i // s % 2 == 1)
                                  for s in LEVELS], axis=1))
    put("ones", 1.0)
    inv_freq = (np.float32(10000.0) ** (-np.arange(0, QK, 2, dtype=np.float32) / np.float32(QK))).astype(np.float32)
    angle = (np.arange(T, dtype=np.float32)[None, :] * inv_freq[:, None]).astype(np.float32).astype(np.float64)
    put("cos", np.tile(np.cos(angle), (4, 1)))
    put("sin", np.concatenate([-np.sin(angle), np.sin(angle)] * 2, axis=0))
    return c


def kernel(x, mem, norm_pre, norm_post, xattn_norm_pre, xattn_norm_post, mem_norm, ab_w_in, a_conv, a_A_log,
           a_dt_bias, a_out_norm, b_lambda, b_out_norm, ab_w_out, c_w_in, c_conv, c_w_out, m_w_q, m_w_kv, m_w_o):
    import concourse.bacc as bacc
    from concourse.bass_utils import run_bass_kernel_spmd

    gains = lambda g: np.asarray(g).reshape(2 * KT, P).T
    taps = lambda w, n: np.asarray(w)[0].reshape(n, -1, P).transpose(2, 1, 0).reshape(P, -1)
    everywhere = lambda v: np.broadcast_to(np.asarray(v).reshape(1, -1), (P, np.asarray(v).size))
    parameters = np.concatenate([gains(norm_pre), gains(norm_post), gains(xattn_norm_pre), gains(xattn_norm_post),
                                 gains(mem_norm), taps(a_conv, 4), taps(c_conv, 3), np.asarray(a_out_norm).T,
                                 np.asarray(b_out_norm).T, everywhere(a_A_log), everywhere(a_dt_bias)], axis=1)
    arrays = {"x": np.asarray(x)[0], "mem": np.asarray(mem)[0], "constants": shape_constants(),
              "parameters": np.ascontiguousarray(parameters), "lambda": np.ascontiguousarray(everywhere(b_lambda)),
              "ab_w_in": np.asarray(ab_w_in)[0], "ab_w_out": np.asarray(ab_w_out)[0], "c_w_in": np.asarray(c_w_in)[0],
              "c_w_out": np.asarray(c_w_out)[0], "m_w_q": np.asarray(m_w_q), "m_w_kv": np.asarray(m_w_kv),
              "m_w_o": np.asarray(m_w_o)}
    books = {}
    for final in (False, True):
        nc = bacc.Bacc("TRN2", target_bir_lowering=False, num_devices=1)
        dram = {n: nc.dram_tensor("in_" + n, a.shape, F32, kind="ExternalInput").ap() for n, a in arrays.items()}
        dram["spill"] = nc.dram_tensor("spill", (KT, P, T), F32, kind="Internal").ap()
        dram["out"] = nc.dram_tensor("out", (T, D), F32, kind="ExternalOutput").ap()
        build(nc, books, dram)
    result = run_bass_kernel_spmd(nc, [{"in_" + n: np.ascontiguousarray(a) for n, a in arrays.items()}], core_ids=[0])
    return result.results[0]["out"].reshape(1, T, D)
```

```python
import concourse.bass as bass
import concourse.mybir as mybir
import math
from contextlib import ExitStack
import numpy as np

F32, F32R = mybir.dt.float32, mybir.dt.float32r
ALU, ACT, AX = mybir.AluOpType, mybir.ActivationFunctionType, mybir.AxisListType

P = 128
T, D, MEM = 512, 2048, 256
KT = D // P
TT = T // P
EPS = 1e-6
HEADS, HD = 8, 128
QK = 64
MH = 4
CH = 64
LAM_INIT = 0.8 - 0.6 * math.exp(0.0)
AB_B = 4 * 1024 + 2 * HEADS
RAW_SLOTS, SPLIT_SLOTS = 4, 2
CW = 4 * 256
NEG = -1e30
LEVELS = (1, 2, 4, 8, 16, 32)

AB_ITERS = 8
C_AB, P_AB = 0, 0
C_KV, P_KV = C_AB + 16 * AB_ITERS, P_AB + 4 * AB_ITERS
C_OUT0, P_OUT0 = C_KV + 32, P_KV + 8
C_Q0, P_Q0 = C_OUT0 + 32, P_OUT0 + 8
C_O0, P_O0 = C_Q0 + 16, P_Q0 + 4
C_C, P_C = C_O0 + 8, P_O0 + 8
C_OUT1, P_OUT1 = C_C + 128, P_C + 32
C_Q1, P_Q1 = C_OUT1 + 32, P_OUT1 + 8
C_O1, P_O1 = C_Q1 + 16, P_Q1 + 4
CHUNKS = C_O1 + 8

CONST = {}
_at = 0
for _name, _width in (("ident", P), ("cumsum", P), ("suffix", P), ("half0", P), ("half1", P), ("causal", P),
                      ("levels", len(LEVELS) * P), ("ones", 1), ("cos", T), ("sin", T)):
    CONST[_name] = (_at, _at + _width)
    _at += _width
CONST_W = _at
RESIDENT_W = CONST["cos"][0]

PARAM = {}
_at = 0
for _name, _width in (("norm_pre", 2 * KT), ("norm_post", 2 * KT), ("x_pre", 2 * KT), ("x_post", 2 * KT),
                      ("mem_norm", 2 * KT), ("a_conv", 24 * 4), ("c_conv", 16 * 3), ("a_norm", 1),
                      ("b_norm", 1), ("A_log", HEADS), ("dt_bias", HEADS)):
    PARAM[_name] = (_at, _at + _width)
    _at += _width
PARAM_W = _at


class Steps:

    def __init__(self, sem, book):
        self.sem, self.book, self.n, self.i = sem, book, 0, 0

    def round(self, i):
        self.n, self.i = 0, i

    def did(self, name=None):
        self.n += 1
        if name is not None:
            self.book[name] = self.n
        self.book["/"] = max(self.book.get("/", 0), self.n)
        return self.sem, 1

    def __call__(self, name, i=0):
        return self.sem, i * self.book.get("/", 0) + self.book.get(name, 1)

    def last(self):
        return self.sem, self.i * self.book.get("/", 0) + self.n


def spread(n_hops, first, last):
    return [first + (k * (last - first)) // max(n_hops - 1, 1) for k in range(n_hops)]



D_HOPS = (["ss", "rows", "tr", "dk", "qb", "p0"] + [f"{x}{s}" for s in range(1, 6) for x in ("p", "y")]
          + ["uw"] + [f"{x}{c}" for c in range(T // CH) for x in ("r", "s")] + ["fs", "fb"])
B_HOPS = ["vt"]
for _h in "01":
    B_HOPS += ["a" + _h + "0"] + [f"{x}{_h}{t + (x == 'a')}" for t in range(TT) for x in ("a", "b")]
    B_HOPS += ["fs" + _h, "fb" + _h]
C_HOPS = [f"{x}{h}" for h in range(MH) for x in "sto"]


def weighted(names, first, last, weights):
    at_, total = [0.0], sum(weights.get(n, weights.get(n[0], 1.0)) for n in names[:-1])
    for n in names[:-1]:
        at_.append(at_[-1] + weights.get(n, weights.get(n[0], 1.0)))
    return [first + int(a * (last - first) / total) for a in at_]


D_REPLY = {"ss": 4.5, "rows": 3.0, "tr": 6.0, "dk": 6.0, "qb": 4.5, "p0": 4.0, "p": 1.7, "y": 3.0, "uw": 3.0,
           "r": 1.5, "s": 1.9, "s7": 3.0, "fs": 4.5}
D_SLOTS, B_SLOTS, C_SLOTS = weighted(D_HOPS, 12, 63, D_REPLY), spread(len(B_HOPS), 18, 63), spread(len(C_HOPS), 32, 62)


VECTOR_ADDS = (1, 4, 7, 10, 13)
PROJECTED_AFTER = 0
AHEAD = (0, 9, 13, 15)


def split_ahead(split, k, c0):
    if k in AHEAD:
        split(c0 + AHEAD.index(k) + 1)


def ab_done(pair):
    return C_AB + 4 * (pair - P_AB + 1)


def hops_at(names, slots, lo, hi):
    return [n for n, s in zip(names, slots) if lo <= s < hi]


def build(nc, books, dram):
    ctx = ExitStack()
    with ctx:
        sb = lambda name, width, dt=F32: ctx.enter_context(nc.sbuf_tensor(name, [P, width], dt))
        sem = lambda name: ctx.enter_context(nc.semaphore(name))
        steps = lambda name: Steps(sem(name), books.setdefault(name, {}))

        X = sb("residual", KT * T)
        H_hi, H_lo = sb("input_hi", KT * T, F32R), sb("input_lo", KT * T, F32R)
        raw = sb("weights_raw", RAW_SLOTS * CW)
        w_hi, w_lo = sb("weights_hi", SPLIT_SLOTS * CW, F32R), sb("weights_lo", SPLIT_SLOTS * CW, F32R)
        const = sb("constants", RESIDENT_W)
        par = sb("parameters", PARAM_W)
        rs = sb("rstd_rows", T)
        small = sb("small", 512)
        gate_hi, gate_lo = sb("gate_hi", KT * 16, F32R), sb("gate_lo", KT * 16, F32R)
        work_w = 17000
        work = sb("work", work_w)

        acc = [ctx.enter_context(nc.psum_tensor(f"acc{n}", [P, T], F32)) for n in range(4)]
        m01 = ctx.enter_context(nc.psum_tensor("m01", [P, 2, T], F32))
        m23 = ctx.enter_context(nc.psum_tensor("m23", [P, 2, T], F32))
        start_banks = [acc[2][:, :], acc[3][:, :], m23[:, 0, :], m23[:, 1, :]]
        M = [m01[:, 0, :], m01[:, 1, :], m23[:, 0, :], m23[:, 1, :]]

        c_ = lambda name: const[:, CONST[name][0]:CONST[name][1]]
        p_ = lambda name: par[:, PARAM[name][0]:PARAM[name][1]]
        pcol = lambda name, k: par[:, bass.ds(PARAM[name][0] + k, 1)]
        ident, ones = c_("ident"), c_("ones")
        level_mask = lambda s: const[:, CONST["levels"][0] + s * P:CONST["levels"][0] + (s + 1) * P]

        at = [0]

        def cols(n):
            at[0] += n
            assert at[0] <= 512
            return small[:, at[0] - n:at[0]]
        stat, powed, minus_half = cols(16), cols(16), cols(16)
        beta, decay, g_col, k_in_scale, k_out_scale, v_scale = (cols(32) for _ in range(6))
        chunk_decay = cols(64)
        t1, t2, t3, t4, t5 = (cols(32) for _ in range(5))
        pair_g, pair_beta = cols(2 * TT), cols(2 * TT)
        a_gain, b_gain, neg_lam, coef = (cols(1) for _ in range(4))
        mx, nmx, ssum, rsum, lam2 = (cols(4) for _ in range(5))

        def wk(n, start=None):
            start = wk.end if start is None else start
            wk.end = start + n
            assert wk.end <= work_w, wk.end
            return work[:, start:start + n]
        x_tok, sq_junk, norm_buf, gate_w = wk(TT * D, 0), wk(D), wk(2 * T), wk(KT * 16)
        lam_in = wk(4 * QK)
        qc, kc, vc, tanh_t = wk(2 * T, 0), wk(2 * T), wk(2 * T), wk(2 * T)
        side = wk.end
        k_in, k_out, v_in, q_dec, qk_t = (wk(2 * T) for _ in range(5))
        gam, n_t, c_t, inv, inv_t, prod = (wk(2 * T) for _ in range(6))
        v_new, state = wk(2 * HD), wk(2 * HD)
        w_t, u_tok = gam, n_t
        sq = work[:, side + 16 * T:side + 20 * T]
        qr, kr, rot, rope_tab, v_tok, prob = (wk(2 * T, side if n == 0 else None) for n in range(6))
        att, att_t, o_sb, o_sq = (wk(T) for _ in range(4))
        v_feat = wk(2 * MEM)
        kv_at = work_w - 4 * MH * MEM
        assert wk.end <= kv_at
        mk, mv = wk(2 * MH * MEM, kv_at), wk(2 * MH * MEM)
        mem_tok = work[:, kv_at:kv_at + 2 * D]
        mem_scaled = (rs, v_feat)
        Y, acc_sq, cq, cz = wk(KT * T, 0), wk(T), wk(MH * T), wk(MH * T)
        assert wk.end <= kv_at
        sqt = cq[:, 0:2 * T]
        cp, cpt = Y[:, 0:2 * T], Y[:, 2 * T:4 * T]
        zt = lambda h: Y[:, (4 + h) * T:(5 + h) * T]
        uu, cu, cv, bb = cq[:, 0:2 * T], cq[:, 2 * T:4 * T], cz[:, 0:2 * T], cz[:, 2 * T:4 * T]

        head2 = lambda t: t.rearrange("p (h n) -> p h n", h=2)
        tiles = lambda t: t.rearrange("p (t n) -> p t n", n=P)
        over_tiles = lambda t, n: t.unsqueeze(1).broadcast_to([P, n, P])
        over_row = lambda t, n, w: t.unsqueeze(2).broadcast_to([P, n, w])
        psum_tiles = lambda m: m[:, :, :].rearrange("p b (t n) -> p (b t) n", n=P)
        flat = lambda m: m[:, :, :].rearrange("p b n -> p (b n)")
        xt = lambda k: X[:, bass.ds(k * T, T)]
        yt = lambda k: Y[:, bass.ds(k * T, T)]
        mem_g = lambda H, l, g: H[:, (l * 8 + g) * T:(l * 8 + g + 1) * T]
        mem_h = lambda H, l, k: H[:, l * KT * MEM + k * MEM:l * KT * MEM + (k + 1) * MEM]
        mkt = lambda l, h: mk[:, (l * MH + h) * MEM:(l * MH + h + 1) * MEM]

        params_in, tables_in, gate_in, spilled, reloaded, out_done = (
            sem(n) for n in ("params_in", "tables_in", "gate_in", "spilled", "reloaded", "out_done"))
        x_in, mem_in = [sem(f"x_in{t}") for t in range(TT)], [sem(f"mem_in{m}") for m in range(2)]
        raw_in = [sem(f"raw_in{n}") for n in range(RAW_SLOTS)]
        hi_ready, lo_ready, chunk_used = sem("hi_ready"), sem("lo_ready"), sem("chunk_used")
        acc_free, z_tanh = sem("acc_free"), sem("z_tanh")
        const_set = sem("const_set")
        SM, SA, SV, SG = steps("start_mm"), steps("start_act"), steps("start_vec"), steps("start_pool")
        EA, EV = steps("evac_act"), steps("evac_vec")
        GM, GA, GV, GG = steps("delta_mm"), steps("delta_act"), steps("delta_vec"), steps("delta_pool")
        BM, BA, BV, BG = steps("attn_mm"), steps("attn_act"), steps("attn_vec"), steps("attn_pool")
        MM, MA, MV, MG = steps("mem_mm"), steps("mem_act"), steps("mem_vec"), steps("mem_pool")
        OA, OG = steps("outproj_act"), steps("outproj_pool")
        ZA, ZV = steps("split_act"), steps("split_vec")
        NM, NA, NV, NG = steps("norm_mm"), steps("norm_act"), steps("norm_vec"), steps("norm_pool")
        CM, CA, CV = steps("cross_mm"), steps("cross_act"), steps("cross_vec")
        VA, VV = steps("conv_act"), steps("conv_vec")
        FM, FA, FV, FG = (steps("final_" + n) for n in ("mm", "act", "vec", "pool"))

        block = ctx.enter_context(nc.Block())
        LAYERS_Q, LAYERS_O, P_Q, P_O = (C_Q0, C_Q1), (C_O0, C_O1), (P_Q0, P_Q1), (P_O0, P_O1)

        @block.sync
        def _(sp):
            sp.dma_start(const[:, :], dram["constants"][:, 0:RESIDENT_W]).then_inc(params_in, 16)
            sp.dma_start(par[:, :], dram["parameters"]).then_inc(params_in, 16)
            for t in range(TT):
                sp.dma_start(x_tok[:, t * D:(t + 1) * D], dram["x"][t * P:(t + 1) * P, :]).then_inc(x_in[t], 16)
            sp.dma_start(gate_w.rearrange("p (k n) -> p k n", n=16),
                         dram["ab_w_in"].rearrange("(k p) n -> p k n", p=P)[:, :, 4096:4096 + 16]).then_inc(gate_in, 16)
            sp.dma_start(lam_in, dram["lambda"]).then_inc(gate_in, 16)

            def load(w, col, g, kt0, n=0):
                if isinstance(n, int):
                    g, n = g + 16 * n, 0
                if g >= RAW_SLOTS:
                    sp.wait_ge(lo_ready, 16 * n + g - RAW_SLOTS + 1)
                c = g % RAW_SLOTS
                src = w.rearrange("(k p) n -> p k n", p=P)[:, kt0:kt0 + 4, bass.ds(col, 256)]
                sp.dma_start(raw[:, c * CW:(c + 1) * CW].rearrange("p (k n) -> p k n", k=4), src)\
                    .then_inc(raw_in[c], 16)

            def load_pair(w, col, g, n=0):
                for c in range(4):
                    load(w, col, g + c, 4 * c, n)

            def ab_loads(like, n=0):
                col = (AB_B + 256 * (like - 4) if like >= 4 else 256 * like) + 256 * n
                for j, sec in enumerate((3072, 0, 1024, 2048)):
                    if like == 5 and j == 3:
                        sp.wait_ge(*GA("end", 3))
                        for m in range(2):
                            sp.dma_start(mem_tok[:, m * D:(m + 1) * D], dram["mem"][m * P:(m + 1) * P, :])\
                                .then_inc(mem_in[m], 16)
                    load_pair(dram["ab_w_in"], col + sec, C_AB + 16 * like + 4 * j, n)
                    if like == 0 and j == 0:
                        for k in range(KT):
                            sp.wait_ge(*SA(f"copy{k}"))
                            sp.dma_start(dram["spill"][k], xt(k)).then_inc(spilled, 16)
            ab_loads(0)
            with sp.Fori(0, 3) as n:
                ab_loads(1, n)
            for it in range(4, AB_ITERS):
                ab_loads(it)
            for l in range(2):
                for j in range(4):
                    load_pair(dram["m_w_kv"][l], 256 * j, C_KV + 16 * l + 4 * j)
            for n in range(8):
                load_pair(dram["ab_w_out"], 256 * n, C_OUT0 + 4 * n)
                if n == 0:
                    for k in range(KT):
                        sp.wait_ge(*ZV(f"lo{k}"))
                        sp.dma_start(xt(k), dram["spill"][k]).then_inc(reloaded, 16)

            def cross_loads(l):
                for j in range(4):
                    load_pair(dram["m_w_q"][l], 256 * j, LAYERS_Q[l] + 4 * j)
                for n in range(8):
                    load(dram["m_w_o"][l], 256 * n, LAYERS_O[l] + n, 0)
            cross_loads(0)
            with sp.Fori(0, 8) as n:
                for j, sec in enumerate((0, 2, 1, 3)):
                    load_pair(dram["c_w_in"], sec * D + 256 * n, C_C + 4 * j, n)
            for n in range(8):
                load_pair(dram["c_w_out"], 256 * n, C_OUT1 + 4 * n)
            cross_loads(1)
            for n in range(16):
                kg, t = n // TT, n % TT
                sp.wait_ge(*FA(f"o{n}"))
                sp.dma_start(dram["out"][t * P:(t + 1) * P, kg * T:(kg + 1) * T], yt(n)).then_inc(out_done, 16)
            sp.wait_ge(out_done, 16 * 16)
            sp.wait_ge(spilled, 16 * KT)

        @block.scalar
        def _(act):
            is_split = set()

            def split(g, n=0):
                if isinstance(n, int):
                    g, n = g + 16 * n, 0
                    if g >= CHUNKS or g in is_split:
                        return
                    is_split.add(g)
                c, s = g % RAW_SLOTS, g % SPLIT_SLOTS
                act.wait_ge(raw_in[c], 16 * (g // RAW_SLOTS + 1) + 16 * (16 // RAW_SLOTS) * n)
                if g >= SPLIT_SLOTS:
                    act.wait_ge(chunk_used, 16 * n + g - SPLIT_SLOTS + 1)
                act.activation(w_hi[:, s * CW:(s + 1) * CW], raw[:, c * CW:(c + 1) * CW], ACT.Copy)\
                    .then_inc(hi_ready, 1)

            act.wait_ge(params_in, 32)
            for t in range(TT):
                act.wait_ge(x_in[t], 16)
                if t:
                    act.wait_ge(*SA.last())
                act.activation(sq_junk, x_tok[:, t * D:(t + 1) * D], ACT.Square,
                               accum_out=stat[:, t:t + 1]).then_inc(*SA.did(f"ss{t}"))
            split(0)
            act.wait_ge(gate_in, 32)
            act.activation(gate_hi[:, :], gate_w, ACT.Copy).then_inc(*SA.did("gate_hi"))

            def start_high(k):
                act.wait_ge(*SV(f"norm{k}"))
                act.activation(H_hi[:, k * T:(k + 1) * T], norm_buf[:, (k % 2) * T:(k % 2 + 1) * T], ACT.Copy)\
                    .then_inc(*SA.did(f"hi{k}"))
                split_ahead(split, k, C_AB)
            for k in range(KT):
                act.wait_ge(*SM(f"tr{k}"))
                act.activation(xt(k), start_banks[k % 4], ACT.Copy).then_inc(*SA.did(f"copy{k}"))
                if k:
                    start_high(k - 1)
            start_high(KT - 1)

            def gates():
                act.wait_ge(*SV("gates"))
                act.activation(t1, t1, ACT.Exp, scale=-1.0).then_inc(*SA.did("eb"))
                act.activation(t3, t2, ACT.Abs).then_inc(*SA.did())
                act.wait_ge(*SA.last())
                act.activation(t3, t3, ACT.Exp, scale=-1.0).then_inc(*SA.did("eg"))
                act.activation(p_("A_log"), p_("A_log"), ACT.Exp).then_inc(*SA.did())
                act.activation(lam2[:, 0:2], lam2[:, 0:2], ACT.Exp).then_inc(*SA.did("small_exp"))

            def decays():
                act.wait_ge(*SM("decays"))
                act.wait_ge(*SV("decay"))
                act.activation(k_in_scale, M[0][:, 0:32], ACT.Exp).then_inc(*SA.did())
                act.activation(k_out_scale, M[0][:, 32:64], ACT.Exp).then_inc(*SA.did())
                act.activation(chunk_decay, M[0][:, 64:128], ACT.Exp).then_inc(*SA.did("decays"))

            def delta(name, i):
                if name == "begin":
                    GA.round(i)
                    act.wait_ge(*EV("s11", i))
                    act.activation(sq[:, 0:2 * T], qc, ACT.Square).then_inc(*GA.did())
                    act.activation(sq[:, 2 * T:4 * T], kc, ACT.Square).then_inc(*GA.did("sq"))
                elif name == "tr":
                    act.wait_ge(*GM("tr", i))
                    for h in range(2):
                        for t in range(TT):
                            c = bass.ds((2 * i + h) * TT + t, 1)
                            o = slice(h * T + t * P, h * T + (t + 1) * P)
                            act.activation(k_in[:, o], M[h][:, t * P:(t + 1) * P], ACT.Copy, scale=k_in_scale[:, c])\
                                .then_inc(*GA.did())
                            act.activation(v_in[:, o], M[2 + h][:, t * P:(t + 1) * P], ACT.Copy, scale=v_scale[:, c])\
                                .then_inc(*GA.did("kv"))
                elif name == "dk":
                    act.wait_ge(*GV("gam", i))
                    act.activation(prod, flat(m01), ACT.Exp).then_inc(*GA.did("edec"))
                    act.activation(gam, gam, ACT.Exp).then_inc(*GA.did("gam"))
                elif name[0] == "p" and name != "p0":
                    act.wait_ge(*GM(name, i))
                    act.activation(prod, flat(m01), ACT.Copy).then_inc(*GA.did(name))
                elif name == "uw":
                    act.wait_ge(*GM("uw", i))
                    act.activation(u_tok, flat(m01), ACT.Copy).then_inc(*GA.did("u"))
                    act.activation(w_t, flat(m23), ACT.Copy).then_inc(*GA.did("w"))
                elif name == "s7":
                    act.wait_ge(*GM("s7", i))
                    act.activation(prod, flat(m23), ACT.Copy).then_inc(*GA.did())
                    act.activation(inv, flat(m23), ACT.Square).then_inc(*GA.did("o"))
                elif name == "end":
                    act.wait_ge(*GV("end", i))
                    act.activation(coef, minus_half[:, 0:1], ACT.Copy).then_inc(*GA.did("end"))

            def attn(name, i):
                if name in ("begin", "begin_k"):
                    src, tag = (kc, "rk") if name == "begin_k" else (qc, "rq")
                    if tag == "rk":
                        act.wait_ge(*BV("rq", i))
                    else:
                        BA.round(i)
                        act.wait_ge(acc_free, 2 * (P_AB + 4 * (4 + i) + 3))
                    for a in range(4):
                        b = a ^ 1
                        act.activation(rot[32 * a:32 * a + 32, :], src[32 * b:32 * b + 32, :], ACT.Copy)\
                            .then_inc(*BA.did(tag))
                elif name == "vt":
                    act.wait_ge(*BM("vt", i))
                    act.activation(v_tok, flat(m01), ACT.Copy).then_inc(*BA.did("v"))
                elif name[0] == "a":
                    h, t = int(name[1]), int(name[2])
                    act.wait_ge(*BM(name, i))
                    if t:
                        act.activation(att_t[:, 0:t * P], M[2][:, 0:t * P], ACT.Copy)\
                            .then_inc(*BA.did(f"at{h}{t - 1}"))
                    if t < TT:
                        n = (t + 1) * P
                        act.wait_ge(*BV(f"nm{h}{t}", i))
                        for m in range(2):
                            act.activation(prob[:, m * T:m * T + n], M[m][:, 0:n], ACT.Exp, bias=nmx[:, m:m + 1],
                                           scale=QK ** -0.5, accum_out=ssum[:, m:m + 1])\
                                .then_inc(*BA.did(f"p{h}{t}"))
                elif name in ("b03", "b13"):
                    act.wait_ge(*BM(name, i))
                    act.activation(o_sb, M[3], ACT.Copy).then_inc(*BA.did())
                    act.activation(o_sq, M[3], ACT.Square).then_inc(*BA.did(f"o{name[1]}"))

            def tanh_z(it, like):
                act.wait_ge(chunk_used, ab_done(P_AB + 4 * it))
                if like:
                    act.wait_ge(acc_free, 2 * (P_AB + 4 * it))
                    if like <= 4:
                        act.wait_ge(*EV("s21", it - 1))
                for n in range(2):
                    act.activation(tanh_t[:, n * T:(n + 1) * T], acc[n][:, :], ACT.Tanh, scale=0.5).then_inc(z_tanh, 1)

            def tanh_conv(it, sec, n):
                act.wait_ge(acc_free, 2 * (P_AB + 4 * it + 1 + sec) + n + 1)
                act.activation(tanh_t[:, n * T:(n + 1) * T], (qc, kc, vc)[sec][:, n * T:(n + 1) * T], ACT.Tanh,
                               scale=0.5).then_inc(*EA.did(f"t{sec}{n}"))

            def mem_squares(m):
                act.wait_ge(mem_in[m], 16)
                for h in range(2):
                    if h or m:
                        act.wait_ge(*MA.last())
                    act.activation(tanh_t, mem_tok[:, m * D + h * 2 * T:m * D + (h + 1) * 2 * T], ACT.Square,
                                   accum_out=t1[:, 2 * h + m:2 * h + m + 1]).then_inc(*MA.did("ss"))

            def mem_rows(m):
                act.wait_ge(*MG("pow"))
                o = slice(m * D, (m + 1) * D)
                act.activation(mem_tok[:, o], mem_tok[:, o], ACT.Copy, scale=t2[:, m:m + 1]).then_inc(*MA.did(f"n{m}"))

            def mem_high(l, g):
                if g == 0:
                    act.wait_ge(chunk_used, C_KV - 2 if l == 0 else C_KV)
                act.wait_ge(*MV(f"m{l}{g}"))
                act.activation(mem_g(H_hi, l, g), mem_scaled[g % 2][:, :], ACT.Copy).then_inc(*MA.did(f"hi{l}{g}"))

            def ab_round(it, like):
                reply, i = (delta, it - 1) if like <= 4 else (attn, it - 5)
                names, slots = (D_HOPS, D_SLOTS) if like <= 4 else (B_HOPS, B_SLOTS)
                if like:
                    EA.i = it - 1

                def projected(c):
                    if 1 <= like <= 4 and c < 2:
                        tanh_conv(it - 1, 2, c)
                    if c == 2:
                        EA.round(it)
                    if like == 0 and c == 5:
                        gates()
                    if c == 4:
                        tanh_z(it, like)
                    if like == 0 and c == 7:
                        decays()
                    if like < 4 and c in (8, 9):
                        tanh_conv(it, 0, c - 8)
                    if like < 4 and c in (12, 13):
                        tanh_conv(it, 1, c - 12)

                for c in range(16):
                    split(C_AB + 16 * like + c + 1, it - like)
                    if like == 6 and c in (8, 9):
                        if c == 8:
                            act.wait_ge(acc_free, 2 * (P_AB + 4 * it + 1))
                        mem_squares(c - 8)
                    if like == 7 and c in (8, 9):
                        mem_rows(c - 8)
                    if like == 0:
                        projected(c)
                        continue
                    if c == 2:
                        reply("begin", i)
                    if c == 3 and like > 4:
                        reply("begin_k", i)
                    for k in range(4):
                        for name in hops_at(names, slots, 4 * c + k, 4 * c + k + 1):
                            reply(name, i)
                        if k == PROJECTED_AFTER:
                            projected(c)
                        if like == 7 and c >= 14:
                            mem_high(0, 4 * (c - 14) + k)
                    if c == 15 and like <= 4:
                        reply("end", i)
                    if c == 15 and like == 4:
                        act.wait_ge(*GA.last())
                        act.dma_start(rope_tab, dram["constants"][:, RESIDENT_W:]).then_inc(tables_in, 16)
            ab_round(0, 0)
            with act.Fori(1, 4) as it:
                ab_round(it, 1)
            for it in range(4, AB_ITERS):
                ab_round(it, it)

            def split_input(r, src, c0, first=0, end=KT):
                if first == 0:
                    ZA.round(r)
                if end == KT:
                    split(c0 + 1)
                for k in range(first, end):
                    if k % 2 == 0:
                        if r == 1:
                            act.wait_ge(*VV("y1", k // 2))
                        elif k == KT - 2:
                            act.wait_ge(*BV("y1", 3))
                    act.wait_ge(chunk_used, c0 - 16 if r == 0 and k < 8 else c0 if r == 0 else c0 - 3 + k // 4)
                    act.activation(H_hi[:, k * T:(k + 1) * T], src(k), ACT.Copy).then_inc(*ZA.did(f"hi{k}"))

            for c in range(32):
                split(C_KV + c + 1)
                for k in range(4):
                    if 1 <= c <= 2:
                        mem_high(1, 4 * (c - 1) + k)
                if c in (0, 3):
                    attn("begin_k" if c else "begin", 3)
                for name in hops_at(B_HOPS, B_SLOTS, 2 * c, 2 * c + 2):
                    attn(name, 3)
                if c >= 24:
                    split_input(0, xt, C_OUT0, c - 24, c - 23)

            def out_square(r, n, pair):
                for j in range(2):
                    act.wait_ge(acc_free, 2 * pair + j + 1)
                    if n:
                        act.wait_ge(*OG(f"a{2 * n + j - 2}", r))
                    act.activation(sqt[:, j * T:(j + 1) * T], yt(2 * n + j), ACT.Square)\
                        .then_inc(*OA.did(f"s{2 * n + j}"))

            def out_phase(r, c0, p0, per):
                OA.round(r)
                for n in range(8):
                    for c in range(per):
                        split(c0 + per * n + c + 1)
                        if c == 0 and n:
                            out_square(r, n - 1, p0 + n - 1)
                out_square(r, 7, p0 + 7)

            def norm(r):
                NA.round(r)
                split((C_Q0, C_C, C_Q1)[r] + 1)
                gain = ("x_pre", "norm_pre", "x_pre")[r]
                layer = (0, 1, 1)[r]
                for k in range(KT):
                    act.wait_ge(*NG(f"x{k}", r))
                    act.activation(H_hi[:, k * T:(k + 1) * T], xt(k), ACT.Copy, scale=pcol(gain, layer * KT + k))\
                        .then_inc(*NA.did(f"hi{k}"))
                    act.activation(yt(k), xt(k), ACT.Square).then_inc(*NA.did(f"sq{k}"))
                    split_ahead(split, k, (C_Q0, C_C, C_Q1)[r])

            def cross(l):
                CA.round(l)

                def gate(n):
                    for h in (2 * n, 2 * n + 1):
                        act.wait_ge(acc_free, 2 * (P_Q[l] + 2 + n) + h % 2 + 1)
                        act.activation(zt(h), cz[:, h * T:(h + 1) * T], ACT.Tanh, scale=0.5).then_inc(*CA.did(f"zt{h}"))

                def outputs(n):
                    act.wait_ge(chunk_used, LAYERS_Q[l] + 13)
                    for h in (2 * n, 2 * n + 1):
                        act.wait_ge(*CV(f"y{h}", l))
                        act.activation(H_hi[:, h * T:(h + 1) * T], cq[:, h * T:(h + 1) * T], ACT.Copy)\
                            .then_inc(*CA.did(f"hi{h}"))
                for c in range(16):
                    split(LAYERS_Q[l] + c + 1)
                    for name in hops_at(C_HOPS, C_SLOTS, 4 * c, 4 * c + 4):
                        h = int(name[1])
                        if name[0] == "s":
                            act.wait_ge(*CV(f"nm{h}", l))
                            for t in range(TT):
                                act.activation(cp[:, t * MEM:(t + 1) * MEM], flat(m01)[:, t * MEM:(t + 1) * MEM],
                                               ACT.Exp, bias=nmx[:, t:t + 1], scale=P ** -0.5,
                                               accum_out=ssum[:, t:t + 1]).then_inc(*CA.did(f"p{h}"))
                        elif name[0] == "t":
                            act.wait_ge(*CM(name, l))
                            act.activation(cpt, flat(m23), ACT.Copy).then_inc(*CA.did(f"t{h}"))
                        else:
                            act.wait_ge(*CM(name, l))
                            act.activation(cq[:, h * T:(h + 1) * T], M[0], ACT.Copy, scale=0.5)\
                                .then_inc(*CA.did(f"o{h}"))
                    if c == 13:
                        gate(0)
                    if c == 15:
                        outputs(0)
                gate(1)
                outputs(1)

            split_input(0, xt, C_OUT0, 8)
            out_phase(0, C_OUT0, P_OUT0, 4)
            norm(0)
            cross(0)
            out_phase(1, C_O0, P_O0, 1)
            norm(1)

            def conv_tanh(n):
                for j in range(2):
                    act.wait_ge(acc_free, 2 * (P_C + 3) + j + 1 + 8 * n)
                    act.activation(uu[:, j * T:(j + 1) * T], bb[:, j * T:(j + 1) * T], ACT.Tanh, scale=0.5)\
                        .then_inc(*VA.did(f"z{j}"))

            def conv_group(n, first=False, last=False):
                for c in range(16):
                    split(C_C + c + 1, n)
                    if c == 0 and not first:
                        conv_tanh(n - 1)
                    if c == 1:
                        VA.round(n)
                    if last and c >= 13:
                        split_input(1, yt, C_OUT1, 4 * (c - 13), 4 * (c - 12))
            conv_group(0, first=True)
            with act.Fori(1, 7) as n:
                conv_group(n)
            conv_group(7, last=True)
            conv_tanh(7)
            split_input(1, yt, C_OUT1, 12)
            out_phase(2, C_OUT1, P_OUT1, 4)
            norm(2)
            cross(1)
            out_phase(3, C_O1, P_O1, 1)
            for n in range(16):
                act.wait_ge(*FM(f"o{n}"))
                act.activation(yt(n), acc[n % 4][:, :], ACT.Copy).then_inc(*FA.did(f"o{n}"))

        @block.tensor
        def _(pe):
            def rows(out, col, n):
                for t in range(n):
                    last = pe.matmul(out(t), col(t).broadcast_to([P, P]), ident, start=True, stop=True)
                return last

            def chunk(g, pair, kt0, last_kt, width=T, hi=None, lo=None, ready=None, between=None, n=0):
                if isinstance(n, int):
                    g, pair, n = g + 16 * n, pair + 4 * n, 0
                s = g % SPLIT_SLOTS
                hi = hi or (lambda k: H_hi[:, k * T:(k + 1) * T])
                lo = lo or (lambda k: H_lo[:, k * T:(k + 1) * T])
                pe.wait_ge(lo_ready, 16 * n + g + 1)
                if kt0 == 0 and pair >= 2:
                    pe.wait_ge(acc_free, 2 * (pair - 1) + 8 * n)
                for k in range(4):
                    kt = kt0 + k
                    if ready is not None:
                        pe.wait_ge(*ready(kt))
                    for j in range(2):
                        o = s * CW + k * 256 + j * P
                        out = acc[2 * (pair % 2) + j][:, 0:width]
                        pe.matmul(out, w_hi[:, o:o + P], hi(kt), start=kt == 0, stop=False)
                        pe.matmul(out, w_hi[:, o:o + P], lo(kt), start=False, stop=False)
                        last = pe.matmul(out, w_lo[:, o:o + P], hi(kt), start=False, stop=kt == last_kt)
                    if k == 3:
                        last.then_inc(chunk_used, 1)
                    if between is not None:
                        between(k)

            pe.wait_ge(params_in, 32)
            for t in range(TT):
                pe.wait_ge(x_in[t], 16)

            def start_transposes(k):
                if k >= 4:
                    pe.wait_ge(*SA(f"hi{k - 4}"))
                if k == 2:
                    pe.wait_ge(*SG("pow"))
                    rows(lambda t: M[1][:, t * P:(t + 1) * P], lambda t: powed[:, t:t + 1], TT)\
                        .then_inc(*SM.did("rows"))
                for t in range(TT):
                    last = pe.transpose(start_banks[k % 4][:, t * P:(t + 1) * P],
                                        x_tok[:, t * D + k * P:t * D + (k + 1) * P],
                                        ident)
                last.then_inc(*SM.did(f"tr{k}"))
            START_AHEAD = 4
            for k in range(START_AHEAD):
                start_transposes(k)

            def gates(step):
                if step == 0:
                    pe.wait_ge(*SV("gate_lo"))
                    pe.wait_ge(*SV("rs"))
                    for k in range(KT):
                        x, g = slice(k * T, (k + 1) * T), slice(k * 16, (k + 1) * 16)
                        pe.matmul(M[1][0:16, :], gate_hi[:, g], H_hi[:, x], start=k == 0, stop=False)
                        pe.matmul(M[1][0:16, :], gate_hi[:, g], H_lo[:, x], start=False, stop=False)
                        last = pe.matmul(M[1][0:16, :], gate_lo[:, g], H_hi[:, x], start=False, stop=k == KT - 1)
                    last.then_inc(*SM.did("gate_cols"))
                else:
                    pe.wait_ge(*SV("gate_cols"))
                    for t in range(TT):
                        last = pe.transpose(M[0][:, t * 16:(t + 1) * 16], norm_buf[0:16, t * P:(t + 1) * P],
                                            ident[0:16, 0:16])
                    last.then_inc(*SM.did("gates"))

            def decays():
                pe.wait_ge(*SV("g"))
                for n, name in enumerate(("cumsum", "suffix", "half0", "half1")):
                    last = pe.matmul(M[0][:, 32 * n:32 * n + 32], c_(name), g_col, start=True, stop=True)
                last.then_inc(*SM.did("decays"))

            def delta(name, i):
                ht = [(h, t) for h in range(2) for t in range(TT)]
                o = lambda h, t: slice(h * T + t * P, h * T + (t + 1) * P)
                m = lambda bank, h, t: bank[:, h, t * P:(t + 1) * P]
                if name == "ss":
                    GM.round(i)
                    pe.wait_ge(*GA("sq", i))
                    if isinstance(i, int) and i == 0:
                        pe.wait_ge(*SA("decays"))
                    for n in range(16):
                        last = pe.matmul(M[0][:, n:n + 1], sq[:, n * P:(n + 1) * P], ones, start=True, stop=True)
                elif name == "rows":
                    pe.wait_ge(*GV("pw", i))
                    for h, t in ht:
                        n = h * TT + t
                        pe.matmul(m(m01, h, t), powed[:, 8 + n:9 + n].broadcast_to([P, P]), ident, start=True, stop=True)
                        last = pe.matmul(m(m23, h, t), powed[:, n:n + 1].broadcast_to([P, P]), ident, start=True, stop=True)
                elif name == "tr":
                    pe.wait_ge(*GV("qn", i))
                    pe.wait_ge(*EV("s21", i))
                    for h, t in ht:
                        pe.transpose(m(m01, h, t), kc[:, o(h, t)], ident)
                        last = pe.transpose(m(m23, h, t), vc[:, o(h, t)], ident)
                elif name == "dk":
                    pe.wait_ge(*GA("kv", i))
                    pe.wait_ge(*GV("k_out", i))
                    for h, t in ht:
                        pe.matmul(m(m01, h, t), pair_g[:, h * TT + t:h * TT + t + 1].broadcast_to([P, P]), c_("cumsum"),
                                  start=True, stop=True)
                        last = pe.matmul(m(m23, h, t), kc[:, o(h, t)], kc[:, o(h, t)], start=True, stop=True)
                elif name == "qb":
                    pe.wait_ge(*GV("nt0", i))
                    for h, t in ht:
                        pe.matmul(m(m01, h, t), kc[:, o(h, t)], qc[:, o(h, t)], start=True, stop=True)
                        last = pe.matmul(m(m23, h, t), pair_beta[:, h * TT + t:h * TT + t + 1].broadcast_to([P, P]), ident,
                                         start=True, stop=True)
                elif name == "p0":
                    pe.wait_ge(*GG("c0", i))
                    pe.wait_ge(*GV("qk", i))
                    for h, t in ht:
                        last = pe.matmul(m(m01, h, t), c_t[:, o(h, t)], ident, start=True, stop=True)
                elif name[0] == "p":
                    pe.wait_ge(*GG("c" + name[1], i))
                    pe.wait_ge(*GV("y" + str(int(name[1]) - 1), i))
                    for h, t in ht:
                        last = pe.matmul(m(m01, h, t), c_t[:, o(h, t)], inv[:, o(h, t)], start=True, stop=True)
                elif name[0] == "y":
                    pe.wait_ge(*GA("p" + name[1], i))
                    for h, t in ht:
                        if name != "y5":
                            pe.matmul(m(m23, h, t), inv_t[:, o(h, t)], prod[:, o(h, t)], start=True, stop=True)
                        last = pe.matmul(m(m01, h, t), prod[:, o(h, t)], inv_t[:, o(h, t)], start=True, stop=True)
                elif name == "uw":
                    pe.wait_ge(*GV("y5", i))
                    for h, t in ht:
                        pe.matmul(m(m01, h, t), inv_t[:, o(h, t)], v_in[:, o(h, t)], start=True, stop=True)
                        last = pe.matmul(m(m23, h, t), k_in[:, o(h, t)], inv_t[:, o(h, t)], start=True, stop=True)
                elif name[0] == "r":
                    c = int(name[1])
                    p0 = CH * (c % 2)
                    if c == 0:
                        pe.wait_ge(*GA("w", i))
                    pe.wait_ge(*GV(f"st{c}", i))
                    for h in range(2):
                        st = state[:, h * HD:(h + 1) * HD]
                        pe.matmul(M[0][p0:p0 + CH, h * HD:(h + 1) * HD], w_t[:, h * T + c * CH:h * T + (c + 1) * CH],
                                  st, start=True, stop=True)
                        last = pe.matmul(m23[:, h, c * CH:(c + 1) * CH], st,
                                         q_dec[:, h * T + c * CH:h * T + (c + 1) * CH], start=True, stop=False)
                elif name[0] == "s":
                    c = int(name[1])
                    t, p0 = c // 2, CH * (c % 2)
                    ps = slice(p0, p0 + CH)
                    pe.wait_ge(*GV(f"vn{c}", i))
                    for h in range(2):
                        vn = v_new[ps, h * HD:(h + 1) * HD]
                        q0 = h * T + t * P + p0
                        last = pe.matmul(m23[:, h, c * CH:(c + 1) * CH], vn, qk_t[ps, q0:q0 + CH],
                                         start=False, stop=True)
                        if c < T // CH - 1:
                            last = pe.matmul(M[1][:, h * HD:(h + 1) * HD], k_out[ps, o(h, t)], vn, start=True, stop=True)
                elif name == "fs":
                    pe.wait_ge(*GA("o", i))
                    for n in range(8):
                        last = pe.matmul(M[0][:, n:n + 1], inv[:, n * P:(n + 1) * P], ones, start=True, stop=True)
                elif name == "fb":
                    pe.wait_ge(*GG("fpow", i))
                    for h, t in ht:
                        n = h * TT + t
                        last = pe.matmul(m(m01, h, t), powed[:, n:n + 1].broadcast_to([P, P]), ident, start=True, stop=True)
                last.then_inc(*GM.did(name))

            def attn(name, i):
                if name == "vt":
                    BM.round(i)
                    if i == 0:
                        pe.wait_ge(*GA("end", 3))
                    else:
                        pe.wait_ge(*BV("y1", i - 1))
                    pe.wait_ge(acc_free, 2 * (P_AB + 4 * (4 + i) + 4))
                    for n in range(8):
                        last = pe.transpose(m01[:, n // TT, (n % TT) * P:(n % TT + 1) * P], vc[:, n * P:(n + 1) * P], ident)
                elif name[0] == "a":
                    h, t = int(name[1]), int(name[2])
                    if t:
                        pe.wait_ge(*BV(f"att{h}{t - 1}", i))
                        for j in range(t):
                            last = pe.transpose(M[2][:, j * P:(j + 1) * P], att[:, j * P:(j + 1) * P], ident)
                    elif h == 0:
                        pe.wait_ge(*BA("v", i))
                        pe.wait_ge(*BV("rk", i))
                    else:
                        pe.wait_ge(*BV("y0", i))
                    if t < TT:
                        if t:
                            pe.wait_ge(*BA(f"p{h}{t - 1}", i))
                        for mp in range(2):
                            r = slice(QK * mp, QK * mp + QK)
                            last = pe.matmul(M[mp][:, 0:(t + 1) * P], qr[r, h * T + t * P:h * T + (t + 1) * P],
                                             kr[r, h * T:h * T + (t + 1) * P], start=True, stop=True)
                elif name[0] == "b":
                    h, t = int(name[1]), int(name[2])
                    pe.wait_ge(*BA(f"at{h}{t}", i))
                    if h and t == 0:
                        pe.wait_ge(*BA("o0", i))
                    for j in range(t + 1):
                        last = pe.matmul(M[3][:, t * P:(t + 1) * P], v_tok[:, h * T + j * P:h * T + (j + 1) * P],
                                         att_t[:, j * P:(j + 1) * P], start=j == 0, stop=j == t)
                elif name[:2] == "fs":
                    pe.wait_ge(*BA("o" + name[2], i))
                    for t in range(TT):
                        last = pe.matmul(M[0][:, t:t + 1], o_sq[:, t * P:(t + 1) * P], ones, start=True, stop=True)
                else:
                    pe.wait_ge(*BG("pow" + name[2], i))
                    last = rows(lambda t: M[0][:, t * P:(t + 1) * P], lambda t: powed[:, t:t + 1], TT)
                last.then_inc(*BM.did(name))

            def mem_transposes(l, g):
                if g == 0:
                    pe.wait_ge(*MA("n1"))
                    pe.wait_ge(acc_free, 2 * (P_KV - 1 + l))
                if g >= 2:
                    pe.wait_ge(*MV(f"m{l}{g - 2}"))
                for n in range(4):
                    k, m = 2 * g + n // 2, n % 2
                    last = pe.transpose(acc[2 * l + g % 2][:, n * P:(n + 1) * P],
                                        mem_tok[:, m * D + k * P:m * D + (k + 1) * P], ident)
                last.then_inc(*MM.did(f"t{l}{g}"))

            def ab_round(it, like):
                hop, i = (delta, it - 1) if like <= 4 else (attn, it - 5)
                names, slots = (D_HOPS, D_SLOTS) if like <= 4 else (B_HOPS, B_SLOTS)
                for c in range(16):
                    def between(k):
                        if like == 0 and 4 * c + k + START_AHEAD < KT:
                            start_transposes(4 * c + k + START_AHEAD)
                        if like:
                            for name in hops_at(names, slots, 4 * c + k, 4 * c + k + 1):
                                hop(name, i)
                        if like == 7 and c >= 14:
                            mem_transposes(0, 4 * (c - 14) + k)
                    if like == 0 and c == 4:
                        pe.wait_ge(*SA("hi15"))
                    if like == 0 and c in (4, 5):
                        gates(c - 4)
                    if like == 0 and c == 7:
                        decays()
                    chunk(C_AB + 16 * like + c, P_AB + 4 * like + c // 4, 4 * (c % 4), KT - 1, between=between,
                          ready=(lambda kt: SV(f"lo{kt}")) if like == 0 and c < 4 else None, n=it - like)
            ab_round(0, 0)
            with pe.Fori(1, 4) as it:
                ab_round(it, 1)
            for it in range(4, AB_ITERS):
                ab_round(it, it)

            def value_transposes(l, j, pair):
                pe.wait_ge(*MV(f"vf{l}{j}"))
                for n in range(4):
                    last = pe.transpose(acc[2 * (pair % 2)][:, n * P:(n + 1) * P], v_feat[:, n * P:(n + 1) * P], ident)
                last.then_inc(*MM.did(f"v{l}{j}"))

            for c in range(32):
                l, q = c // 16, c // 4 - 1

                def between(k):
                    if 1 <= c <= 2:
                        mem_transposes(1, 4 * (c - 1) + k)
                    if k % 2:
                        for name in hops_at(B_HOPS, B_SLOTS, 2 * c + k // 2, 2 * c + k // 2 + 1):
                            attn(name, 3)
                if q >= 0 and c % 4 == 1 and q % 4 >= 2:
                    value_transposes(q // 4, q % 4, P_KV + q)
                if c % 16 == 0 or c == 4:
                    pe.wait_ge(*MV(f"m{int(c > 0)}7"))
                chunk(C_KV + c, P_KV + c // 4, 4 * (c % 4), KT - 1, width=MEM, between=between,
                      ready=(lambda kt: MV(f"lo{l}{kt // 2}")) if c % 16 < 4 else None,
                      hi=lambda k: mem_h(H_hi, l, k), lo=lambda k: mem_h(H_lo, l, k))
            value_transposes(1, 3, P_KV + 7)

            def out_phase(c0, p0, per, ready):
                for n in range(8):
                    for c in range(per):
                        chunk(c0 + per * n + c, p0 + n, 4 * c, 4 * per - 1, ready=ready if n == 0 else None)

            def norm(r):
                NM.round(r)
                pe.wait_ge(*OG("a13", r))
                pe.wait_ge(*OA("s15", r))
                for t in range(TT):
                    for n, part in enumerate((acc_sq, sqt[:, 0:T], sqt[:, T:2 * T])):
                        last = pe.matmul(M[0][:, t:t + 1], part[:, t * P:(t + 1) * P], ones, start=n == 0, stop=n == 2)
                last.then_inc(*NM.did("ss"))
                pe.wait_ge(*NG("pow", r))
                rows(lambda t: M[1][:, t * P:(t + 1) * P], lambda t: powed[:, t:t + 1], TT).then_inc(*NM.did("rows"))

            def next_rms(r, c, k):
                if (c, k) == (6, 1):
                    pe.wait_ge(*NV("sum", r))
                    for t in range(TT):
                        last = pe.matmul(M[0][:, t:t + 1], acc_sq[:, t * P:(t + 1) * P], ones, start=True, stop=True)
                    last.then_inc(*NM.did("ss2"))
                if (c, k) == (7, 1):
                    pe.wait_ge(*NG("pow2", r))
                    rows(lambda t: M[1][:, t * P:(t + 1) * P], lambda t: powed[:, t:t + 1], TT)\
                        .then_inc(*NM.did("rows2"))

            def cross(l, r):
                CM.round(l)

                def hop(name):
                    h = int(name[1])
                    if name[0] == "s":
                        pe.wait_ge(acc_free, 2 * (P_Q[l] + h // 2) + h % 2 + 1)
                        pe.wait_ge(*(NV("rs", r) if h == 0 else CA(f"o{h - 1}", l)))
                        for t in range(TT):
                            last = pe.matmul(flat(m01)[:, t * MEM:(t + 1) * MEM], cq[:, h * T + t * P:h * T + (t + 1) * P],
                                             mkt(l, h), start=True, stop=True)
                    elif name[0] == "t":
                        pe.wait_ge(*CV(f"p{h}", l))
                        for t in range(TT):
                            for m in range(2):
                                last = pe.transpose(m23[:, m, t * P:(t + 1) * P],
                                                    cp[:, t * MEM + m * P:t * MEM + (m + 1) * P], ident)
                    else:
                        pe.wait_ge(*CA(f"t{h}", l))
                        for m in range(2):
                            v0 = (l * 2 + m) * MH * HD + h * HD
                            last = pe.matmul(M[0], mv[:, v0:v0 + HD], cpt[:, m * T:(m + 1) * T], start=m == 0, stop=m == 1)
                    last.then_inc(*CM.did(name))
                for c in range(16):
                    def between(k):
                        next_rms(r, c, k)
                        for name in hops_at(C_HOPS, C_SLOTS, 4 * c + k, 4 * c + k + 1):
                            hop(name)
                    chunk(LAYERS_Q[l] + c, P_Q[l] + c // 4, 4 * (c % 4), KT - 1, between=between,
                          ready=(lambda kt: NV(f"lo{kt}", r)) if c < 4 else None)
                out_phase(LAYERS_O[l], P_O[l], 1, lambda kt: CV(f"lo{kt}", l))

            out_phase(C_OUT0, P_OUT0, 4, lambda kt: ZV(f"lo{kt}", 0))
            norm(0)
            cross(0, 0)
            norm(1)

            def conv_group(n, first=False):
                for c in range(16):
                    chunk(C_C + c, P_C + c // 4, 4 * (c % 4), KT - 1, n=n,
                          between=(lambda k: next_rms(1, c, k)) if first else None,
                          ready=(lambda kt: NV(f"lo{kt}", 1)) if first and c < 4 else None)
            conv_group(0, first=True)
            with pe.Fori(1, 8) as n:
                conv_group(n)
            out_phase(C_OUT1, P_OUT1, 4, lambda kt: ZV(f"lo{kt}", 1))
            norm(2)
            cross(1, 2)
            norm(3)
            for n in range(16):
                kg, t = n // TT, n % TT
                pe.wait_ge(*FG(f"x{max(k for k in range(4 * kg + 4) if k not in VECTOR_ADDS)}"))
                pe.wait_ge(*FV(f"x{max(k for k in range(4 * kg + 4) if k in VECTOR_ADDS)}"))
                if n >= 4:
                    pe.wait_ge(*FA(f"o{n - 4}"))
                else:
                    pe.wait_ge(acc_free, 2 * (P_O1 + 8))
                for j in range(4):
                    last = pe.transpose(acc[n % 4][:, j * P:(j + 1) * P],
                                        X[:, (4 * kg + j) * T + t * P:(4 * kg + j) * T + (t + 1) * P], ident)
                last.then_inc(*FM.did(f"o{n}"))

        @block.vector
        def _(dve):
            TTO, STT, TS = dve.tensor_tensor, dve.scalar_tensor_tensor, dve.tensor_scalar

            is_split = set()

            def split(g, n=0):
                if isinstance(n, int):
                    g, n = g + 16 * n, 0
                    if g >= CHUNKS or g in is_split:
                        return
                    is_split.add(g)
                c, s = g % RAW_SLOTS, g % SPLIT_SLOTS
                dve.wait_ge(hi_ready, 16 * n + g + 1)
                TTO(w_lo[:, s * CW:(s + 1) * CW], raw[:, c * CW:(c + 1) * CW],
                    w_hi[:, s * CW:(s + 1) * CW].bitcast(F32), ALU.subtract).then_inc(lo_ready, 1)

            def bank(pair, n, width=T):
                return acc[2 * (pair % 2) + n][:, 0:width]

            dve.wait_ge(params_in, 32)
            dve.wait_ge(gate_in, 32)
            lam4 = lam_in.rearrange("p (a b n) -> p a b n", a=2, b=2)
            TTO(norm_buf[:, 0:2 * QK].rearrange("p (a n) -> p a n", a=2), lam4[:, :, 0, :], lam4[:, :, 1, :], ALU.mult)\
                .then_inc(*SV.did())
            dve.wait_ge(*SV.last())
            dve.reduce_sum(lam2[:, 0:2], norm_buf[:, 0:2 * QK].rearrange("p (a n) -> p a n", a=2), axis=AX.X)\
                .then_inc(*SV.did("lamsum"))
            dve.wait_ge(*SA("ss3"))
            TS(stat[:, 0:4], stat[:, 0:4], 1.0 / D, EPS, ALU.mult, ALU.add).then_inc(*SV.did("stat"))
            split(0)
            dve.wait_ge(*SA("gate_hi"))
            TTO(gate_lo[:, :], gate_w, gate_hi[:, :].bitcast(F32), ALU.subtract).then_inc(*SV.did("gate_lo"))
            dve.wait_ge(*SM("rows"))
            dve.tensor_copy(rs[:, :], M[1]).then_inc(*SV.did("rs"))

            def start_low(k):
                dve.wait_ge(*SA(f"hi{k}"))
                TTO(H_lo[:, k * T:(k + 1) * T], norm_buf[:, (k % 2) * T:(k % 2 + 1) * T],
                    H_hi[:, k * T:(k + 1) * T].bitcast(F32), ALU.subtract).then_inc(*SV.did(f"lo{k}"))
            for k in range(KT):
                dve.wait_ge(*SA(f"copy{k}"))
                dve.wait_ge(*SV.last())
                STT(out=norm_buf[:, (k % 2) * T:(k % 2 + 1) * T], in0=start_banks[k % 4], scalar=pcol("norm_pre", k),
                    in1=rs[:, :], op0=ALU.mult, op1=ALU.mult).then_inc(*SV.did(f"norm{k}"))
                if k:
                    start_low(k - 1)
                    split_ahead(split, k - 1, C_AB)
            start_low(KT - 1)

            def gate_columns():
                dve.wait_ge(*SM("gate_cols"))
                dve.tensor_copy(norm_buf[0:16, 0:T], M[1][0:16, :]).then_inc(*SV.did("gate_cols"))

            def gates_in():
                dve.wait_ge(*SM("gates"))
                g16 = M[0][:, 0:TT * 16].rearrange("p (t n) -> p n t", n=16)
                v = lambda t: t.rearrange("p (h t) -> p h t", t=TT)
                dve.tensor_copy(v(t1), g16[:, 0:HEADS, :]).then_inc(*SV.did())
                TTO(v(t2), g16[:, HEADS:2 * HEADS, :], over_row(p_("dt_bias"), HEADS, TT), ALU.add)\
                    .then_inc(*SV.did("gates"))

            def gates_out():
                dve.wait_ge(*SA("small_exp"))

                def then(ins, name=None):
                    ins.then_inc(*SV.did(name))
                    dve.wait_ge(*SV.last())
                then(STT(out=neg_lam, in0=lam2[:, 1:2], scalar=LAM_INIT, in1=lam2[:, 0:1], op0=ALU.subtract,
                         op1=ALU.subtract))
                then(TS(a_gain, p_("a_norm"), 0.5, None, ALU.mult))
                then(TS(b_gain, p_("b_norm"), 0.5 * (1.0 - LAM_INIT), None, ALU.mult))
                then(TS(t1, t1, 1.0, None, ALU.add))
                then(dve.reciprocal(beta, t1))
                then(TS(v_scale, beta, 0.5, None, ALU.mult))
                then(TS(t4, t3, 2.0, None, ALU.add))
                then(dve.reciprocal(t4, t4))
                then(TTO(t4, t3, t4, ALU.mult))
                then(TTO(t5, t4, t4, ALU.mult))
                then(TS(t3, t5, 1.0 / 15, None, ALU.mult))
                for n in (13, 11, 9, 7, 5, 3):
                    then(STT(out=t3, in0=t3, scalar=1.0 / n, in1=t5, op0=ALU.add, op1=ALU.mult))
                then(STT(out=t3, in0=t3, scalar=1.0, in1=t4, op0=ALU.add, op1=ALU.mult))
                then(TS(t2, t2, 0.0, None, ALU.max))
                then(STT(out=t2, in0=t3, scalar=2.0, in1=t2, op0=ALU.mult, op1=ALU.add))
                v = lambda t: t.rearrange("p (h t) -> p h t", t=TT)
                then(STT(out=v(g_col), in0=v(t2), scalar=-1.0, in1=over_row(p_("A_log"), HEADS, TT), op0=ALU.mult,
                         op1=ALU.mult), "g")

            def decays():
                dve.wait_ge(*SM("decays"))
                dve.tensor_copy(decay, M[0][:, 0:32]).then_inc(*SV.did("decay"))
                dve.wait_ge(*SA("decays"))
                TTO(k_in_scale, k_in_scale, beta, ALU.mult).then_inc(*SV.did("kin"))

            def delta(name, i):
                def then(ins, tag=None):
                    ins.then_inc(*GV.did(tag))
                    dve.wait_ge(*GV.last())
                hc = bass.ds(2 * i * TT, 2 * TT)
                if name == "ss":
                    GV.round(i)
                    dve.tensor_copy(pair_g, g_col[:, hc]).then_inc(*GV.did())
                    dve.tensor_copy(pair_beta, beta[:, hc]).then_inc(*GV.did())
                    dve.wait_ge(*GM("ss", i))
                    TS(stat, M[0][:, 0:16], 0.25, EPS, ALU.mult, ALU.add).then_inc(*GV.did("stat"))
                    dve.wait_ge(*GG("pow", i))
                    TS(powed[:, 0:8], powed[:, 0:8], 0.5 * HD ** -0.5, None, ALU.mult).then_inc(*GV.did())
                    TS(powed[:, 8:16], powed[:, 8:16], 0.5, None, ALU.mult).then_inc(*GV.did("pw"))
                elif name == "rows":
                    dve.wait_ge(*GM("rows", i))
                    TTO(kc, kc, flat(m01), ALU.mult).then_inc(*GV.did())
                    TTO(qc, qc, flat(m23), ALU.mult).then_inc(*GV.did("qn"))
                elif name == "tr":
                    dve.wait_ge(*GA("kv", i))
                    TTO(tiles(k_out), psum_tiles(m01), over_row(k_out_scale[:, hc], 8, P), ALU.mult)\
                        .then_inc(*GV.did("k_out"))
                elif name == "dk":
                    dve.wait_ge(*GM("dk", i))
                    then(TTO(tiles(gam), psum_tiles(m01), over_row(decay[:, hc], 8, P), ALU.subtract))
                    then(TTO(tiles(gam), tiles(gam), over_tiles(c_("causal"), 8), ALU.add), "gam")
                    dve.wait_ge(*GA("edec", i))
                    TTO(q_dec, qc, prod, ALU.mult).then_inc(*GV.did("qd"))
                    dve.wait_ge(*GA("gam", i))
                    then(TTO(n_t, flat(m23), gam, ALU.mult), "nt0")
                elif name == "qb":
                    dve.wait_ge(*GM("qb", i))
                    TTO(n_t, flat(m23), n_t, ALU.mult).then_inc(*GV.did("nt"))
                    TTO(qk_t, flat(m01), gam, ALU.mult).then_inc(*GV.did("qk"))
                elif name == "p0":
                    dve.wait_ge(*GM("p0", i))
                    TTO(tiles(inv), over_tiles(ident, 8), psum_tiles(m01), ALU.subtract).then_inc(*GV.did())
                    TTO(tiles(inv_t), over_tiles(ident, 8), tiles(c_t), ALU.subtract).then_inc(*GV.did("y0"))
                elif name[0] == "y":
                    dve.wait_ge(*GM(name, i))
                    if name != "y5":
                        dve.wait_ge(*GV.last())
                        TTO(inv, inv, flat(m23), ALU.subtract).then_inc(*GV.did())
                    TTO(inv_t, inv_t, flat(m01), ALU.subtract).then_inc(*GV.did(name))
                elif name == "uw":
                    dve.memset(state, 0.0).then_inc(*GV.did("st0"))
                elif name[0] == "r":
                    c = int(name[1])
                    t, p0 = c // 2, CH * (c % 2)
                    ps = slice(p0, p0 + CH)
                    dve.wait_ge(*GM(name, i))
                    TTO(head2(v_new[ps, :]), head2(u_tok[ps, :])[:, :, t * P:(t + 1) * P],
                        head2(M[0][ps, 0:2 * HD]), ALU.subtract).then_inc(*GV.did(f"vn{c}"))
                elif name[0] == "s" and name != "s7":
                    c = int(name[1])
                    t, half = c // 2, c % 2
                    dve.wait_ge(*GM(name, i))
                    for h in range(2):
                        o = slice(h * HD, (h + 1) * HD)
                        STT(out=state[:, o], in0=state[:, o], scalar=chunk_decay[:, bass.ds(half * 32 + (2 * i + h) * TT + t, 1)],
                            in1=M[1][:, o], op0=ALU.mult, op1=ALU.add).then_inc(*GV.did(f"st{c + 1}"))
                elif name == "fs":
                    dve.wait_ge(*GM("fs", i))
                    TS(stat[:, 0:8], M[0][:, 0:8], 1.0 / HD, EPS, ALU.mult, ALU.add).then_inc(*GV.did("fstat"))
                elif name == "fb":
                    dve.wait_ge(*GM("fb", i))
                    then(STT(out=prod, in0=prod, scalar=a_gain, in1=flat(m01), op0=ALU.mult, op1=ALU.mult))
                    y = X[:, bass.ds(2 * i * T, 2 * T)]
                    TTO(y, y, prod, ALU.mult).then_inc(*GV.did("end"))

            def attn(name, i):
                def then(ins, tag=None):
                    ins.then_inc(*BV.did(tag))
                    dve.wait_ge(*BV.last())
                if name in ("begin", "begin_k"):
                    dst, tag = (kr, "k") if name == "begin_k" else (qr, "q")
                    if tag == "q":
                        BV.round(i)
                        dve.wait_ge(tables_in, 16)
                    sin = rope_tab[:, T:2 * T].unsqueeze(1).broadcast_to([P, 2, T])
                    dve.wait_ge(*BA("r" + tag, i))
                    then(TTO(head2(rot), head2(rot), sin, ALU.mult))
                    dve.wait_ge(*BG("cos_" + tag, i))
                    TTO(dst, dst, rot, ALU.add).then_inc(*BV.did("r" + tag))
                elif name[0] == "a" and name[2] != "4":
                    h, t = int(name[1]), int(name[2])
                    n = (t + 1) * P
                    dve.wait_ge(*BM(name, i))
                    then(dve.memset(m01[0:CH, :, n - CH:n], NEG))
                    then(dve.reduce_max(mx[:, 0:2], m01[:, :, 0:n], axis=AX.X))
                    TS(nmx[:, 0:2], mx[:, 0:2], -QK ** -0.5, None, ALU.mult).then_inc(*BV.did(f"nm{h}{t}"))
                    dve.wait_ge(*BA(f"p{h}{t}", i))
                    then(dve.reciprocal(rsum[:, 0:2], ssum[:, 0:2]))
                    TTO(coef, rsum[:, 1:2], neg_lam, ALU.mult).then_inc(*BV.did())
                    then(TS(att[:, 0:n], prob[:, 0:n], rsum[:, 0:1], None, ALU.mult))
                    STT(out=att[:, 0:n], in0=prob[:, T:T + n], scalar=coef, in1=att[:, 0:n], op0=ALU.mult,
                        op1=ALU.add).then_inc(*BV.did(f"att{h}{t}"))
                elif name[:2] == "fs":
                    dve.wait_ge(*BM(name, i))
                    TS(stat[:, 0:4], M[0][:, 0:4], 1.0 / HD, EPS, ALU.mult, ALU.add).then_inc(*BV.did("stat" + name[2]))
                elif name[:2] == "fb":
                    h = int(name[2])
                    dve.wait_ge(*BM(name, i))
                    then(STT(out=o_sb, in0=o_sb, scalar=b_gain, in1=M[0], op0=ALU.mult, op1=ALU.mult))
                    y = xt(HEADS + 2 * i + h)
                    TTO(y, y, o_sb, ALU.mult).then_inc(*BV.did(f"y{h}"))

            def convolve(it, sec, n):
                pair = P_AB + 4 * it + 1 + sec
                src, dst = bank(1 + sec, n), (qc, kc, vc)[sec][:, n * T:(n + 1) * T]
                tap = lambda k: pcol("a_conv", (8 * sec + 2 * it + n) * 4 + k)
                dve.wait_ge(chunk_used, ab_done(pair))
                TS(dst, src, tap(3), None, ALU.mult).then_inc(*EV.did())
                for d in (1, 2, 3):
                    dve.wait_ge(*EV.last())
                    ins = STT(out=dst[:, d:T], in0=src[:, 0:T - d], scalar=tap(3 - d), in1=dst[:, d:T],
                              op0=ALU.mult, op1=ALU.add)
                    if d < 3:
                        ins.then_inc(*EV.did())
                    else:
                        ins.then_inc(acc_free, 1)

            def gate(it, sec, n):
                dst, o = (qc, kc, vc)[sec], slice(n * T, (n + 1) * T)
                dve.wait_ge(*EA(f"t{sec}{n}", it))
                STT(out=dst[:, o], in0=tanh_t[:, o], scalar=1.0, in1=dst[:, o], op0=ALU.add, op1=ALU.mult)\
                    .then_inc(*EV.did(f"s{sec}{n}"))

            def keep(it, sec, n):
                pair = P_AB + 4 * it + 1 + sec
                dve.wait_ge(chunk_used, ab_done(pair))
                dve.tensor_copy((qc, kc, vc)[sec][:, n * T:(n + 1) * T], bank(1 + sec, n)).then_inc(acc_free, 1)

            def gate_z(it, like):
                if like == 0:
                    dve.wait_ge(spilled, 16 * KT)
                for n in range(2):
                    dve.wait_ge(z_tanh, 2 * it + n + 1)
                    head = HEADS + 2 * (it - 4) + n if like >= 4 else 2 * it + n
                    STT(out=xt(head), in0=tanh_t[:, n * T:(n + 1) * T], scalar=1.0, in1=bank(0, n), op0=ALU.add,
                        op1=ALU.mult).then_inc(acc_free, 1)

            def evacuate(it, like, sec, c):
                if like < 4:
                    if c:
                        gate(it, sec, c - 1)
                    if c < 2:
                        convolve(it, sec, c)
                elif c < 2:
                    keep(it, sec, c)

            def mem_stat():
                dve.wait_ge(*MA("ss"))
                TTO(t1[:, 4:6], t1[:, 0:2], t1[:, 2:4], ALU.add).then_inc(*MV.did())
                dve.wait_ge(*MV.last())
                TS(t1[:, 6:8], t1[:, 4:6], 1.0 / D, EPS, ALU.mult, ALU.add).then_inc(*MV.did("stat"))

            def mem_low(l, g):
                def low(g):
                    dve.wait_ge(*MA(f"hi{l}{g}"))
                    TTO(mem_g(H_lo, l, g), mem_scaled[g % 2][:, :], mem_g(H_hi, l, g).bitcast(F32), ALU.subtract)\
                        .then_inc(*MV.did(f"lo{l}{g}"))
                dve.wait_ge(*MM(f"t{l}{g}"))
                dve.wait_ge(*MV.last())
                gain = p_("mem_norm")[:, l * KT + 2 * g:l * KT + 2 * g + 2]
                rows_of = lambda t: t.rearrange("p (k n) -> p k n", n=MEM)
                TTO(rows_of(mem_scaled[g % 2][:, :]), rows_of(acc[2 * l + g % 2][:, :]), over_row(gain, 2, MEM), ALU.mult)\
                    .then_inc(*MV.did(f"m{l}{g}"))
                if g:
                    low(g - 1)
                if g == 7:
                    low(g)

            def ab_round(it, like):
                reply, i = (delta, it - 1) if like <= 4 else (attn, it - 5)
                names, slots = (D_HOPS, D_SLOTS) if like <= 4 else (B_HOPS, B_SLOTS)
                if like:
                    EV.i = it - 1

                def projected(c):
                    if like and c < 3:
                        evacuate(it - 1, like - 1, 2, c)
                    if c == 2:
                        EV.round(it)
                    if like == 0 and c == 4:
                        gate_columns()
                    if c == 4:
                        gate_z(it, like)
                    if like == 0 and c == 5:
                        gates_in()
                        gates_out()
                    if like == 0 and c == 7:
                        decays()
                    for sec, at_ in ((0, 8), (1, 12)):
                        if at_ <= c < at_ + 3:
                            evacuate(it, like, sec, c - at_)

                for c in range(16):
                    split(C_AB + 16 * like + c + 1, it - like)
                    if like == 6 and c == 12:
                        mem_stat()
                    if like == 0:
                        projected(c)
                        continue
                    if c == 2:
                        reply("begin", i)
                    if c == 3 and like > 4:
                        reply("begin_k", i)
                    for k in range(4):
                        for name in hops_at(names, slots, 4 * c + k, 4 * c + k + 1):
                            reply(name, i)
                        if k == PROJECTED_AFTER:
                            projected(c)
                        if like == 7 and c >= 14:
                            mem_low(0, 4 * (c - 14) + k)
            ab_round(0, 0)
            with dve.Fori(1, 4) as it:
                ab_round(it, 1)
            for it in range(4, AB_ITERS):
                ab_round(it, it)

            def take_kv(q, c):
                l, j, pair = q // 4, q % 4, P_KV + q
                if c == 0:
                    dve.wait_ge(chunk_used, done_at(pair))
                    for n in range(2):
                        if j < 2:
                            dve.tensor_copy(mkt(l, 2 * j + n), bank(pair, n, MEM)).then_inc(acc_free, 1)
                        else:
                            dve.tensor_copy(v_feat[:, n * MEM:(n + 1) * MEM], bank(pair, n, MEM))\
                                .then_inc(*MV.did(f"vf{l}{j}"))
                elif c == 2 and j >= 2:
                    dve.wait_ge(*MM(f"v{l}{j}"))
                    for n in range(2):
                        h = 2 * (j - 2) + n
                        dst = mv[:, l * 2 * MH * HD:(l + 1) * 2 * MH * HD].rearrange("p (m h n) -> p m h n", m=2, h=MH)
                        dve.tensor_copy(dst[:, :, h, :], bank(pair, 0)[:, n * MEM:(n + 1) * MEM].rearrange(
                            "p (m n) -> p m n", m=2)).then_inc(acc_free, 1)
            def split_input(r, src, c0, first=0, end=KT):
                if first == 0:
                    ZV.round(r)
                if end == KT:
                    split(c0 + 1)
                for k in range(first, end):
                    dve.wait_ge(*ZA(f"hi{k}", r))
                    TTO(H_lo[:, k * T:(k + 1) * T], src(k), H_hi[:, k * T:(k + 1) * T].bitcast(F32), ALU.subtract)\
                        .then_inc(*ZV.did(f"lo{k}"))

            for c in range(32):
                split(C_KV + c + 1)
                if c == 0:
                    for n in range(2):
                        keep(7, 2, n)
                if 1 <= c <= 2:
                    for k in range(4):
                        mem_low(1, 4 * (c - 1) + k)
                if c in (0, 3):
                    attn("begin_k" if c else "begin", 3)
                if c >= 4:
                    take_kv(c // 4 - 1, c % 4)
                for name in hops_at(B_HOPS, B_SLOTS, 2 * c, 2 * c + 2):
                    attn(name, 3)
                if c >= 24:
                    split_input(0, xt, C_OUT0, c - 24, c - 23)
            take_kv(7, 0)
            take_kv(7, 2)

            def out_phase(c0, p0, per):
                def take(n):
                    dve.wait_ge(chunk_used, done_at(p0 + n))
                    for j in range(2):
                        dve.tensor_copy(yt(2 * n + j), bank(p0 + n, j)).then_inc(acc_free, 1)
                for n in range(8):
                    for c in range(per):
                        split(c0 + per * n + c + 1)
                        if c == 0 and n:
                            take(n - 1)
                take(7)

            def norm(r):
                NV.round(r)
                dve.wait_ge(*NM("ss", r))
                TS(stat[:, 0:4], M[0][:, 0:4], 1.0 / D, EPS, ALU.mult, ALU.add).then_inc(*NV.did("stat"))
                if r < 3:
                    split((C_Q0, C_C, C_Q1)[r] + 1)
                dve.wait_ge(*NM("rows", r))
                post = ("norm_post", "x_post", "norm_post", "x_post")[r]
                pre = ("x_pre", "norm_pre", "x_pre", None)[r]
                layer, next_layer = r // 2, (0, 1, 1, 1)[r]

                def low(k):
                    dve.wait_ge(*NA(f"hi{k}", r))
                    STT(out=H_lo[:, k * T:(k + 1) * T], in0=xt(k), scalar=pcol(pre, next_layer * KT + k),
                        in1=H_hi[:, k * T:(k + 1) * T].bitcast(F32), op0=ALU.mult, op1=ALU.subtract)\
                        .then_inc(*NV.did(f"lo{k}"))
                for k in range(KT):
                    if k == 0:
                        dve.wait_ge(acc_free, 2 * (P_OUT0 + 8, P_O0 + 8, P_OUT1 + 8, P_O1 + 8)[r])
                    STT(out=yt(k), in0=yt(k), scalar=pcol(post, layer * KT + k), in1=M[1], op0=ALU.mult, op1=ALU.mult)\
                        .then_inc(*(NV if r < 3 else FV).did(f"y{k}"))
                    if r == 3 and k in VECTOR_ADDS:
                        dve.wait_ge(*FV.last())
                        TTO(xt(k), xt(k), yt(k), ALU.add).then_inc(*FV.did(f"x{k}"))
                    if k >= 2 and pre:
                        low(k - 2)
                        if k > 2:
                            split_ahead(split, k, (C_Q0, C_C, C_Q1)[r])
                if pre:
                    low(KT - 2)
                    low(KT - 1)
                    dve.wait_ge(*NA("sq15", r))

            def sum_squares(r, c):
                for t in {3: (0, 1), 4: (2,), 5: (3,)}.get(c, ()):
                    o = slice(t * P, (t + 1) * P)
                    dve.reduce_sum(acc_sq[:, o], Y[:, :].rearrange("p (k t) -> p t k", k=KT)[:, o, :], axis=AX.X)\
                        .then_inc(*NV.did("sum"))
                if c == 6:
                    dve.wait_ge(*NM("ss2", r))
                    TS(stat[:, 0:4], M[0][:, 0:4], 1.0 / D, EPS, ALU.mult, ALU.add).then_inc(*NV.did("stat2"))
                elif c == 7:
                    dve.wait_ge(*NM("rows2", r))
                    dve.tensor_copy(rs[:, :], M[1]).then_inc(*NV.did("rs"))
                    dve.wait_ge(*NV.last())

            def cross(l, r):
                CV.round(l)

                def then(ins, tag=None):
                    ins.then_inc(*CV.did(tag))
                    dve.wait_ge(*CV.last())

                def take(n):
                    dve.wait_ge(chunk_used, done_at(P_Q[l] + n))
                    for j in range(2):
                        dst = (cq, cz)[n // 2][:, (2 * (n % 2) + j) * T:(2 * (n % 2) + j + 1) * T]
                        TTO(dst, bank(P_Q[l] + n, j), rs[:, :], ALU.mult).then_inc(acc_free, 1)

                def gate(n):
                    for h in (2 * n, 2 * n + 1):
                        o = slice(h * T, (h + 1) * T)
                        dve.wait_ge(*CA(f"zt{h}", l))
                        STT(out=cz[:, o], in0=zt(h), scalar=1.0, in1=cz[:, o], op0=ALU.add, op1=ALU.mult)\
                            .then_inc(*CV.did(f"zz{h}"))

                def outputs(n):
                    for h in (2 * n, 2 * n + 1):
                        o = slice(h * T, (h + 1) * T)
                        if n == 1 and h == 2:
                            dve.wait_ge(*CA("o3", l))
                        dve.wait_ge(*CV(f"zz{h}", l))
                        TTO(cq[:, o], cq[:, o], cz[:, o], ALU.mult).then_inc(*CV.did(f"y{h}"))
                    for h in (2 * n, 2 * n + 1):
                        o = slice(h * T, (h + 1) * T)
                        dve.wait_ge(*CA(f"hi{h}", l))
                        TTO(H_lo[:, o], cq[:, o], H_hi[:, o].bitcast(F32), ALU.subtract).then_inc(*CV.did(f"lo{h}"))

                def reply(name):
                    h = int(name[1])
                    s4 = flat(m01).rearrange("p (t m) -> p t m", m=MEM)
                    if name[0] == "s":
                        dve.wait_ge(*CM(name, l))
                        then(dve.reduce_max(mx, s4, axis=AX.X))
                        TS(nmx, mx, -P ** -0.5, None, ALU.mult).then_inc(*CV.did(f"nm{h}"))
                        dve.wait_ge(*CA(f"p{h}", l))
                        then(dve.reciprocal(rsum, ssum))
                        c4 = cp.rearrange("p (t m) -> p t m", m=MEM)
                        TTO(c4, c4, over_row(rsum, TT, MEM), ALU.mult).then_inc(*CV.did(f"p{h}"))
                for c in range(16):
                    split(LAYERS_Q[l] + c + 1)
                    sum_squares(r, c)
                    if c == 7:
                        take(0)
                    for name in hops_at(C_HOPS, C_SLOTS, 4 * c, 4 * c + 4):
                        reply(name)
                    if c in (8, 12):
                        take(c // 4 - 1)
                    if c == 13:
                        gate(0)
                    if c == 15:
                        outputs(0)
                take(3)
                gate(1)
                outputs(1)
                out_phase(LAYERS_O[l], P_O[l], 1)

            def take_conv(n, j):
                dve.wait_ge(chunk_used, C_C + 4 * (j + 1) + 16 * n)
                for k in range(2):
                    o = slice(k * T, (k + 1) * T)
                    dst = (uu, cu, bb, bb)[j]
                    if j == 3:
                        dve.wait_ge(*VV.last())
                    TTO(dst[:, o], bank(P_C + j, k), rs[:, :], ALU.mult).then_inc(acc_free, 1)
                dve.wait_ge(acc_free, 2 * (P_C + j + 1) + 8 * n)
                for k in range(2):
                    o = slice(k * T, (k + 1) * T)
                    tap = lambda d: pcol("c_conv", (2 * n + k) * 3 + d)
                    if j == 1:
                        TTO(cu[:, o], cu[:, o], uu[:, o], ALU.mult).then_inc(*VV.did())
                        dve.wait_ge(*VV.last())
                        TS(cv[:, o], cu[:, o], tap(2), None, ALU.mult).then_inc(*VV.did())
                        for d in (1, 2):
                            dve.wait_ge(*VV.last())
                            STT(out=cv[:, k * T + d:(k + 1) * T], in0=cu[:, k * T:(k + 1) * T - d], scalar=tap(2 - d),
                                in1=cv[:, k * T + d:(k + 1) * T], op0=ALU.mult, op1=ALU.add).then_inc(*VV.did())
                    elif j == 2:
                        if k == 0:
                            dve.wait_ge(*VV.last())
                        TTO(cv[:, o], cv[:, o], bb[:, o], ALU.mult).then_inc(*VV.did())
                    elif j == 3:
                        dve.wait_ge(*VA(f"z{k}", n))
                        STT(out=bb[:, o], in0=uu[:, o], scalar=1.0, in1=bb[:, o], op0=ALU.add, op1=ALU.mult)\
                            .then_inc(*VV.did())
                        dve.wait_ge(*VV.last())
                        STT(out=yt(2 * n + k), in0=cv[:, o], scalar=0.5, in1=bb[:, o], op0=ALU.mult, op1=ALU.mult)\
                            .then_inc(*VV.did(f"y{k}"))

            split_input(0, xt, C_OUT0, 8)
            out_phase(C_OUT0, P_OUT0, 4)
            norm(0)
            cross(0, 0)
            norm(1)

            def conv_group(n, first=False, last=False):
                for c in range(16):
                    split(C_C + c + 1, n)
                    if first:
                        sum_squares(1, c)
                    elif c == 0:
                        VV.i = n - 1
                        take_conv(n - 1, 3)
                    if c == 1:
                        VV.round(n)
                    if c == (7 if first else 4):
                        take_conv(n, 0)
                    if c in (8, 12):
                        take_conv(n, c // 4 - 1)
                    if last and c >= 13:
                        split_input(1, yt, C_OUT1, 4 * (c - 13), 4 * (c - 12))
            conv_group(0, first=True)
            with dve.Fori(1, 7) as n:
                conv_group(n)
            conv_group(7, last=True)
            take_conv(7, 3)
            split_input(1, yt, C_OUT1, 12)
            out_phase(C_OUT1, P_OUT1, 4)
            norm(2)
            cross(1, 2)
            norm(3)

        @block.gpsimd
        def _(pool):
            def power(src, dst, n):
                return pool.tensor_tensor(dst[:, 0:n], src[:, 0:n], minus_half[:, 0:n], ALU.pow)

            pool.memset(minus_half, -0.5).then_inc(const_set, 1)
            pool.wait_ge(const_set, 1)
            pool.wait_ge(*SV("stat"))
            power(stat, powed, 4).then_inc(*SG.did("pow"))

            def delta(i):
                GG.round(i)
                pool.wait_ge(*GV("stat", i))
                power(stat, powed, 16).then_inc(*GG.did("pow"))
                for s in range(len(LEVELS)):
                    pool.wait_ge(*(GV("nt", i) if s == 0 else GV("y0", i) if s == 1 else GM(f"p{s - 1}", i)))
                    pool.tensor_tensor(tiles(c_t), tiles(n_t), over_tiles(level_mask(s), 8), ALU.mult)\
                        .then_inc(*GG.did(f"c{s}"))
                pool.wait_ge(*GV("fstat", i))
                power(stat, powed, 8).then_inc(*GG.did("fpow"))
            with pool.Fori(0, 4) as i:
                delta(i)

            def attention_pair(i):
                BG.round(i)
                pool.wait_ge(tables_in, 16)
                pool.wait_ge(acc_free, 2 * (P_AB + 4 * (4 + i) + 3))
                if i:
                    pool.wait_ge(*BM("a14", i - 1))
                cos = rope_tab[:, 0:T].unsqueeze(1).broadcast_to([P, 2, T])
                for src, dst, tag in ((qc, qr, "q"), (kc, kr, "k")):
                    pool.tensor_tensor(head2(dst), head2(src), cos, ALU.mult).then_inc(*BG.did("cos_" + tag))
                for h in range(2):
                    if h:
                        pool.wait_ge(*BM("fb0", i))
                    pool.wait_ge(*BV(f"stat{h}", i))
                    power(stat, powed, 4).then_inc(*BG.did(f"pow{h}"))
            pool.wait_ge(*GM("fb", 3))
            for i in range(4):
                attention_pair(i)
                if i == 1:
                    pool.wait_ge(*MV("stat"))
                    pool.tensor_tensor(t2[:, 0:2], t1[:, 6:8], minus_half[:, 0:2], ALU.pow).then_inc(*MG.did("pow"))

            for r in range(4):
                OG.round(r)
                NG.round(r)
                if r == 0:
                    pool.wait_ge(reloaded, 16 * KT)
                else:
                    pool.wait_ge(*NM("ss2", r - 1))
                pool.memset(acc_sq, 0.0).then_inc(*OG.did())
                for k in range(KT - 2):
                    pool.wait_ge(*OA(f"s{k}", r))
                    pool.wait_ge(*OG.last())
                    pool.tensor_tensor(acc_sq, acc_sq, sqt[:, (k % 2) * T:(k % 2 + 1) * T], ALU.add)\
                        .then_inc(*OG.did(f"a{k}"))
                pool.wait_ge(*NV("stat", r))
                power(stat, powed, 4).then_inc(*NG.did("pow"))
                for k in range(KT):
                    if r == 3 and k in VECTOR_ADDS:
                        continue
                    pool.wait_ge(*(NV(f"y{k}", r) if r < 3 else FV(f"y{k}")))
                    pool.tensor_tensor(xt(k), xt(k), yt(k), ALU.add).then_inc(*(NG if r < 3 else FG).did(f"x{k}"))
                if r < 3:
                    pool.wait_ge(*NV("stat2", r))
                    power(stat, powed, 4).then_inc(*NG.did("pow2"))


def done_at(pair):
    for p0, c0, n, per in ((P_O1, C_O1, 8, 1), (P_Q1, C_Q1, 4, 4), (P_OUT1, C_OUT1, 8, 4), (P_C, C_C, 32, 4),
                           (P_O0, C_O0, 8, 1), (P_AB, C_AB, 52, 4)):
        if not isinstance(pair, int) or pair >= p0:
            return c0 + per * (pair - p0 + 1)


def shape_constants():
    c = np.zeros((P, CONST_W), np.float32)
    j, i = np.mgrid[0:P, 0:P]
    same = j // CH == i // CH
    put = lambda name, a: c.__setitem__((slice(None), slice(*CONST[name])), a)
    put("ident", j == i)
    put("cumsum", same & (j <= i))
    put("suffix", same & (j > i))
    put("half0", j < CH)
    put("half1", j >= CH)
    put("causal", np.where(same & (j <= i), 0.0, NEG))
    put("levels", np.concatenate([(j // (2 * s) == i // (2 * s)) & (j // s % 2 == 0) & (i // s % 2 == 1)
                                  for s in LEVELS], axis=1))
    put("ones", 1.0)
    inv_freq = (np.float32(10000.0) ** (-np.arange(0, QK, 2, dtype=np.float32) / np.float32(QK))).astype(np.float32)
    angle = (np.arange(T, dtype=np.float32)[None, :] * inv_freq[:, None]).astype(np.float32).astype(np.float64)
    put("cos", np.tile(np.cos(angle), (4, 1)))
    put("sin", np.concatenate([-np.sin(angle), np.sin(angle)] * 2, axis=0))
    return c


def kernel(x, mem, norm_pre, norm_post, xattn_norm_pre, xattn_norm_post, mem_norm, ab_w_in, a_conv, a_A_log,
           a_dt_bias, a_out_norm, b_lambda, b_out_norm, ab_w_out, c_w_in, c_conv, c_w_out, m_w_q, m_w_kv, m_w_o):
    import concourse.bacc as bacc
    from concourse.bass_utils import run_bass_kernel_spmd

    gains = lambda g: np.asarray(g).reshape(2 * KT, P).T
    taps = lambda w, n: np.asarray(w)[0].reshape(n, -1, P).transpose(2, 1, 0).reshape(P, -1)
    everywhere = lambda v: np.broadcast_to(np.asarray(v).reshape(1, -1), (P, np.asarray(v).size))
    parameters = np.concatenate([gains(norm_pre), gains(norm_post), gains(xattn_norm_pre), gains(xattn_norm_post),
                                 gains(mem_norm), taps(a_conv, 4), taps(c_conv, 3), np.asarray(a_out_norm).T,
                                 np.asarray(b_out_norm).T, everywhere(a_A_log), everywhere(a_dt_bias)], axis=1)
    arrays = {"x": np.asarray(x)[0], "mem": np.asarray(mem)[0], "constants": shape_constants(),
              "parameters": np.ascontiguousarray(parameters), "lambda": np.ascontiguousarray(everywhere(b_lambda)),
              "ab_w_in": np.asarray(ab_w_in)[0], "ab_w_out": np.asarray(ab_w_out)[0], "c_w_in": np.asarray(c_w_in)[0],
              "c_w_out": np.asarray(c_w_out)[0], "m_w_q": np.asarray(m_w_q), "m_w_kv": np.asarray(m_w_kv),
              "m_w_o": np.asarray(m_w_o)}
    books = {}
    for final in (False, True):
        nc = bacc.Bacc("TRN2", target_bir_lowering=False, num_devices=1)
        dram = {n: nc.dram_tensor("in_" + n, a.shape, F32, kind="ExternalInput").ap() for n, a in arrays.items()}
        dram["spill"] = nc.dram_tensor("spill", (KT, P, T), F32, kind="Internal").ap()
        dram["out"] = nc.dram_tensor("out", (T, D), F32, kind="ExternalOutput").ap()
        build(nc, books, dram)
    result = run_bass_kernel_spmd(nc, [{"in_" + n: np.ascontiguousarray(a) for n, a in arrays.items()}], core_ids=[0])
    return result.results[0]["out"].reshape(1, T, D)
```
